# Optimizing a Trainium2 kernel written in Bass

```python
import jax, jax.numpy as jnp
from jax import lax
import numpy as np
import math

D_MODEL = 1024
BATCH = 1
SEQ = 256
DEPTH = 1

CONV_CH = 512
CONV_WIDTH = 31
N_HEADS = 8
N_KV_HEADS = 2
HEAD_DIM = 64
WINDOW = 128
ATTN_BLOCK = 128
N_GROUPS = 4
EXPERTS_PER_GROUP = 8
N_EXPERTS = N_GROUPS * EXPERTS_PER_GROUP
EXPERT_TOP_K = 2
D_FF_EXPERT = 512
MOE_BLOCK = 128
NORM_EPS = 1e-6

Q_DIM = N_HEADS * HEAD_DIM
KV_DIM = N_KV_HEADS * HEAD_DIM
IN_COLS = 2 * CONV_CH + Q_DIM + 2 * KV_DIM + 2 * D_MODEL


def rms_norm(x, g):
    xf = x.astype(jnp.float32)
    y = xf * lax.rsqrt(jnp.mean(xf * xf, axis=-1, keepdims=True) + NORM_EPS)
    return (y * g.astype(jnp.float32)).astype(x.dtype)

def layer_norm(x, g, b):
    xf = x.astype(jnp.float32)
    mu = jnp.mean(xf, axis=-1, keepdims=True)
    var = jnp.mean(jnp.square(xf - mu), axis=-1, keepdims=True)
    y = (xf - mu) * lax.rsqrt(var + NORM_EPS)
    return (y * g.astype(jnp.float32) + b.astype(jnp.float32)).astype(x.dtype)

def alibi_slopes():
    return jnp.asarray(np.array([2.0 ** (-8.0 * (h + 1) / N_HEADS) for h in range(N_HEADS)], np.float32))

def conformer_conv(u, w_dw, b_dw, ln_g, ln_b):
    a, gate = jnp.split(u, 2, axis=-1)
    v = a * jax.nn.sigmoid(gate)
    y = lax.conv_general_dilated(
        v, w_dw, window_strides=(1,), padding=[(CONV_WIDTH - 1, 0)],
        dimension_numbers=("NWC", "WIO", "NWC"), feature_group_count=CONV_CH)
    y = y + b_dw
    return jax.nn.silu(layer_norm(y, ln_g, ln_b))

def sliding_window_attention(q, k, v, sinks):
    b, s = q.shape[0], q.shape[1]
    nb = s // ATTN_BLOCK
    grp = N_HEADS // N_KV_HEADS
    qb = q.reshape(b, nb, ATTN_BLOCK, N_KV_HEADS, grp, HEAD_DIM)
    kb = k.reshape(b, nb, ATTN_BLOCK, N_KV_HEADS, HEAD_DIM)
    vb = v.reshape(b, nb, ATTN_BLOCK, N_KV_HEADS, HEAD_DIM)

    def with_prev(t):
        prev = jnp.pad(t[:, :-1], ((0, 0), (1, 0), (0, 0), (0, 0), (0, 0)))
        return jnp.concatenate([prev, t], axis=2)

    kk, vv = with_prev(kb), with_prev(vb)
    scores = jnp.einsum("bnqhgd,bnkhd->bnhgqk", qb, kk,
                        preferred_element_type=jnp.float32) * (HEAD_DIM ** -0.5)
    qi = jnp.arange(ATTN_BLOCK)[:, None]
    kj = jnp.arange(2 * ATTN_BLOCK)[None, :]
    rel = ATTN_BLOCK + qi - kj
    in_window = (rel >= 0) & (rel < WINDOW)
    key_exists = (jnp.arange(nb)[:, None, None] * ATTN_BLOCK + kj[None] - ATTN_BLOCK) >= 0
    mask = in_window[None] & key_exists
    slopes = alibi_slopes().reshape(N_KV_HEADS, grp)
    scores = scores - slopes[:, :, None, None] * rel.astype(jnp.float32)
    scores = jnp.where(mask[None, :, None, None], scores, -jnp.inf)
    sink = sinks.astype(jnp.float32).reshape(N_KV_HEADS, grp)[None, None, :, :, None, None]
    m = jnp.maximum(jnp.max(scores, axis=-1, keepdims=True), sink)
    p = jnp.exp(scores - m)
    p = p / (jnp.sum(p, axis=-1, keepdims=True) + jnp.exp(sink - m))
    out = jnp.einsum("bnhgqk,bnkhd->bnqhgd", p.astype(v.dtype), vv)
    return out.reshape(b, s, Q_DIM)

def hierarchical_moe(xn, w_group, b_group, w_expert, b_expert, w_gate, w_up, w_down):
    b, s, d = xn.shape
    t = b * s
    xt = xn.reshape(t, d)
    g_logits = (xt @ w_group).astype(jnp.float32) + b_group.astype(jnp.float32)
    g_prob = jax.nn.softmax(g_logits, axis=-1)
    g_sel = jnp.argmax(g_logits, axis=-1).astype(jnp.int32)
    p_group = jnp.take_along_axis(g_prob, g_sel[:, None], axis=-1)[:, 0]
    e_logits = ((xt @ w_expert).astype(jnp.float32) + b_expert.astype(jnp.float32)).reshape(t, N_GROUPS, EXPERTS_PER_GROUP)
    e_in = jnp.take_along_axis(e_logits, g_sel[:, None, None], axis=1)[:, 0]
    top_val, top_idx = lax.top_k(e_in, EXPERT_TOP_K)
    weights = p_group[:, None] * jax.nn.softmax(top_val, axis=-1)
    expert_id = (g_sel[:, None] * EXPERTS_PER_GROUP + top_idx.astype(jnp.int32)).reshape(-1)
    token_id = jnp.repeat(jnp.arange(t, dtype=jnp.int32), EXPERT_TOP_K)
    w_flat = weights.reshape(-1)
    n_assign = t * EXPERT_TOP_K
    n_blocks = -(-(n_assign + N_EXPERTS * (MOE_BLOCK - 1)) // MOE_BLOCK)
    order = jnp.argsort(expert_id, stable=True)
    sorted_e = expert_id[order]
    counts = jnp.zeros((N_EXPERTS,), jnp.int32).at[expert_id].add(1)
    padded = ((counts + MOE_BLOCK - 1) // MOE_BLOCK) * MOE_BLOCK
    padded_ends = jnp.cumsum(padded)
    padded_starts = padded_ends - padded
    starts = jnp.cumsum(counts) - counts
    rank = jnp.arange(n_assign, dtype=jnp.int32) - starts[sorted_e]
    dest = padded_starts[sorted_e] + rank
    slot_token = jnp.zeros((n_blocks * MOE_BLOCK,), jnp.int32).at[dest].set(token_id[order])
    slot_w = jnp.zeros((n_blocks * MOE_BLOCK,), jnp.float32).at[dest].set(w_flat[order])
    block_start = jnp.arange(n_blocks, dtype=jnp.int32) * MOE_BLOCK
    block_expert = jnp.clip(jnp.searchsorted(padded_ends, block_start, side="right"), 0, N_EXPERTS - 1).astype(jnp.int32)

    def run_block(args):
        tok, wt, e = args
        xb = xt[tok]
        hmid = jax.nn.silu(xb @ w_gate[e]) * (xb @ w_up[e])
        return (hmid @ w_down[e]) * wt[:, None].astype(xb.dtype)

    ys = lax.map(run_block, (slot_token.reshape(n_blocks, MOE_BLOCK),
                             slot_w.reshape(n_blocks, MOE_BLOCK), block_expert))
    out = jnp.zeros((t, d), xn.dtype).at[slot_token].add(ys.reshape(-1, d))
    return out.reshape(b, s, d)

def first_inputs(seed: int = 0) -> dict:
    key = jax.random.key(seed)
    ks = jax.random.split(key, 24)
    f32 = jnp.float32

    def nrm(k, shape, scale):
        return jax.random.normal(k, shape, f32) * scale

    L = DEPTH
    return {
        "x": jax.random.normal(ks[0], (BATCH, SEQ, D_MODEL), f32),
        "g_mix": 1.0 + nrm(ks[1], (L, D_MODEL), 0.02),
        "w_in": nrm(ks[2], (L, D_MODEL, IN_COLS), D_MODEL ** -0.5),
        "w_dw": nrm(ks[3], (L, CONV_WIDTH, 1, CONV_CH), CONV_WIDTH ** -0.5),
        "b_dw": nrm(ks[4], (L, CONV_CH), 0.02),
        "ln_conv_g": 1.0 + nrm(ks[5], (L, CONV_CH), 0.02),
        "ln_conv_b": nrm(ks[6], (L, CONV_CH), 0.02),
        "sinks": nrm(ks[7], (L, N_HEADS), 0.5),
        "w_conv_out": nrm(ks[8], (L, CONV_CH, D_MODEL), CONV_CH ** -0.5),
        "w_attn_out": nrm(ks[9], (L, Q_DIM, D_MODEL), Q_DIM ** -0.5),
        "w_out": nrm(ks[10], (L, D_MODEL, D_MODEL), D_MODEL ** -0.5),
        "g_ffn": 1.0 + nrm(ks[11], (L, D_MODEL), 0.02),
        "w_group": nrm(ks[12], (L, D_MODEL, N_GROUPS), D_MODEL ** -0.5),
        "b_group": nrm(ks[13], (L, N_GROUPS), 0.01),
        "w_expert": nrm(ks[14], (L, D_MODEL, N_EXPERTS), D_MODEL ** -0.5),
        "b_expert": nrm(ks[15], (L, N_EXPERTS), 0.01),
        "w_gate": nrm(ks[16], (L, N_EXPERTS, D_MODEL, D_FF_EXPERT), D_MODEL ** -0.5),
        "w_up": nrm(ks[17], (L, N_EXPERTS, D_MODEL, D_FF_EXPERT), D_MODEL ** -0.5),
        "w_down": nrm(ks[18], (L, N_EXPERTS, D_FF_EXPERT, D_MODEL), D_FF_EXPERT ** -0.5),
        "g_final": 1.0 + nrm(ks[19], (D_MODEL,), 0.02),
    }

def first_block(x, g_mix, w_in, w_dw, b_dw, ln_conv_g, ln_conv_b, sinks, w_conv_out, w_attn_out,
              w_out, g_ffn, w_group, b_group, w_expert, b_expert, w_gate, w_up, w_down, g_final):
    b, s, _ = x.shape
    cuts = list(np.cumsum([2 * CONV_CH, Q_DIM, KV_DIM, KV_DIM, D_MODEL]))
    h = x
    for l in range(DEPTH):
        xn = rms_norm(h, g_mix[l])
        proj = xn @ w_in[l]
        u_conv, q, k, v, gate_conv, gate_attn = jnp.split(proj, cuts, axis=-1)
        conv_o = conformer_conv(u_conv, w_dw[l], b_dw[l], ln_conv_g[l], ln_conv_b[l]) @ w_conv_out[l]
        attn = sliding_window_attention(q.reshape(b, s, N_HEADS, HEAD_DIM),
                                        k.reshape(b, s, N_KV_HEADS, HEAD_DIM),
                                        v.reshape(b, s, N_KV_HEADS, HEAD_DIM), sinks[l])
        attn_o = attn @ w_attn_out[l]
        merged = jax.nn.sigmoid(gate_conv) * conv_o + jax.nn.sigmoid(gate_attn) * attn_o
        h = h + merged @ w_out[l]
        h = h + hierarchical_moe(rms_norm(h, g_ffn[l]), w_group[l], b_group[l], w_expert[l],
                                 b_expert[l], w_gate[l], w_up[l], w_down[l])
    return rms_norm(h, g_final)


GRID_W = 64
CTX_LEN = 256
EPS = 1e-6

AXIS_ROPE_DIM = HEAD_DIM // 2
ROPE_THETA = 10000.0
Q_BLOCK = 128

HY_DIM = D_MODEL // 2
HY_ORDER = 2
HY_SHORT = 3
HY_EMB_BANDS = 16
HY_EMB_DIM = 1 + 2 * HY_EMB_BANDS
HY_FFN = 64
HY_FAST_DECAY = 0.3
HY_SLOW_DECAY = 1.5
HY_TARGET = 1e-2

Q_DIM_2 = N_HEADS * HEAD_DIM
KV_DIM_2 = N_KV_HEADS * HEAD_DIM
HY_COLS = (HY_ORDER + 1) * HY_DIM
GATE_COLS = 2 * D_MODEL
IN_COLS_2 = Q_DIM_2 + 2 * KV_DIM_2 + HY_COLS + GATE_COLS

PEER_HEADS = 8
PEER_N_KEYS = 128
PEER_N_EXPERTS = PEER_N_KEYS * PEER_N_KEYS
PEER_DK = 256
PEER_TOPK = 16
PEER_CHUNK = 128


def rmsnorm(x, g):
    xf = x.astype(jnp.float32)
    y = xf * lax.rsqrt(jnp.mean(xf * xf, axis=-1, keepdims=True) + EPS)
    return (y * g.astype(jnp.float32)).astype(x.dtype)

def modulate(h, shift, scale):
    return h * (1.0 + scale) + shift

def axial_rope(rows):
    t = jnp.arange(rows * GRID_W)
    row = (t // GRID_W).astype(jnp.float32)
    col = (t % GRID_W).astype(jnp.float32)
    inv = ROPE_THETA ** (-jnp.arange(0, AXIS_ROPE_DIM, 2, dtype=jnp.float32) / AXIS_ROPE_DIM)
    ar = row[:, None] * inv
    ac = col[:, None] * inv
    ang = jnp.concatenate([ar, ar, ac, ac], axis=-1)
    return jnp.cos(ang), jnp.sin(ang)

def apply_rope(x, cos, sin):
    xf = x.astype(jnp.float32)
    half = AXIS_ROPE_DIM // 2

    def rot(a):
        return jnp.concatenate([-a[..., half:], a[..., :half]], axis=-1)

    xr = jnp.concatenate([rot(xf[..., :AXIS_ROPE_DIM]), rot(xf[..., AXIS_ROPE_DIM:])], axis=-1)
    return (xf * cos[:, None] + xr * sin[:, None]).astype(x.dtype)

def gqa_blocks(q, k, v):
    B, L, _, _ = q.shape
    G = N_HEADS // N_KV_HEADS
    nb = L // Q_BLOCK
    qb = jnp.moveaxis(q.reshape(B, nb, Q_BLOCK, N_KV_HEADS, G, HEAD_DIM), 1, 0)
    scale = HEAD_DIM ** -0.5

    def one_block(qblk):
        s = jnp.einsum('bqkgd,btkd->bkgqt', qblk, k) * scale
        p = jax.nn.softmax(s.astype(jnp.float32), axis=-1).astype(v.dtype)
        return jnp.einsum('bkgqt,btkd->bqkgd', p, v)

    o = lax.map(one_block, qb)
    return jnp.moveaxis(o, 0, 1).reshape(B, L, Q_DIM_2)

def short_conv(z, w, b):
    zp = jnp.pad(z, ((0, 0), (1, 1), (0, 0)))
    return zp[:, :-2] * w[0] + zp[:, 1:-1] * w[1] + zp[:, 2:] * w[2] + b

def implicit_filters(L, w1, b1, w2, b2, w3, b3, w4, freq):
    t01 = jnp.linspace(0.0, 1.0, L, dtype=jnp.float32)[:, None]
    w = 2.0 * math.pi * jnp.arange(L, dtype=jnp.float32)[:, None] / L
    f = jnp.linspace(1e-4, HY_EMB_BANDS - 1, HY_EMB_BANDS, dtype=jnp.float32)[None]
    z = jnp.concatenate([t01, jnp.cos(f * w), -jnp.sin(f * w)], axis=-1)
    act = lambda a: jnp.sin(freq * a)
    hmid = act(z @ w1 + b1)
    hmid = act(hmid @ w2 + b2)
    hmid = act(hmid @ w3 + b3)
    h = (hmid @ w4).astype(jnp.float32).reshape(L, HY_ORDER, 2, HY_DIM)
    max_decay = math.log(HY_TARGET) / HY_FAST_DECAY
    min_decay = math.log(HY_TARGET) / HY_SLOW_DECAY
    deltas = jnp.abs(jnp.linspace(min_decay, max_decay, HY_DIM, dtype=jnp.float32))
    h = h * jnp.exp(-t01[:, :, None, None] * deltas)
    fwd = h[:, :, 0]
    bwd = h[:, :, 1]
    k = jnp.concatenate([fwd, jnp.zeros_like(fwd[:1]), bwd[:0:-1]], axis=0)
    k = k / (jnp.sum(jnp.abs(k), axis=0, keepdims=True) + EPS)
    return jnp.fft.rfft(k, axis=0)

def fftconv(u, kf, d):
    L = u.shape[1]
    uf = u.astype(jnp.float32)
    U = jnp.fft.rfft(uf, n=2 * L, axis=1)
    y = jnp.fft.irfft(U * kf[None], n=2 * L, axis=1)[:, :L]
    return y + uf * d.astype(jnp.float32)

def hyena(z_hy, conv_w, conv_b, kf, skip):
    zs = short_conv(z_hy, conv_w, conv_b)
    v, x1, x2 = jnp.split(zs, 3, axis=-1)
    y = x1.astype(jnp.float32) * fftconv(v, kf[:, 0], skip[0])
    y = x2.astype(jnp.float32) * fftconv(y, kf[:, 1], skip[1])
    return y.astype(z_hy.dtype)

def mix(h, p, rope, kv_ext):
    B, L, _ = h.shape
    z = h @ p["w_in"]
    q, k, v, z_hy, gates = jnp.split(
        z, [Q_DIM_2, Q_DIM_2 + KV_DIM_2, Q_DIM_2 + 2 * KV_DIM_2, Q_DIM_2 + 2 * KV_DIM_2 + HY_COLS], axis=-1)
    q = rmsnorm(q.reshape(B, L, N_HEADS, HEAD_DIM), p["q_norm_g"])
    k = rmsnorm(k.reshape(B, L, N_KV_HEADS, HEAD_DIM), p["k_norm_g"])
    v = v.reshape(B, L, N_KV_HEADS, HEAD_DIM)
    if rope is not None:
        q = apply_rope(q, rope[0], rope[1])
        k = apply_rope(k, rope[0], rope[1])
    k_self, v_self = k, v
    if kv_ext is not None:
        k = jnp.concatenate([k, kv_ext[0]], axis=1)
        v = jnp.concatenate([v, kv_ext[1]], axis=1)
    attn = gqa_blocks(q, k, v)
    kf = implicit_filters(L, p["hf_w1"], p["hf_b1"], p["hf_w2"], p["hf_b2"],
                          p["hf_w3"], p["hf_b3"], p["hf_w4"], p["hf_freq"])
    hy = hyena(z_hy, p["hy_conv_w"], p["hy_conv_b"], kf, p["hy_skip"])
    g_attn, g_hy = jnp.split(gates, 2, axis=-1)
    merged = (jax.nn.sigmoid(g_attn) * (attn @ p["w_attn_out"])
              + jax.nn.sigmoid(g_hy) * (hy @ p["w_hy_out"]))
    return merged @ p["w_out"], k_self, v_self

def context_kv(hc, p):
    B, L, _ = hc.shape
    z = hc @ p["w_in"][:, Q_DIM_2:Q_DIM_2 + 2 * KV_DIM_2]
    k, v = jnp.split(z, 2, axis=-1)
    k = rmsnorm(k.reshape(B, L, N_KV_HEADS, HEAD_DIM), p["k_norm_g"])
    return k, v.reshape(B, L, N_KV_HEADS, HEAD_DIM)

def peer(h, wq, keys1, keys2, u_tab, v_tab):
    B, L, D = h.shape
    xt = h.reshape(B * L // PEER_CHUNK, PEER_CHUNK, D)
    half = PEER_DK // 2

    def chunk(xc):
        q = (xc @ wq).reshape(PEER_CHUNK, PEER_HEADS, 2, half)
        s1 = jnp.einsum('chd,hnd->chn', q[:, :, 0], keys1).astype(jnp.float32)
        s2 = jnp.einsum('chd,hnd->chn', q[:, :, 1], keys2).astype(jnp.float32)
        v1, i1 = lax.top_k(s1, PEER_TOPK)
        v2, i2 = lax.top_k(s2, PEER_TOPK)
        cand = (v1[..., :, None] + v2[..., None, :]).reshape(PEER_CHUNK, PEER_HEADS, PEER_TOPK * PEER_TOPK)
        cidx = (i1[..., :, None] * PEER_N_KEYS + i2[..., None, :]).reshape(PEER_CHUNK, PEER_HEADS, PEER_TOPK * PEER_TOPK)
        best, pos = lax.top_k(cand, PEER_TOPK)
        eidx = jnp.take_along_axis(cidx, pos, axis=-1)
        g = jax.nn.softmax(best, axis=-1)
        a = jnp.einsum('chkd,cd->chk', u_tab[eidx], xc)
        wgt = (jax.nn.gelu(a.astype(jnp.float32)) * g).astype(xc.dtype)
        return jnp.einsum('chk,chkd->cd', wgt, v_tab[eidx])

    return lax.map(chunk, xt).reshape(B, L, D)

def second_inputs(seed: int = 0) -> dict:
    key = jax.random.key(seed)
    ks = iter(jax.random.split(key, 40))

    def nrm(shape, scale):
        return jax.random.normal(next(ks), shape, jnp.float32) * scale

    L = DEPTH
    return {
        "x": nrm((BATCH, SEQ, D_MODEL), 1.0),
        "c": nrm((BATCH, D_MODEL), 1.0),
        "ctx": nrm((BATCH, CTX_LEN, D_MODEL), 1.0),
        "c_ctx": nrm((D_MODEL,), 1.0),
        "ada_w": nrm((L, D_MODEL, 6 * D_MODEL), D_MODEL ** -0.5),
        "ada_b": nrm((L, 6 * D_MODEL), 0.02),
        "norm_mix_g": 1.0 + nrm((L, D_MODEL), 0.02),
        "norm_ffn_g": 1.0 + nrm((L, D_MODEL), 0.02),
        "w_in": nrm((L, D_MODEL, IN_COLS_2), D_MODEL ** -0.5),
        "q_norm_g": 1.0 + nrm((L, HEAD_DIM), 0.02),
        "k_norm_g": 1.0 + nrm((L, HEAD_DIM), 0.02),
        "hy_conv_w": nrm((L, HY_SHORT, HY_COLS), HY_SHORT ** -0.5),
        "hy_conv_b": nrm((L, HY_COLS), 0.02),
        "hf_w1": nrm((L, HY_EMB_DIM, HY_FFN), HY_EMB_DIM ** -0.5),
        "hf_b1": nrm((L, HY_FFN), 0.02),
        "hf_w2": nrm((L, HY_FFN, HY_FFN), HY_FFN ** -0.5),
        "hf_b2": nrm((L, HY_FFN), 0.02),
        "hf_w3": nrm((L, HY_FFN, HY_FFN), HY_FFN ** -0.5),
        "hf_b3": nrm((L, HY_FFN), 0.02),
        "hf_w4": nrm((L, HY_FFN, HY_ORDER * 2 * HY_DIM), HY_FFN ** -0.5),
        "hf_freq": 1.0 + nrm((L, HY_FFN), 0.02),
        "hy_skip": nrm((L, HY_ORDER, HY_DIM), 0.5),
        "w_attn_out": nrm((L, Q_DIM_2, D_MODEL), Q_DIM_2 ** -0.5),
        "w_hy_out": nrm((L, HY_DIM, D_MODEL), HY_DIM ** -0.5),
        "w_out": nrm((L, D_MODEL, D_MODEL), D_MODEL ** -0.5),
        "peer_wq": nrm((L, D_MODEL, PEER_HEADS * PEER_DK), D_MODEL ** -0.5),
        "peer_keys1": nrm((L, PEER_HEADS, PEER_N_KEYS, PEER_DK // 2), (PEER_DK // 2) ** -0.5),
        "peer_keys2": nrm((L, PEER_HEADS, PEER_N_KEYS, PEER_DK // 2), (PEER_DK // 2) ** -0.5),
        "peer_u": nrm((L, PEER_N_EXPERTS, D_MODEL), D_MODEL ** -0.5),
        "peer_v": nrm((L, PEER_N_EXPERTS, D_MODEL), PEER_HEADS ** -0.5),
        "final_norm_g": 1.0 + nrm((D_MODEL,), 0.02),
    }

def second_block(x, c, ctx, c_ctx, ada_w, ada_b, norm_mix_g, norm_ffn_g, w_in, q_norm_g, k_norm_g,
              hy_conv_w, hy_conv_b, hf_w1, hf_b1, hf_w2, hf_b2, hf_w3, hf_b3, hf_w4, hf_freq, hy_skip,
              w_attn_out, w_hy_out, w_out, peer_wq, peer_keys1, peer_keys2, peer_u, peer_v, final_norm_g):
    ROWS = x.shape[1] // GRID_W
    rope = axial_rope(ROWS)
    sc = jax.nn.silu(c)
    scc = jax.nn.silu(c_ctx)
    for i in range(DEPTH):
        p = dict(w_in=w_in[i], q_norm_g=q_norm_g[i], k_norm_g=k_norm_g[i],
                 hy_conv_w=hy_conv_w[i], hy_conv_b=hy_conv_b[i],
                 hf_w1=hf_w1[i], hf_b1=hf_b1[i], hf_w2=hf_w2[i], hf_b2=hf_b2[i],
                 hf_w3=hf_w3[i], hf_b3=hf_b3[i], hf_w4=hf_w4[i], hf_freq=hf_freq[i],
                 hy_skip=hy_skip[i], w_attn_out=w_attn_out[i], w_hy_out=w_hy_out[i], w_out=w_out[i])
        mod = (sc @ ada_w[i] + ada_b[i])[:, None, :]
        mod_c = scc @ ada_w[i] + ada_b[i]
        sh1, sc1, g1, sh2, sc2, g2 = jnp.split(mod, 6, axis=-1)
        csh1, csc1, cg1, csh2, csc2, cg2 = jnp.split(mod_c, 6, axis=-1)

        h = modulate(rmsnorm(x, norm_mix_g[i]), sh1, sc1)
        hc = modulate(rmsnorm(ctx, norm_mix_g[i]), csh1, csc1)
        if i < DEPTH - 1:
            out_c, kc, vc = mix(hc, p, None, None)
        else:
            kc, vc = context_kv(hc, p)
        out, _, _ = mix(h, p, rope, (kc, vc))
        x = x + g1 * out
        x = x + g2 * peer(modulate(rmsnorm(x, norm_ffn_g[i]), sh2, sc2),
                          peer_wq[i], peer_keys1[i], peer_keys2[i], peer_u[i], peer_v[i])
        if i < DEPTH - 1:
            ctx = ctx + cg1 * out_c
            ctx = ctx + cg2 * peer(modulate(rmsnorm(ctx, norm_ffn_g[i]), csh2, csc2),
                                   peer_wq[i], peer_keys1[i], peer_keys2[i], peer_u[i], peer_v[i])
    return rmsnorm(x, final_norm_g)


def setup_inputs(seed=0):
    out = dict(first_inputs(seed))
    for name, value in second_inputs(seed + 1).items():
        if name != "x":
            out[name + "_2"] = value
    return out


def reference(
    x, g_mix, w_in, w_dw, b_dw, ln_conv_g, ln_conv_b, sinks, w_conv_out, w_attn_out, w_out,
    g_ffn, w_group, b_group, w_expert, b_expert, w_gate, w_up, w_down, g_final, c_2, ctx_2,
    c_ctx_2, ada_w_2, ada_b_2, norm_mix_g_2, norm_ffn_g_2, w_in_2, q_norm_g_2, k_norm_g_2,
    hy_conv_w_2, hy_conv_b_2, hf_w1_2, hf_b1_2, hf_w2_2, hf_b2_2, hf_w3_2, hf_b3_2, hf_w4_2,
    hf_freq_2, hy_skip_2, w_attn_out_2, w_hy_out_2, w_out_2, peer_wq_2, peer_keys1_2,
    peer_keys2_2, peer_u_2, peer_v_2, final_norm_g_2,
):
    x = first_block(
        x, g_mix, w_in, w_dw, b_dw, ln_conv_g, ln_conv_b, sinks, w_conv_out, w_attn_out, w_out,
        g_ffn, w_group, b_group, w_expert, b_expert, w_gate, w_up, w_down, g_final,
    )
    return second_block(
        x, c_2, ctx_2, c_ctx_2, ada_w_2, ada_b_2, norm_mix_g_2, norm_ffn_g_2, w_in_2,
        q_norm_g_2, k_norm_g_2, hy_conv_w_2, hy_conv_b_2, hf_w1_2, hf_b1_2, hf_w2_2, hf_b2_2,
        hf_w3_2, hf_b3_2, hf_w4_2, hf_freq_2, hy_skip_2, w_attn_out_2, w_hy_out_2, w_out_2,
        peer_wq_2, peer_keys1_2, peer_keys2_2, peer_u_2, peer_v_2, final_norm_g_2,
    )


_drawn_inputs = setup_inputs


def setup_inputs(seed=0):
    import zlib

    import numpy as np

    out = dict(_drawn_inputs(seed))
    spreads = {}
    factors = {'g_mix': 2.696,
     'ln_conv_b': 3.033,
     'sinks': 3.08,
     'b_group': 4.952,
     'b_expert': 3.096,
     'norm_mix_g_2': 5.067,
     'norm_ffn_g_2': 23.96,
     'q_norm_g_2': 23.706,
     'k_norm_g_2': 27.862,
     'hy_conv_b_2': 4.854,
     'hf_b1_2': 5.451,
     'hf_b2_2': 5.047,
     'hf_b3_2': 3.728,
     'hf_freq_2': 8.0,
     'final_norm_g_2': 7.849,
     'b_dw': 3.029,
     'ln_conv_g': 4.182}
    for name, (base, spread) in spreads.items():
        noise = np.random.default_rng([zlib.crc32(name.encode()), seed]).standard_normal(out[name].shape)
        drawn = base * np.exp(spread * noise) if base else spread * noise
        out[name] = __import__('jax').numpy.asarray(drawn.astype(out[name].dtype))
    for name, factor in factors.items():
        out[name] = (out[name] * factor).astype(out[name].dtype)
    return out
```

```python
from contextlib import ExitStack

import numpy as np
import concourse.bass as bass
from concourse import mybir

P = 128
F32 = mybir.dt.float32
I32 = mybir.dt.int32
U32 = mybir.dt.uint32
ALU = mybir.AluOpType
ACT = mybir.ActivationFunctionType
AX = mybir.AxisListType

T = 256
NT = T // P
D = 1024
KD = D // P
CH = 512
KC = CH // P
TAPS = 31
HEADS, KV, HD = 8, 2, 64
EXPERTS, GROUPS, PER_GROUP = 32, 4, 8
FF = 512
CAP = 64
BLOCKS = T // CAP
EXTRA = 2 * T // CAP
SLOTS = 6
PIECE = 4096
STEPS = EXPERTS // 2
MAXSTEPS = (EXPERTS + EXTRA) // 2
ROWS = (EXPERTS + EXTRA) * CAP
PH, PKEYS, PTOP = 8, 128, 16
PICKS = PH * PTOP
ROWBUFS = 8
EPS = 1e-6
SLOPES = [2.0 ** (-8.0 * (h + 1) / HEADS) for h in range(HEADS)]
MASKED = 1.0e30


def shape_constants():
    c = {}
    c["c_ident"] = np.eye(P, dtype=np.float32)
    c["c_before"] = np.triu(np.ones((P, P), np.float32), 1)
    q = np.arange(P)[:, None]
    k = np.arange(2 * P)[None, :]
    rel = P + q - k
    c["c_rel"] = np.where((rel >= 0) & (rel < P), rel, MASKED).astype(np.float32)
    t = np.arange(T, dtype=np.float64)
    theta = 2 * np.pi * (t + 0.5) / (2 * T)
    ang = t[:, None] * theta[None, :]
    cs = np.stack([np.cos(ang), np.sin(ang)])
    c["c_dft"] = cs.reshape(2, NT, P, T).transpose(2, 0, 1, 3).astype(np.float32).copy()
    inv = (np.stack([np.cos(ang).T, np.sin(ang).T]) / T)
    c["c_idft"] = inv.reshape(2 * NT, P, T).transpose(1, 0, 2).astype(np.float32).copy()
    row, col = np.arange(T) // 64, np.arange(T) % 64
    f = (10000.0 ** (-np.arange(0, 32, 2) / 32)).astype(np.float32)
    ar, ac = row[:, None].astype(np.float32) * f, col[:, None].astype(np.float32) * f
    a = np.concatenate([ar, ar, ac, ac], -1)
    sign = np.tile(np.concatenate([-np.ones(16), np.ones(16)]), 2)
    c["c_rope"] = np.stack([np.cos(a), np.sin(a) * sign]).reshape(2, NT, P, HD).transpose(2, 0, 1, 3).astype(np.float32).copy()
    t01 = np.linspace(0.0, 1.0, T, dtype=np.float32)[:, None]
    w = (2.0 * np.pi * np.arange(T, dtype=np.float32)[:, None] / T).astype(np.float32)
    fr = np.linspace(1e-4, 15, 16, dtype=np.float32)[None]
    z = np.concatenate([t01, np.cos(fr * w), -np.sin(fr * w)], -1)
    c["c_feat"] = z.T.astype(np.float32).copy()
    deltas = np.abs(np.linspace(np.log(1e-2) / 1.5, np.log(1e-2) / 0.3, CH, dtype=np.float32))
    decay = np.exp(-t01 * deltas)
    back = decay.copy()
    back[0] = 0.0
    c["c_decay"] = np.stack([decay, back]).reshape(2, NT, P, CH).transpose(2, 1, 0, 3).astype(np.float32).copy()
    c["c_iota"] = np.tile(np.arange(EXPERTS, dtype=np.float32), (P, 1))
    return c


def build(nc, A, out):
    ctx = ExitStack()
    with ctx:
        def sb(name, shape, dt=F32):
            return ctx.enter_context(nc.sbuf_tensor(name, shape, dt))

        def sem(name):
            return ctx.enter_context(nc.semaphore(name))

        psum = ctx.enter_context(nc.psum_tensor("psum", [P, 8, 512], F32))
        ring = sb("ring", [P, SLOTS, PIECE])
        resid = sb("resid", [P, NT, D])
        scratch = sb("scratch", [P, NT, D])
        tok2 = sb("tok2", [P, NT, D])
        actT = sb("actT", [P, KD, T])
        spec = sb("spec", [P, 2, 2, NT, CH])
        dft = sb("dft", [P, 2, NT, T])
        idft = sb("idft", [P, 2 * NT, T])
        arena1 = sb("arena1", [P, 4224])
        arena2 = sb("arena2", [P, 4096])
        qT = sb("qT", [P, KC, T])
        kdup = sb("kdup", [P, KV, 2 * T])
        vtok = sb("vtok", [P, 2 * NT, KV * HD])
        attnT = sb("attnT", [P, KC, T])
        ident = sb("ident", [P, P])
        ones = sb("ones", [P, P])
        before = sb("before", [P, P])
        rel = sb("rel", [P, 2 * P])
        rope = sb("rope", [P, 2, NT, HD])
        iota = sb("iota", [P, EXPERTS])
        colsA = sb("colsA", [P, 104])
        colsB = sb("colsB", [P, 124])
        colsC = sb("colsC", [P, 48])
        colsD = sb("colsD", [64, 4])
        mod = sb("mod", [P, 6 * KD, 2])
        modsc = sb("modsc", [P, 3, KD])
        scT = sb("scT", [P, KD, 2])
        rbias = sb("rbias", [P, GROUPS + EXPERTS])
        sinkrow = sb("sinkrow", [P, HEADS])
        qkg = sb("qkg", [P, 2, HD])
        wroute = sb("wroute", [P, KD, GROUPS + EXPERTS])
        st = sb("st", [P, 400])
        epscol = sb("epscol", [P, 1])
        picks = sb("picks", [P, 4])
        slotf = sb("slotf", [P, 4])
        sloti = sb("sloti", [P, 4], I32)
        trips = sb("trips", [1, 1], I32)
        elist = sb("elist", [1, EXPERTS + EXTRA], I32)

        aT = arena1[:, 0:1024].rearrange("p (c t) -> p c t", c=KC)
        sgT = arena1[:, 1024:2048].rearrange("p (c t) -> p c t", c=KC)
        vpad = arena1[:, 2048:2048 + KC * (T + 30)].rearrange("p (c t) -> p c t", c=KC)
        yT = arena1[:, 3200:4224].rearrange("p (c t) -> p c t", c=KC)
        ytok = arena1[:, 0:1024].rearrange("p (a c) -> p a c", a=NT)
        yactT = arena1[:, 1024:2048].rearrange("p (c t) -> p c t", c=KC)
        prob1 = arena2[:, :].rearrange("p (t h k) -> p t h k", t=NT, h=HEADS)
        pTbuf = scratch[:, :, :].rearrange("p a (s c) -> p (a s) c", c=512)
        sgate = arena2[:, 0:1024].rearrange("p (b c) -> p b c", b=2)
        mtmp = arena2[:, 1024:2048].rearrange("p (b c) -> p b c", b=2)
        mergedT = tok2[:, :, :].rearrange("p a (c t) -> p (a c) t", t=T)
        filt = arena1[:, 0:4096].rearrange("p (a m c) -> p a m c", a=NT, m=4)
        decay = tok2[:, :, :].rearrange("p a (m c) -> p a m c", m=2)
        fsmall = arena2[0:64, 0:2048].rearrange("p (a t) -> p a t", t=T)
        feat = arena2[0:33, 2048:2304]
        w1s = arena2[0:33, 2304:2368]
        w23 = arena2[0:64, 2368:2496].rearrange("p (a n) -> p a n", a=2)
        absb = arena2[:, 2560:3584].rearrange("p (a c) -> p a c", a=2)
        ctxr = resid
        ctxT = actT
        kvt = qT[:, :, :].rearrange("p c t -> p (c t)")

        kflat = kdup[:, :, :].rearrange("p a t -> p (a t)")
        prm = kflat[:, 0:384].rearrange("p (a t) -> p a t", t=P)
        prmD = kflat[0:4, 384:448]
        crow = kflat[0:16, 512:640]
        zeros = attnT[:, :, :].rearrange("p c t -> p (c t)")
        rt = arena2[:, 0:1024]
        xrow = scratch[0:CAP, :, :]
        yrow = tok2[0:CAP, :, :]
        xT = arena1[:, 0:1024].rearrange("p (h k c) -> p h k c", h=2, k=KD)
        hidT = arena1[:, 1024:1536].rearrange("p (h k c) -> p h k c", h=2, k=4)
        silu = arena1[0:CAP, 1536:2560].rearrange("p (h c) -> p h c", h=2)
        hrow = arena1[0:CAP, 2560:3584].rearrange("p (h c) -> p h c", h=2)
        back = arena2[:, :].rearrange("p (a d) -> p a d", d=D)
        zs = arena1[:, 0:3072].rearrange("p (c t) -> p c t", t=T)
        y1T, hyoT = zs[:, 4:8, :], zs[:, 8:12, :]
        hpad = arena1[:, 3072:3072 + 4 * (T + 2)].rearrange("p (b c t) -> p b c t", b=2, c=2)
        qtok = arena2[:, 0:1024].rearrange("p (a c) -> p a c", a=NT)
        ktok = arena2[:, 1024:1280].rearrange("p (a c) -> p a c", a=NT)
        sq = arena2[:, 1280:2304].rearrange("p (a c) -> p a c", a=NT)
        rtmp = arena2[:, 2304:3328].rearrange("p (a c) -> p a c", a=NT)
        prob2 = arena2[:, :].rearrange("p (u c) -> p u c", c=512)
        vtime = tok2[:, 0, :].rearrange("p (a c) -> p a c", a=NT)
        Usb = arena2[:, 0:2048].rearrange("p (k c) -> p k c", c=CH)
        Y = arena2[:, 2048:4096].rearrange("p (k c) -> p k c", c=CH)
        prod = scratch[:, :, :]
        g1row = kflat
        gfrow = attnT[:, :, :].rearrange("p c t -> p (c t)")
        pqT = arena2[:, :].rearrange("p (c t) -> p c t", t=T)
        keysT = spec[:, 0, :, :, :].rearrange("p a b c -> p (a b c)").rearrange("p (c n) -> p c n", n=P)
        cand = spec[:, 1, :, :, :].rearrange("p a b c -> p (a b c)")
        S = arena1[:, 0:4096].rearrange("p (t c n) -> p t c n", t=NT, n=P)
        qflat = qT[:, :, :].rearrange("p c t -> p (c t)")
        vflat = vtok[:, :, :].rearrange("p c t -> p (c t)")
        aflat = attnT[:, :, :].rearrange("p c t -> p (c t)")
        top_v = qflat[:, 0:512].rearrange("p (t c k) -> p t c k", t=NT, k=PTOP)
        top_i = qflat[:, 512:1024].bitcast(U32).rearrange("p (t c k) -> p t c k", t=NT, k=PTOP)
        top_f = kflat[:, 0:512].rearrange("p (t c k) -> p t c k", t=NT, k=PTOP)
        best = kflat[:, 512:768].rearrange("p (t h k) -> p t h k", t=NT, k=PTOP)
        where = kflat[:, 768:1024].bitcast(U32).rearrange("p (t n) -> p t n", t=NT)
        wi = vflat[:, 0:256].bitcast(U32).rearrange("p (t n) -> p t n", t=NT)
        wf = vflat[:, 256:512].rearrange("p (t n) -> p t n", t=NT)
        dots = aflat[:, 0:256].rearrange("p (t n) -> p t n", t=NT)
        gates = aflat[:, 256:512].rearrange("p (t n) -> p t n", t=NT)
        rowid = aflat[:, 512:768].bitcast(I32).rearrange("p (t n) -> p t n", t=NT)
        rowf = aflat[:, 768:1024].rearrange("p (t n) -> p t n", t=NT)
        rows = ring[:, 0:2, :].rearrange("p s (b d) -> p (s b) d", d=D)
        g2row, flrow = ring[:, 5, 0:D], ring[:, 5, D:2 * D]
        dotjunk = actT[:, 0:4, :].rearrange("p c t -> p (c t)")
        cur = sb("cur", [P, ROWBUFS], I32)
        dot8 = sb("dot8", [P, ROWBUFS])

        xs = nc.dram_tensor("moe_rows_in", (ROWS + P, D), F32, kind="Internal").ap()
        ys = nc.dram_tensor("moe_rows_out", (ROWS, D), F32, kind="Internal").ap()

        bank_full = [sem(f"bank_full{b}") for b in range(8)]
        bank_read = [sem(f"bank_read{b}") for b in range(8)]
        piece_in = [sem(f"piece_in{s}") for s in range(SLOTS)]
        piece2_in = [sem(f"piece2_in{s}") for s in range(SLOTS)]
        prm_in = sem("prm_in")
        const_in = sem("const_in")
        ctx_in = sem("ctx_in")
        x_in = sem("x_in")
        grow_in = sem("grow_in")
        dec_in = sem("dec_in")
        act_step = sem("act_step")
        dve_step = sem("dve_step")
        pool_step = sem("pool_step")
        pe_step = sem("pe_step")
        events = {}

        def ev(name):
            if name not in events:
                events[name] = sem(name)
            return events[name]

        def kpiece(w, c0, n=512):
            return w[:, c0:c0 + n].rearrange("(k p) n -> p k n", p=P)

        w_in, w_in2, ada = A["w_in"][0], A["w_in_2"][0], A["ada_w_2"][0]
        pieces = []
        for j in (0, 1, 2, 3, 6, 7, 8, 9):
            pieces.append((f"ada{j}", kpiece(ada, 512 * j)))
        pieces.append(("ctxkv", kpiece(w_in2, CH, 2 * KV * HD)))
        pieces.append(("filt4", A["hf_w4_2"][0]))
        pieces += [("wa", kpiece(w_in, 0)), ("wg", kpiece(w_in, CH)), ("wq", kpiece(w_in, 2 * CH)),
                   ("wkv", kpiece(w_in, 3 * CH, 2 * KV * HD))]
        g0 = 3 * CH + 2 * KV * HD
        pieces += [("o0", A["w_conv_out"][0].rearrange("(k p) n -> p k n", p=P)),
                   ("g00", kpiece(w_in, g0)), ("g01", kpiece(w_in, g0 + 512)),
                   ("o1", A["w_attn_out"][0].rearrange("(k p) n -> p k n", p=P)),
                   ("g10", kpiece(w_in, g0 + D)), ("g11", kpiece(w_in, g0 + D + 512)),
                   ("wo0", kpiece(A["w_out"][0], 0)), ("wo1", kpiece(A["w_out"][0], 512))]
        place1 = {n: (i % SLOTS, i // SLOTS + 1) for i, (n, _) in enumerate(pieces)}
        base_use = [len([1 for i in range(len(pieces)) if i % SLOTS == s]) for s in range(SLOTS)]
        h0 = CH + 2 * KV * HD
        g2 = h0 + 3 * CH
        pieces2 = [("q", kpiece(w_in2, 0)), ("kv", kpiece(w_in2, CH, 2 * KV * HD)),
                   ("hy0", kpiece(w_in2, h0)), ("hy1", kpiece(w_in2, h0 + CH)), ("hy2", kpiece(w_in2, h0 + 2 * CH)),
                   ("o0", A["w_attn_out_2"][0].rearrange("(k p) n -> p k n", p=P)),
                   ("g00", kpiece(w_in2, g2)), ("g01", kpiece(w_in2, g2 + 512)),
                   ("o1", A["w_hy_out_2"][0].rearrange("(k p) n -> p k n", p=P)),
                   ("g10", kpiece(w_in2, g2 + D)), ("g11", kpiece(w_in2, g2 + D + 512)),
                   ("m4", kpiece(ada, 2048)), ("m5", kpiece(ada, 2560)),
                   ("wo0", kpiece(A["w_out_2"][0], 0)), ("wo1", kpiece(A["w_out_2"][0], 512)),
                   ("keys", None),
                   ("pq0", kpiece(A["peer_wq_2"][0], 0)), ("pq1", kpiece(A["peer_wq_2"][0], 512)),
                   ("pq2", kpiece(A["peer_wq_2"][0], 1024)), ("pq3", kpiece(A["peer_wq_2"][0], 1536)),
                   ("m10", kpiece(ada, 5120)), ("m11", kpiece(ada, 5632))]
        place2 = {n: (i % SLOTS, i // SLOTS + 1) for i, (n, _) in enumerate(pieces2)}

        def view(slot, src):
            k, n = src.shape[1], src.shape[2]
            return ring[:, slot, 0:k * n].rearrange("p (k n) -> p k n", k=k)

        def pview(places, name, n=512):
            s = places[name][0]
            k = PIECE // n if n != 256 else KD
            return ring[:, s, 0:k * n].rearrange("p (k n) -> p k n", k=k)

        A_cols = dict(g_mix=0, b_dw=8, ln_g=12, ln_b=16, mixg=20, ffng2=28, g_ffn=36, hyw=44, hyb=80, skip=92)

        N_CONST, N_PRM = 3, 18
        ZEROED = ROWS // P + 1 + EXTRA * CAP // P
        stat_cols = {}

        def stat(name, n=NT):
            if name not in stat_cols:
                a = sum(w for _, w in stat_cols.values())
                assert a + n <= 400
                stat_cols[name] = (a, n)
            a, w = stat_cols[name]
            assert w == n
            return st[:, a:a + n]

        def rep_(ap, axis, shape):
            return ap.unsqueeze(axis).to_broadcast(shape)

        groups = {}

        def full(eng, name):
            b, n = groups[name]
            eng.wait_ge(bank_full[b], n)
            return psum[:, b, :]

        def emptied(eng, name):
            b, n = groups[name]
            eng.wait_ge(bank_read[b], n)

        block = ctx.enter_context(nc.Block())

        @block.tensor
        def _(pe):
            fills = [0] * 8
            order = [0]

            def bank(name):
                b = order[0] % 8
                order[0] += 1
                if fills[b]:
                    pe.wait_ge(bank_read[b], fills[b])
                fills[b] += 1
                groups[name] = (b, fills[b])
                return b

            def mm(o, lhsT, rhs, k, n):
                return nc.tensor.matmul(o, lhsT, rhs, start=(k == 0), stop=(k == n - 1))

            def to_T(name, rows, ev_name, n):
                pe.wait_ge(ev(ev_name), n)
                for g in range(4):
                    b = bank(f"{name}{g}")
                    for c in range(2):
                        for t in range(NT):
                            last = nc.tensor.transpose(psum[:, b, c * T + t * P:c * T + t * P + P],
                                                       rows[:, t, (2 * g + c) * P:(2 * g + c + 1) * P], ident[:, :])
                    last.then_inc(bank_full[b], 1)

            def proj_T(name, w, src, nk, chunks):
                for g in range(chunks // 2):
                    b = bank(f"{name}{g}")
                    for c in range(2):
                        m = (2 * g + c) * P
                        for k in range(nk):
                            last = mm(psum[:, b, c * T:(c + 1) * T], w[:, k, m:m + P], src[:, k, :], k, nk)
                    last.then_inc(bank_full[b], 1)

            def landed(places, name):
                s, n = places[name]
                pe.wait_ge((piece_in if places is place1 else piece2_in)[s], 16 * n)

            pe.wait_ge(const_in, 16 * N_CONST)
            pe.wait_ge(prm_in, 16 * N_PRM)
            b = bank("prm")
            nc.tensor.transpose(psum[:, b, 0:100], prm[0:100, 0, :], ident[0:100, 0:100])
            nc.tensor.transpose(psum[:, b, 104:228], prm[0:124, 1, :], ident[0:124, 0:124])
            nc.tensor.transpose(psum[:, b, 228:276], prm[0:48, 2, :], ident[0:48, 0:48])
            nc.tensor.transpose(psum[0:64, b, 276:280], prmD[:, :], ident[0:4, 0:4])
            nc.tensor.transpose(psum[:, b, 280:296], crow[:, :], ident[0:16, 0:16]).then_inc(bank_full[b], 1)

            for i in range(3):
                b = bank(f"f{i}")
                if i == 0:
                    pe.wait_ge(ev("filt_in"), 16 * 4)
                    last = mm(psum[0:64, b, 0:T], w1s, feat, 0, 1)
                else:
                    pe.wait_ge(ev("sine_done"), i)
                    last = mm(psum[0:64, b, 0:T], w23[:, i - 1, :], fsmall[:, 2 * (i - 1), :], 0, 1)
                last.then_inc(bank_full[b], 1)

            pe.wait_ge(ev("sc_ready"), 1)
            for q in range(4):
                b = bank(f"mod{q}")
                for half in range(2):
                    j = (0, 2, 6, 8)[q] + half
                    landed(place1, f"ada{j}")
                    w = pview(place1, f"ada{j}")
                    for m in range(4):
                        o = 2 * (4 * half + m)
                        for k in range(KD):
                            last = mm(psum[:, b, o:o + 2], w[:, k, m * P:(m + 1) * P], scT[:, k, :], k, KD)
                last.then_inc(bank_full[b], 1)
            to_T("cx", scratch, "ctxn_ready", 1)
            landed(place1, "ctxkv")
            for g in range(4):
                emptied(pe, f"cx{g}")
            w = pview(place1, "ctxkv", 256)
            for t in range(NT):
                b = bank(f"ckv{t}")
                for k in range(KD):
                    last = mm(psum[:, b, 0:256], actT[:, k, t * P:(t + 1) * P], w[:, k, :], k, KD)
                last.then_inc(bank_full[b], 1)
            b = bank("ckT")
            pe.wait_ge(ev("ck_ready"), 1)
            for t in range(NT):
                last = nc.tensor.transpose(psum[:, b, t * P:(t + 1) * P], kvt[:, t * 256:t * 256 + P], ident[:, :])
            last.then_inc(bank_full[b], 1)

            pe.wait_ge(ev("sine_done"), 3)
            landed(place1, "filt4")
            w4 = ring[0:64, place1["filt4"][0], 0:2048]
            for t in range(NT):
                for m in range(4):
                    b = bank(f"h{t}{m}")
                    mm(psum[:, b, :], fsmall[:, 4, t * P:(t + 1) * P], w4[:, m * CH:(m + 1) * CH], 0, 1) \
                        .then_inc(bank_full[b], 1)
            pe.wait_ge(ev("tables_in"), 16 * 6)
            for o in range(2):
                b = bank(f"habs{o}")
                for t in range(NT):
                    pe.wait_ge(ev("abs_ready"), NT * o + t + 1)
                    last = mm(psum[:, b, :], ones[:, :], absb[:, t, :], t, NT)
                last.then_inc(bank_full[b], 1)
                pe.wait_ge(ev("ed_ready"), o + 1)
                for part in range(2):
                    for f in range(NT):
                        b = bank(f"sp{o}{part}{f}")
                        for t in range(NT):
                            last = mm(psum[:, b, :], dft[:, part, t, f * P:(f + 1) * P], filt[:, t, 2 * o + part, :], t, NT)
                        last.then_inc(bank_full[b], 1)

            to_T("xn", scratch, "xn_ready", 1)
            for g in range(4):
                emptied(pe, f"xn{g}")
            for name in ("wa", "wg", "wq"):
                landed(place1, name)
                proj_T(name, pview(place1, name), actT, KD, 4)
            landed(place1, "wkv")
            w = pview(place1, "wkv", 256)
            b = bank("k1")
            for k in range(KD):
                last = mm(psum[:, b, 0:T], w[:, k, 0:P], actT[:, k, :], k, KD)
            last.then_inc(bank_full[b], 1)
            b = bank("v1")
            for t in range(NT):
                for k in range(KD):
                    last = mm(psum[:, b, t * P:(t + 1) * P], actT[:, k, t * P:(t + 1) * P], w[:, k, P:2 * P], k, KD)
            last.then_inc(bank_full[b], 1)
            emptied(pe, "wq0")
            emptied(pe, "wq1")
            pe.wait_ge(ev("k1_ready"), 1)

            def score(b, col, h, t, k0, k1):
                r = slice((h % 2) * HD, (h % 2) * HD + HD)
                return mm(psum[:, b, col:col + k1 - k0], qT[r, h // 2, t * P:(t + 1) * P], kdup[r, h // 4, k0:k1], 0, 1)

            for par in range(2):
                b = bank(f"s0{par}")
                for i in range(4):
                    last = score(b, i * P, 2 * i + par, 0, 0, P)
                last.then_inc(bank_full[b], 1)
            for par in range(2):
                for pr in range(2):
                    b = bank(f"s1{par}{pr}")
                    for i in range(2):
                        last = score(b, i * T, 4 * pr + 2 * i + par, 1, 0, T)
                    last.then_inc(bank_full[b], 1)
            pe.wait_ge(ev("p1_ready"), 2)

            def pv1(h):
                r = slice((h % 2) * HD, (h % 2) * HD + HD)
                emptied(pe, f"pt{h}")
                if h % 2 == 0:
                    bank(f"pv{h // 2}")
                b = groups[f"pv{h // 2}"][0]
                g = (h // 4) * HD
                s = pTbuf[:, h % 4, :]
                mm(psum[r, b, 0:P], vtok[:, 0, g:g + HD], s[:, 0:P], 0, 1)
                mm(psum[r, b, P:T], vtok[:, 0, g:g + HD], s[:, P:2 * P], 0, 2)
                last = mm(psum[r, b, P:T], vtok[:, 1, g:g + HD], s[:, 2 * P:3 * P], 1, 2)
                if h % 2:
                    last.then_inc(bank_full[b], 1)
                return last

            emptied(pe, "v1")
            for h in range(HEADS):
                b = bank(f"pt{h}")
                for i, (t, kc) in enumerate(((0, 0), (1, 0), (1, 1))):
                    last = nc.tensor.transpose(psum[:, b, i * P:(i + 1) * P], prob1[:, t, h, kc * P:(kc + 1) * P], ident[:, :])
                last.then_inc(bank_full[b], 1)
                if h:
                    pv1(h - 1)
            pv1(HEADS - 1)
            pe.wait_ge(ev("conv_ready"), 1)
            for t in range(NT):
                b = bank(f"yt{t}")
                for c in range(KC):
                    last = nc.tensor.transpose(psum[:, b, c * P:(c + 1) * P], yT[:, c, t * P:(t + 1) * P], ident[:, :])
                last.then_inc(bank_full[b], 1)
            for g in range(2):
                emptied(pe, "yt0")
                emptied(pe, "yt1")
                b = bank(f"yb{g}")
                for c in range(2):
                    for t in range(NT):
                        last = nc.tensor.transpose(psum[:, b, c * T + t * P:c * T + t * P + P],
                                                   ytok[:, t, (2 * g + c) * P:(2 * g + c + 1) * P], ident[:, :])
                last.then_inc(bank_full[b], 1)

            def merge(pl, tag, branches):
                for br in range(2):
                    src, need = branches[br]
                    for nm in need:
                        emptied(pe, nm)
                    landed(pl, f"o{br}")
                    wo = ring[:, pl[f"o{br}"][0], :].rearrange("p (k n) -> p k n", k=KC)
                    for half in range(2):
                        landed(pl, f"g{br}{half}")
                        wg = pview(pl, f"g{br}{half}")
                        for g in range(2):
                            i = 2 * half + g
                            b = bank(f"{tag}g{br}{i}")
                            for c in range(2):
                                for k in range(KD):
                                    last = mm(psum[:, b, c * T:(c + 1) * T], wg[:, k, (2 * g + c) * P:(2 * g + c + 1) * P],
                                              actT[:, k, :], k, KD)
                            last.then_inc(bank_full[b], 1)
                            b = bank(f"{tag}o{br}{i}")
                            for c in range(2):
                                m = (2 * i + c) * P
                                for k in range(KC):
                                    last = mm(psum[:, b, c * T:(c + 1) * T], wo[:, k, m:m + P], src[:, k, :], k, KC)
                            last.then_inc(bank_full[b], 1)

            def out_proj(pl, tag):
                pe.wait_ge(ev(f"{tag}merged"), 1)
                for n in range(2):
                    landed(pl, f"wo{n}")
                    w = pview(pl, f"wo{n}")
                    for t in range(NT):
                        b = bank(f"{tag}x{t}{n}")
                        for k in range(KD):
                            last = mm(psum[:, b, :], mergedT[:, k, t * P:(t + 1) * P], w[:, k, :], k, KD)
                        last.then_inc(bank_full[b], 1)

            merge(place1, "a", [(yactT, ("yb0", "yb1")), (attnT, tuple(f"pv{i}" for i in range(4)))])
            out_proj(place1, "a")
            to_T("rn", scratch, "rn_ready", 1)
            for g in range(4):
                emptied(pe, f"rn{g}")
            b = bank("route")
            for t in range(NT):
                for k in range(KD):
                    last = mm(psum[:, b, t * 64:t * 64 + 36], actT[:, k, t * P:(t + 1) * P], wroute[:, k, :], k, KD)
            last.then_inc(bank_full[b], 1)
            pe.wait_ge(ev("assign_ready"), 1)
            asg = arena2[:, 512:576].rearrange("p (t e) -> p t e", t=NT)
            b = bank("pos")
            mm(psum[:, b, 0:32], before[:, :], asg[:, 0, :], 0, 1)
            mm(psum[:, b, 32:64], ones[:, :], asg[:, 0, :], 0, 2)
            mm(psum[:, b, 32:64], before[:, :], asg[:, 1, :], 1, 2)
            mm(psum[:, b, 64:96], ones[:, :], asg[:, 0, :], 0, 2)
            mm(psum[:, b, 64:96], ones[:, :], asg[:, 1, :], 1, 2).then_inc(bank_full[b], 1)
            for b in range(8):
                pe.wait_ge(bank_read[b], fills[b])

            pe.wait_ge(ev("trips_ready"), 1)
            n_iter = pe.value_load(trips[0:1, 0:1], min_val=STEPS, max_val=MAXSTEPS)
            pe.sem_inc(ev("rowsT_full1"), 1)
            pe.sem_inc(ev("down_full1"), 1)

            def rows_T(h, n):
                pe.wait_ge(ev(f"rows_in{h}"), 16 * n)
                pe.sem_inc(pe_step, 1)
                for c in range(KD):
                    last = nc.tensor.transpose(psum[:, 0, c * CAP:(c + 1) * CAP], xrow[:, h, c * P:(c + 1) * P],
                                               ident[0:CAP, 0:CAP])
                last.then_inc(ev(f"rowsT_full{h}"), 1)

            pe.wait_ge(ev("rows_in0"), 16)
            rows_T(0, 1)
            with pe.Fori(0, n_iter) as i:
                def up(h, j):
                    s = 3 * h + j
                    pe.wait_ge(piece_in[s], 16 * i + 16 * (base_use[s] + 1))
                    if j == 0:
                        pe.wait_ge(ev(f"rowsT_ready{h}"), i + 1)
                    w = ring[:, s, :].rearrange("p (k n) -> p k n", k=KD)
                    for k in range(KD):
                        last = mm(psum[0:CAP, 2 + 2 * h + j, :], xT[:, h, k, :], w[:, k, :], k, KD)
                    last.then_inc(ev(("gate_full", "up_full")[j] + str(h)), 1)

                def hid_T(h):
                    pe.wait_ge(ev(f"hid_ready{h}"), i + 1)
                    pe.sem_inc(pe_step, 1)
                    for k in range(4):
                        last = nc.tensor.transpose(psum[:, 1, (4 * h + k) * CAP:(4 * h + k + 1) * CAP],
                                                   hrow[:, h, k * P:(k + 1) * P], ident[0:CAP, 0:CAP])
                    last.then_inc(ev(f"hidT_full{h}"), 1)

                def down(h, n):
                    s = 3 * h + 2
                    if n == 0:
                        pe.wait_ge(piece_in[s], 16 * i + 16 * (base_use[s] + 1))
                        pe.wait_ge(ev(f"hidT_ready{h}"), i + 1)
                    w = ring[:, s, :].rearrange("p (k n) -> p k n", k=4)
                    pe.wait_ge(ev(f"down_read{n}"), 2 * i + h + 1)
                    for k in range(4):
                        last = mm(psum[0:CAP, 6 + n, :], hidT[:, h, k, :], w[:, k, n * 512:(n + 1) * 512], k, 4)
                    last.then_inc(ev(f"down_full{n}"), 1)

                up(0, 0)
                rows_T(1, i + 1)
                up(0, 1)
                up(1, 0)
                hid_T(0)
                up(1, 1)
                down(0, 0)
                hid_T(1)
                down(0, 1)
                rows_T(0, i + 2)
                down(1, 0)
                down(1, 1)

            pe.wait_ge(ev("down_read0"), n_iter * 2 + 1)
            pe.wait_ge(ev("down_read1"), n_iter * 2 + 1)
            to_T("zn", scratch, "zn_ready", 1)
            for g in range(4):
                emptied(pe, f"zn{g}")
            landed(place2, "q")
            w = pview(place2, "q")
            for t in range(NT):
                b = bank(f"q{t}")
                for k in range(KD):
                    last = mm(psum[:, b, :], actT[:, k, t * P:(t + 1) * P], w[:, k, :], k, KD)
                last.then_inc(bank_full[b], 1)
            landed(place2, "kv")
            w = pview(place2, "kv", 256)
            for t in range(NT):
                b = bank(f"kv{t}")
                for k in range(KD):
                    last = mm(psum[:, b, 0:256], actT[:, k, t * P:(t + 1) * P], w[:, k, :], k, KD)
                last.then_inc(bank_full[b], 1)
            for j in range(3):
                landed(place2, f"hy{j}")
                proj_T(f"hy{j}", pview(place2, f"hy{j}"), actT, KD, 4)
            pe.wait_ge(ev("qk2_ready"), 1)
            for g in range(2):
                b = bank(f"qT{g}")
                for c in range(2):
                    for t in range(NT):
                        last = nc.tensor.transpose(psum[:, b, c * T + t * P:c * T + t * P + P],
                                                   qtok[:, t, (2 * g + c) * P:(2 * g + c + 1) * P], ident[:, :])
                last.then_inc(bank_full[b], 1)
            b = bank("kT")
            for t in range(NT):
                last = nc.tensor.transpose(psum[:, b, t * P:(t + 1) * P], ktok[:, t, :], ident[:, :])
            last.then_inc(bank_full[b], 1)
            emptied(pe, "qT0")
            emptied(pe, "qT1")
            pe.wait_ge(ev("k2_ready"), 1)
            units = [(h, t) for h in range(HEADS) for t in range(NT)]

            def score2(u):
                h, t = units[u]
                b = bank(f"sc{u}")
                score(b, 0, h, t, 0, 2 * T).then_inc(bank_full[b], 1)

            def pt2(u):
                pe.wait_ge(ev("p2_ready"), u + 1)
                b = bank(f"qt{u}")
                for kc in range(4):
                    last = nc.tensor.transpose(psum[:, b, kc * P:(kc + 1) * P], prob2[:, u % 8, kc * P:(kc + 1) * P], ident[:, :])
                last.then_inc(bank_full[b], 1)

            def pv2(u):
                h, t = units[u]
                emptied(pe, f"qt{u}")
                if u % 4 == 0:
                    bank(f"pw{h // 2}")
                b = groups[f"pw{h // 2}"][0]
                r = slice((h % 2) * HD, (h % 2) * HD + HD)
                for kc in range(4):
                    last = mm(psum[r, b, t * P:(t + 1) * P], vtok[:, kc, (h // 4) * HD:(h // 4 + 1) * HD],
                              pTbuf[:, u % 4, kc * P:(kc + 1) * P], kc, 4)
                if u % 4 == 3:
                    last.then_inc(bank_full[b], 1)

            score2(0)
            score2(1)
            for u in range(16):
                if u + 2 < 16:
                    score2(u + 2)
                pt2(u)
                if u:
                    pv2(u - 1)
            pv2(15)

            def rows_of(name, src, ready, n):
                pe.wait_ge(ev(ready), n)
                for t in range(NT):
                    b = bank(f"{name}{t}")
                    for c in range(KC):
                        last = nc.tensor.transpose(psum[:, b, c * P:(c + 1) * P], src[:, c, t * P:(t + 1) * P], ident[:, :])
                    last.then_inc(bank_full[b], 1)

            for o in range(2):
                rows_of(f"vt{o}", (zs[:, 0:4, :], y1T)[o], ("short_ready", "y1_ready")[o], 1)
                emptied(pe, f"vt{o}0")
                emptied(pe, f"vt{o}1")
                for part in range(2):
                    for f in range(NT):
                        b = bank(f"U{o}{part}{f}")
                        for t in range(NT):
                            last = mm(psum[:, b, :], dft[:, part, t, f * P:(f + 1) * P], vtime[:, t, :], t, NT)
                        last.then_inc(bank_full[b], 1)
                pe.wait_ge(ev("Y_ready"), o + 1)
                for g in range(2):
                    b = bank(f"I{o}{g}")
                    for c in range(2):
                        for k in range(4):
                            last = mm(psum[:, b, c * T:(c + 1) * T], Y[:, k, (2 * g + c) * P:(2 * g + c + 1) * P], idft[:, k, :], k, 4)
                    last.then_inc(bank_full[b], 1)
            pe.wait_ge(ev("hy_ready"), 1)
            merge(place2, "b", [(attnT, tuple(f"pw{i}" for i in range(4))), (hyoT, ())])

            def row_mod(tag, names):
                for j, nm in enumerate(names):
                    landed(place2, nm)
                    w = pview(place2, nm)
                    b = bank(f"{tag}{j}")
                    for k in range(KD):
                        last = mm(psum[:, b, :], scT[:, k, 0:1].to_broadcast([P, P]), w[:, k, :], k, KD)
                    last.then_inc(bank_full[b], 1)

            row_mod("G1", ("m4", "m5"))
            out_proj(place2, "b")
            pe.wait_ge(ev("keys1_in"), 16)
            landed(place2, "keys")
            kp = ring[:, place2["keys"][0], 0:2048].rearrange("p (c d) -> p c d", d=P)
            for g in range(4):
                b = bank(f"keyT{g}")
                for c in range(4):
                    last = nc.tensor.transpose(psum[:, b, c * P:(c + 1) * P], kp[:, 4 * g + c, :], ident[:, :])
                last.then_inc(bank_full[b], 1)
            to_T("pn", scratch, "pn_ready", 1)
            for g in range(4):
                emptied(pe, f"pn{g}")
            for j in range(4):
                landed(place2, f"pq{j}")
                proj_T(f"pq{j}", pview(place2, f"pq{j}"), actT, KD, 4)
            for t in range(NT):
                for n in range(2):
                    b = bank(f"xp{t}{n}")
                    for c in range(4):
                        last = nc.tensor.transpose(psum[:, b, c * P:(c + 1) * P], actT[:, 4 * n + c, t * P:(t + 1) * P], ident[:, :])
                    last.then_inc(bank_full[b], 1)
            for g in range(4):
                emptied(pe, f"keyT{g}")
            for j in range(4):
                for g in range(2):
                    emptied(pe, f"pq{j}{g}")
            for t in range(NT):
                for g in range(4):
                    b = bank(f"ks{t}{g}")
                    for i in range(4):
                        h, half = (4 * g + i) // 2, (4 * g + i) % 2
                        last = mm(psum[:, b, i * P:(i + 1) * P], pqT[:, 2 * h + half, t * P:(t + 1) * P],
                                  keysT[:, half * 8 + h, :], 0, 1)
                    last.then_inc(bank_full[b], 1)
            row_mod("G2", ("m10", "m11"))

        @block.sync
        def _(sp):
            sp.dma_start(ident[:, :], A["c_ident"]).then_inc(const_in, 16)
            rows_A = [("g_mix", 8), ("b_dw", 4), ("ln_conv_g", 4), ("ln_conv_b", 4), ("norm_mix_g_2", 8),
                      ("norm_ffn_g_2", 8), ("g_ffn", 8)]
            r = 0
            for nm, n in rows_A:
                sp.dma_start(prm[r:r + n, 0, :], A[nm][0].rearrange("(r c) -> r c", c=P)).then_inc(prm_in, 16)
                r += n
            sp.dma_start(prm[r:r + 36, 0, :], A["hy_conv_w_2"][0].rearrange("j (r c) -> (j r) c", c=P)).then_inc(prm_in, 16)
            r += 36
            sp.dma_start(prm[r:r + 12, 0, :], A["hy_conv_b_2"][0].rearrange("(r c) -> r c", c=P)).then_inc(prm_in, 16)
            r += 12
            sp.dma_start(prm[r:r + 8, 0, :], A["hy_skip_2"][0].rearrange("j (r c) -> (j r) c", c=P)).then_inc(prm_in, 16)
            assert r + 8 == 100
            sp.dma_start(prm[0:124, 1, :], A["w_dw"][0, :, 0, :].rearrange("j (r c) -> (j r) c", c=P)).then_inc(prm_in, 16)
            sp.dma_start(prm[0:48, 2, :], A["ada_b_2"][0].rearrange("(r c) -> r c", c=P)).then_inc(prm_in, 16)
            for i, nm in enumerate(("hf_b1_2", "hf_b2_2", "hf_b3_2", "hf_freq_2")):
                sp.dma_start(prmD[i:i + 1, :], A[nm]).then_inc(prm_in, 16)
            sp.dma_start(crow[0:8, :], A["c_2"][0].rearrange("(r c) -> r c", c=P)).then_inc(prm_in, 16)
            sp.dma_start(crow[8:16, :], A["c_ctx_2"].rearrange("(r c) -> r c", c=P)).then_inc(prm_in, 16)
            sp.dma_start(resid[:, :, :], A["ctx_2"][0].rearrange("(t p) d -> p t d", p=P)).then_inc(ctx_in, 16)
            sp.dma_start(w1s, A["hf_w1_2"][0]).then_inc(ev("filt_in"), 16)
            sp.dma_start(feat, A["c_feat"]).then_inc(ev("filt_in"), 16)
            sp.dma_start(w23[:, 0, :], A["hf_w2_2"][0]).then_inc(ev("filt_in"), 16)
            sp.dma_start(w23[:, 1, :], A["hf_w3_2"][0]).then_inc(ev("filt_in"), 16)

            last_reader = {"ada0": "mod0", "ada1": "mod0", "ada2": "mod1", "ada3": "mod1", "ada6": "mod2", "ada7": "mod2",
                           "ada8": "mod3", "ada9": "mod3", "ctxkv": "ckv1", "filt4": "h13", "wa": "wa1", "wg": "wg1",
                           "wq": "wq1", "wkv": "v1", "o0": "ao03", "g00": "ag01", "g01": "ag03", "o1": "ao13",
                           "g10": "ag11", "g11": "ag13", "wo0": "ax10", "wo1": "ax11"}

            def filled(name):
                b, n = groups[name]
                sp.wait_ge(bank_full[b], n)

            for i, (nm, src) in enumerate(pieces):
                s = i % SLOTS
                if i >= SLOTS:
                    filled(last_reader[pieces[i - SLOTS][0]])
                dst = ring[0:64, s, 0:2048] if nm == "filt4" else view(s, src)
                sp.dma_start(dst, src).then_inc(piece_in[s], 16)
                if i == 3:
                    for dstt, cn in ((before, "c_before"), (rel, "c_rel"), (iota, "c_iota")):
                        sp.dma_start(dstt[:, :], A[cn]).then_inc(ev("tables_in"), 16)
                    sp.dma_start(dft[:, :, :, :], A["c_dft"]).then_inc(ev("tables_in"), 16)
                    sp.dma_start(idft[:, :, :], A["c_idft"]).then_inc(ev("tables_in"), 16)
                    sp.dma_start(rope[:, :, :, :], A["c_rope"]).then_inc(ev("tables_in"), 16)
                    sp.dma_start(tok2[:, :, :], A["c_decay"].rearrange("p a m c -> p a (m c)")).then_inc(dec_in, 16)
                if nm == "filt4":
                    sp.wait_ge(ev("ctxn_ready"), 1)
                    sp.dma_start(resid[:, :, :], A["x"][0].rearrange("(t p) d -> p t d", p=P)).then_inc(x_in, 16)

            def expert_piece(s, e):
                h, j = s // 3, s % 3
                w = (A["w_gate"], A["w_up"], A["w_down"])[j][0]
                src = w[e, :, :] if isinstance(e, int) else w[bass.ds(e, 1), :, :].rearrange("e k n -> (e k) n")
                k = 4 if j == 2 else KD
                sp.dma_start(ring[:, s, :].rearrange("p (k n) -> p k n", k=k),
                             src.rearrange("(k p) n -> p k n", p=P)).then_inc(piece_in[s], 16)

            for s in range(SLOTS):
                prev = [nm for i, (nm, _) in enumerate(pieces) if i % SLOTS == s][-1]
                filled(last_reader[prev])
                expert_piece(s, s // 3)

            def expert_step(i, experts):
                for s in range(SLOTS):
                    h = s // 3
                    if s % 3 < 2:
                        sp.wait_ge(ev(("gate_full", "up_full")[s % 3] + str(h)), i)
                    else:
                        sp.wait_ge(ev("down_full1"), 2 * i + h)
                    expert_piece(s, experts[h])

            with sp.Fori(1, STEPS - 1) as i:
                expert_step(i, (2 * i, 2 * i + 1))
            sp.wait_ge(ev("trips_ready"), 1)
            n_iter = sp.value_load(trips[0:1, 0:1], min_val=STEPS, max_val=MAXSTEPS)
            with sp.Fori(STEPS - 1, n_iter) as i:
                expert_step(i, [sp.value_load(elist[0:1, bass.ds(i * 2 + h, 1)], min_val=0, max_val=EXPERTS - 1) for h in range(2)])

            last2 = {"q": "q1", "kv": "kv1", "hy0": "hy01", "hy1": "hy11", "hy2": "hy21", "o0": "bo03", "g00": "bg01",
                     "g01": "bg03", "o1": "bo13", "g10": "bg11", "g11": "bg13", "m4": "G10", "m5": "G11",
                     "wo0": "bx10", "wo1": "bx11", "keys": "keyT3", "pq0": "pq01", "pq1": "pq11", "pq2": "pq21",
                     "pq3": "pq31"}
            for i, (nm, src) in enumerate(pieces2):
                s = i % SLOTS
                if i < SLOTS:
                    if s % 3 < 2:
                        sp.wait_ge(ev(("gate_full", "up_full")[s % 3] + str(s // 3)), n_iter)
                    else:
                        sp.wait_ge(ev("down_full1"), 2 * n_iter + s // 3)
                else:
                    filled(last2[pieces2[i - SLOTS][0]])
                if nm == "keys":
                    kp = ring[:, s, 0:2048].rearrange("p (a h d) -> p a h d", a=2, d=P)
                    for half, knm in enumerate(("peer_keys1_2", "peer_keys2_2")):
                        sp.dma_start(kp[:, half, :, :], A[knm][0].rearrange("h n d -> n h d")).then_inc(
                            (ev("keys1_in"), piece2_in[s])[half], 16)
                    continue
                sp.dma_start(view(s, src), src).then_inc(piece2_in[s], 16)
                if nm == "q":
                    sp.wait_ge(ev("amerged"), 1)
                    sp.dma_start(gfrow, A["g_final"].rearrange("(a n) -> a n", a=1).to_broadcast([P, D])).then_inc(ev("gf_in"), 16)
                if nm == "g11":
                    filled("pw3")
                    sp.dma_start(g1row, A["ada_b_2"][:, 2 * D:3 * D].to_broadcast([P, D])).then_inc(ev("g1_in"), 16)
                if nm == "m11":
                    filled("pq11")
                    sp.dma_start(g2row, A["ada_b_2"][:, 5 * D:6 * D].to_broadcast([P, D])).then_inc(ev("g2_in"), 16)
                    sp.dma_start(flrow, A["final_norm_g_2"].rearrange("(a n) -> a n", a=1).to_broadcast([P, D])).then_inc(ev("g2_in"), 16)
            for t in range(NT):
                sp.wait_ge(ev("final_ready"), t + 1)
                sp.dma_start(out[0, t * P:(t + 1) * P, :], resid[:, t, :]).then_inc(ev("out_sent"), 16)
            sp.wait_ge(ev("out_sent"), 16 * NT)

        @block.gpsimd
        def _(pool):
            steps = [0]

            def own(ins):
                steps[0] += 1
                ins.then_inc(pool_step, 1)
                pool.wait_ge(pool_step, steps[0])

            nc.gpsimd.memset(ones[:, :], 1.0).then_inc(const_in, 16)
            nc.gpsimd.memset(epscol[:, :], EPS).then_inc(const_in, 16)
            own(nc.gpsimd.memset(zeros, 0.0))
            for dst, nm in ((rbias[:, 0:GROUPS], "b_group"), (rbias[:, GROUPS:], "b_expert"), (sinkrow[:, :], "sinks"),
                            (qkg[:, 0, :], "q_norm_g_2"), (qkg[:, 1, :], "k_norm_g_2")):
                pool.dma_start(dst, A[nm].to_broadcast([P, A[nm].shape[1]])).then_inc(ev("rows_in"), 16)
            pool.dma_start(wroute[:, :, 0:GROUPS], A["w_group"][0].rearrange("(k p) n -> p k n", p=P)).then_inc(ev("rows_in"), 16)
            pool.dma_start(wroute[:, :, GROUPS:], A["w_expert"][0].rearrange("(k p) n -> p k n", p=P)).then_inc(ev("rows_in"), 16)
            for b in range(ROWS // P + 1):
                pool.dma_start(xs[b * P:(b + 1) * P, :], zeros).then_inc(ev("zeroed"), 16)
            for b in range(EXPERTS * CAP // P, ROWS // P):
                pool.dma_start(ys[b * P:(b + 1) * P, :], zeros).then_inc(ev("zeroed"), 16)
            pool.wait_ge(ev("trips_ready"), 1)
            n_iter = pool.value_load(trips[0:1, 0:1], min_val=STEPS, max_val=MAXSTEPS)
            pool.wait_ge(ev("zeroed"), 16 * ZEROED)
            pool.wait_ge(ev("rn_ready"), 1)
            for t in range(NT):
                for k in range(2):
                    pool.indirect_dma_start(out=xs[:, :], out_offset=bass.IndirectOffsetOnAxis(ap=sloti[:, 2 * t + k:2 * t + k + 1], axis=0),
                                            in_=scratch[:, t, :], in_offset=None).then_inc(ev("sent"), 16)
            pool.wait_ge(ev("sent"), 16 * 2 * NT)
            pool.dma_start(xrow[:, 0, :], xs[0:CAP, :]).then_inc(ev("rows_in0"), 16)
            with pool.Fori(0, n_iter) as i:
                pool.wait_ge(ev("rowsT_full1"), i + 1)
                pool.sem_inc(pool_step, 1)
                pool.dma_start(xrow[:, 1, :], xs[bass.ds((i * 2 + 1) * CAP, CAP), :]).then_inc(ev("rows_in1"), 16)
                pool.wait_ge(ev("rowsT_full0"), i + 1)
                pool.sem_inc(pool_step, 1)
                pool.dma_start(xrow[:, 0, :], xs[bass.ds((i * 2 + 2) * CAP, CAP), :]).then_inc(ev("rows_in0"), 16)
            pool.wait_ge(ev("stored0"), n_iter * 16 + 1)
            pool.sem_inc(pool_step, 1)
            pool.wait_ge(ev("stored1"), n_iter * 16 + 1)
            pool.sem_inc(pool_step, 1)
            for j in range(4):
                pool.indirect_dma_start(out=back[:, j, :], out_offset=None, in_=ys[:, :],
                                        in_offset=bass.IndirectOffsetOnAxis(ap=sloti[:, j:j + 1], axis=0)).then_inc(ev("fetched"), 16)

            filled_b, filled_n = groups["G21"]
            pool.wait_ge(bank_full[filled_b], filled_n)
            per = PICKS // ROWBUFS
            for r, tab in enumerate(("peer_u_2", "peer_v_2")):
                for t in range(NT):
                    if r == 0:
                        pool.wait_ge(ev("rowid_ready"), t + 1)
                    with pool.Fori(0, per) as i:
                        for b in range(ROWBUFS):
                            pool.wait_ge(ev("row_used"), (i + (2 * r + t) * per) * ROWBUFS + b + 1)
                            pool.sem_inc(pool_step, 1)
                            nc.gpsimd.tensor_copy(cur[:, b:b + 1], rowid[:, t, bass.ds(i * ROWBUFS + b, 1)]).then_inc(ev("cur_set"), 1)
                            pool.wait_ge(ev("cur_set"), (i + (2 * r + t) * per) * ROWBUFS + b + 1)
                            pool.sem_inc(pool_step, 1)
                            pool.indirect_dma_start(out=rows[:, b, :], out_offset=None, in_=A[tab][0],
                                                    in_offset=bass.IndirectOffsetOnAxis(ap=cur[:, b:b + 1], axis=0)).then_inc(ev(f"row_in{b}"), 16)

        @block.scalar
        def _(act):
            counts = {}

            def a(ins, name=None):
                s = ev(name) if name else act_step
                counts[s.name] = counts.get(s.name, 0) + 1
                ins.then_inc(s, 1)
                act.wait_ge(s, counts[s.name])

            def last(ins, name):
                b, n = groups[name]
                ins.then_inc(bank_read[b], 1)
                act.wait_ge(bank_read[b], n)

            def squares(tag, src):
                for t in range(NT):
                    a(nc.scalar.activation(scratch[:, t, :], src[:, t, :], ACT.Square, accum_out=stat(f"{tag}_ss")[:, t:t + 1]))
                a(nc.scalar.activation(stat(f"{tag}_sd"), stat(f"{tag}_ss"), ACT.Sqrt, bias=epscol[:, 0:1], scale=1.0 / D), f"{tag}_sd")

            def take_T(name, scale, bias=None):
                for g in range(4):
                    ps = full(act, f"{name}{g}")
                    for c in range(2):
                        k = 2 * g + c
                        kw = {} if bias is None else {"bias": bias[:, k:k + 1]}
                        ins = nc.scalar.activation(actT[:, k, :], ps[:, c * T:(c + 1) * T], ACT.Identity, scale=scale[:, k:k + 1], **kw)
                    last(ins, f"{name}{g}")

            def copy_out(name, dst, w=512, func=ACT.Copy, **kw):
                last(nc.scalar.activation(dst, full(act, name)[:, 0:w], func, **kw), name)

            act.wait_ge(const_in, 16 * N_CONST)
            act.wait_ge(ctx_in, 16)
            squares("cx", resid)
            act.wait_ge(ev("cols_ready"), 1)
            ps = full(act, "prm")
            last(nc.scalar.activation(scT[:, :, :].rearrange("p k j -> p j k"), ps[:, 280:296].rearrange("p (j k) -> p j k", j=2), ACT.Silu), "prm")
            a(nc.scalar.activation(epscol[:, 0:1], epscol[:, 0:1], ACT.Copy), "sc_ready")
            for i in range(3):
                act.wait_ge(ev("sine_arg"), i + 1)
                a(nc.scalar.activation(fsmall[:, 2 * i, :], fsmall[:, 2 * i + 1, :], ACT.Sin), "sine_done")
            act.wait_ge(ev("modsc_ready"), 1)
            take_T("cx", modsc[:, 1, :], mod[:, 0:KD, 1])
            act.wait_ge(ev("ck_ss"), 1)
            a(nc.scalar.activation(stat("ck_sd", 4), stat("ck_ss", 4), ACT.Sqrt, bias=epscol[:, 0:1], scale=1.0 / HD), "ck_sd")

            act.wait_ge(x_in, 16)
            act.wait_ge(ev("ck_sq_done"), 1)
            squares("xn", resid)
            take_T("xn", colsA[:, 0:8])
            act.wait_ge(ev("filters_ready"), 1)
            for g in range(2):
                copy_out(f"wa{g}", aT[:, 2 * g:2 * g + 2, :].rearrange("p c t -> p (c t)"))
            for g in range(2):
                copy_out(f"wg{g}", sgT[:, 2 * g:2 * g + 2, :].rearrange("p c t -> p (c t)"), func=ACT.Sigmoid)
            for g in range(2):
                copy_out(f"wq{g}", qT[:, 2 * g:2 * g + 2, :].rearrange("p c t -> p (c t)"))
            copy_out("v1", vtok[:, 0:2, :].rearrange("p t c -> p (t c)"), 256)
            for par in range(2):
                ps = full(act, f"s0{par}").rearrange("p (i k) -> p i k", i=4)
                dst = prob1[:, 0, :, 0:P].rearrange("p (i r) k -> p r i k", r=2)[:, par, :, :]
                last(nc.scalar.activation(dst, ps, ACT.Copy, scale=HD ** -0.5), f"s0{par}")
            for par in range(2):
                for pr in range(2):
                    ps = full(act, f"s1{par}{pr}").rearrange("p (i k) -> p i k", i=2)
                    dst = prob1[:, 1, 4 * pr:4 * pr + 4, :].rearrange("p (i r) k -> p r i k", r=2)[:, par, :, :]
                    last(nc.scalar.activation(dst, ps, ACT.Copy, scale=HD ** -0.5), f"s1{par}{pr}")
            for t in range(NT):
                act.wait_ge(ev("p1_shift"), t + 1)
                w = P * (t + 1)
                a(nc.scalar.activation(prob1[:, t, :, 0:w], prob1[:, t, :, 0:w], ACT.Exp))
                a(nc.scalar.activation(stat("p1_es", 16)[:, 8 * t:8 * t + 8], stat("p1_sm", 16)[:, 8 * t:8 * t + 8], ACT.Exp), "p1_exp")
            act.wait_ge(ev("zeroed"), 16 * ZEROED)
            for h in range(HEADS):
                copy_out(f"pt{h}", pTbuf[:, h % 4, 0:384], 384)
                if h % 2 == 0 and h:
                    copy_out(f"pv{h // 2 - 1}", attnT[:, h // 2 - 1, :], T)
            copy_out("pv3", attnT[:, 3, :], T)
            act.wait_ge(ev("ln_var"), 1)
            a(nc.scalar.activation(stat("ln_sd"), stat("ln_v"), ACT.Sqrt, bias=epscol[:, 0:1]), "ln_sd")
            for g in range(2):
                ps = full(act, f"yb{g}")
                for c in range(2):
                    k = 2 * g + c
                    ins = nc.scalar.activation(yactT[:, k, :], ps[:, c * T:(c + 1) * T], ACT.Silu, scale=colsA[:, 12 + k:13 + k], bias=colsA[:, 16 + k:17 + k])
                last(ins, f"yb{g}")

            def gates_of(tag):
                for j in range(8):
                    br, i = j // 4, j % 4
                    if j >= 2:
                        emptied(act, f"{tag}o{(j - 2) // 4}{(j - 2) % 4}")
                    copy_out(f"{tag}g{br}{i}", sgate[:, j % 2, :], func=ACT.Sigmoid)

            gates_of("a")
            act.wait_ge(ev("ah_ready"), 1)
            squares("rn", resid)
            take_T("rn", colsA[:, 36:44])
            act.wait_ge(ev("rt_gmax"), 1)
            for t in range(NT):
                a(nc.scalar.activation(rt[:, 600 + 4 * t:604 + 4 * t], rt[:, 72 + 36 * t:76 + 36 * t], ACT.Exp, bias=stat("rt_ng")[:, t:t + 1],
                                       accum_out=stat("rt_gs")[:, t:t + 1]), "rt_gsum")
            act.wait_ge(ev("rt_top"), 1)
            for t in range(NT):
                a(nc.scalar.activation(stat("rt_e1")[:, t:t + 1], rt[:, 144 + 8 * t + 1:144 + 8 * t + 2], ACT.Exp, bias=stat("rt_nv")[:, t:t + 1]), "rt_e1")

            act.wait_ge(ev("trips_ready"), 1)
            n_iter = act.value_load(trips[0:1, 0:1], min_val=STEPS, max_val=MAXSTEPS)
            act.sem_inc(ev("down_read0"), 1)
            act.sem_inc(ev("stored0"), 1)
            act.sem_inc(ev("stored1"), 1)
            with act.Fori(0, n_iter) as i:
                for h in range(2):
                    act.wait_ge(ev(f"gate_full{h}"), i + 1)
                    nc.scalar.activation(silu[:, h, :], psum[0:CAP, 2 + 2 * h, :], ACT.Silu).then_inc(ev(f"silu_ready{h}"), 1)

                def hid_out(h):
                    act.wait_ge(ev(f"hidT_full{h}"), i + 1)
                    nc.scalar.activation(hidT[:, h, :, :].rearrange("p k c -> p (k c)"), psum[:, 1, h * 256:(h + 1) * 256],
                                         ACT.Copy).then_inc(ev(f"hidT_ready{h}"), 1)

                def down_out(h):
                    act.wait_ge(ev("down_full0"), 2 * i + h + 1)
                    act.wait_ge(ev(f"stored{h}"), 16 * i + 1)
                    nc.scalar.activation(yrow[:, h, 0:512], psum[0:CAP, 6, :], ACT.Copy).then_inc(ev("down_read0"), 1)

                def store(h):
                    act.wait_ge(ev("down_read0"), 2 * i + h + 2)
                    act.wait_ge(ev("down_read1"), 2 * i + h + 2)
                    act.dma_start(ys[bass.ds((i * 2 + h) * CAP, CAP), :], yrow[:, h, :]).then_inc(ev(f"stored{h}"), 16)

                hid_out(0)
                down_out(0)
                hid_out(1)
                store(0)
                down_out(1)
                store(1)

            act.wait_ge(ev("moe_added"), 1)
            squares("fn", resid)
            act.wait_ge(ev("x2_ready"), 1)
            squares("zn", resid)
            take_T("zn", modsc[:, 0, :], mod[:, 0:KD, 0])
            for t in range(NT):
                copy_out(f"q{t}", qtok[:, t, :])
            act.wait_ge(ev("qk_ss"), 1)
            a(nc.scalar.activation(stat("qk_sd", 20), stat("qk_ss", 20), ACT.Sqrt, bias=epscol[:, 0:1], scale=1.0 / HD), "qk_sd")
            for j in range(6):
                if j == 0:
                    act.wait_ge(ev("pads_zero"), 1)
                if j >= 2:
                    act.wait_ge(ev("short_done"), j - 1)
                ps = full(act, f"hy{j // 2}{j % 2}").rearrange("p (c t) -> p c t", c=2)
                last(nc.scalar.activation(hpad[:, j % 2, :, 1:T + 1], ps, ACT.Copy), f"hy{j // 2}{j % 2}")
            for g in range(2):
                copy_out(f"qT{g}", qT[:, 2 * g:2 * g + 2, :].rearrange("p c t -> p (c t)"))

            def exp_unit(u):
                act.wait_ge(ev("nmax"), u + 1)
                if u >= 8:
                    full(act, f"qt{u - 8}")
                else:
                    full(act, "kT")
                last(nc.scalar.activation(prob2[:, u % 8, :], full(act, f"sc{u}"), ACT.Exp, bias=stat("nm2", 16)[:, u:u + 1], scale=HD ** -0.5,
                                          accum_out=stat("sum2", 16)[:, u:u + 1]), f"sc{u}")

            exp_unit(0)
            for u in range(16):
                if u + 1 < 16:
                    exp_unit(u + 1)
                copy_out(f"qt{u}", pTbuf[:, u % 4, :])
                if u % 4 == 0 and u:
                    copy_out(f"pw{u // 4 - 1}", attnT[:, u // 4 - 1, :], T)
            copy_out("pw3", attnT[:, 3, :], T)
            for o in range(2):
                for t in range(NT):
                    copy_out(f"vt{o}{t}", vtime[:, t, :])
                for part in range(2):
                    for f in range(NT):
                        copy_out(f"U{o}{part}{f}", Usb[:, 2 * part + f, :])
            act.wait_ge(ev("hy_ready"), 1)
            gates_of("b")
            for g in range(4):
                copy_out(f"keyT{g}", keysT[:, 4 * g:4 * g + 4, :].rearrange("p c n -> p (c n)"))
            act.wait_ge(ev("bh_ready"), 1)
            squares("pn", resid)
            take_T("pn", modsc[:, 2, :], mod[:, 24:32, 0])
            for j in range(4):
                for g in range(2):
                    k = 4 * j + 2 * g
                    copy_out(f"pq{j}{g}", pqT[:, k:k + 2, :].rearrange("p c t -> p (c t)"))
            for t in range(NT):
                for n in range(2):
                    copy_out(f"xp{t}{n}", tok2[:, t, n * 512:(n + 1) * 512])
            for t in range(NT):
                for g in range(4):
                    copy_out(f"ks{t}{g}", S[:, t, 4 * g:4 * g + 4, :].rearrange("p c n -> p (c n)"))
            for t in range(NT):
                act.wait_ge(ev("best_shift"), t + 1)
                a(nc.scalar.activation(gates[:, t, :], gates[:, t, :], ACT.Exp), "best_exp")
            for t in range(NT):
                act.wait_ge(ev("dots_ready"), t + 1)
                a(nc.scalar.activation(dots[:, t, :], dots[:, t, :], ACT.Gelu_apprx_tanh), "gelu_done")
            for t in range(NT):
                act.wait_ge(ev("x3_ready"), t + 1)
                a(nc.scalar.activation(tok2[:, t, :], resid[:, t, :], ACT.Square, accum_out=stat("ff_ss")[:, t:t + 1]))
                a(nc.scalar.activation(stat("ff_sd")[:, t:t + 1], stat("ff_ss")[:, t:t + 1], ACT.Sqrt, bias=epscol[:, 0:1], scale=1.0 / D), "ff_sd")

        @block.vector
        def _(dve):
            counts = {}
            V = nc.vector

            def v(ins, name=None):
                s = ev(name) if name else dve_step
                counts[s.name] = counts.get(s.name, 0) + 1
                ins.then_inc(s, 1)
                dve.wait_ge(s, counts[s.name])

            def last(ins, name):
                b, n = groups[name]
                ins.then_inc(bank_read[b], 1)
                dve.wait_ge(bank_read[b], n)

            def norm_rows(tag, src, name):
                dve.wait_ge(ev(f"{tag}_sd"), 1)
                v(V.reciprocal(stat(f"{tag}_r"), stat(f"{tag}_sd")))
                for t in range(NT):
                    v(V.tensor_scalar(scratch[:, t, :], src[:, t, :], stat(f"{tag}_r")[:, t:t + 1], None, ALU.mult),
                      name if t == NT - 1 else None)

            dve.wait_ge(const_in, 16 * N_CONST)
            ps = full(dve, "prm")
            v(V.tensor_copy(colsA[:, 0:100], ps[:, 0:100]))
            v(V.tensor_copy(colsB[:, :], ps[:, 104:228]))
            v(V.tensor_copy(colsC[:, :], ps[:, 228:276]))
            v(V.tensor_copy(colsD[:, :], ps[0:64, 276:280]), "cols_ready")
            norm_rows("cx", resid, "ctxn_ready")
            C1 = 6.28125
            C2 = 2 * np.pi - C1
            MAGIC = 12582912.0
            for i in range(3):
                x, n = fsmall[:, 2 * i + 1, :], fsmall[:, 6, :]
                ps = full(dve, f"f{i}")
                last(V.tensor_scalar(x, ps[0:64, 0:T], colsD[:, i:i + 1], colsD[:, 3:4], ALU.add, ALU.mult), f"f{i}")
                v(V.tensor_scalar(n, x, 1.0 / (2 * np.pi), MAGIC, ALU.mult, ALU.add))
                v(V.tensor_scalar(n, n, MAGIC, None, ALU.subtract))
                v(V.scalar_tensor_tensor(x, n, -C1, x, ALU.mult, ALU.add))
                v(V.scalar_tensor_tensor(x, n, -C2, x, ALU.mult, ALU.add))
                v(V.tensor_scalar(x, x, 3.1415925, -3.1415925, ALU.min, ALU.max), "sine_arg")
            for q in range(4):
                j = (0, 1, 3, 4)[q]
                ps = full(dve, f"mod{q}")
                last(V.tensor_tensor(mod[:, 8 * j:8 * j + 8, :], ps[:, 0:16].rearrange("p (k j) -> p k j", j=2),
                                     rep_(colsC[:, 8 * j:8 * j + 8], 2, [P, 8, 2]), ALU.add), f"mod{q}")
            for r, (c, j, g) in enumerate(((8, 0, 20), (8, 1, 20), (32, 0, 28))):
                v(V.scalar_tensor_tensor(modsc[:, r, :], mod[:, c:c + 8, j], 1.0, colsA[:, g:g + 8], ALU.add, ALU.mult),
                  "modsc_ready" if r == 2 else None)

            dve.wait_ge(ev("rows_in"), 16 * 7)
            kk = kvt[:, 0:512].rearrange("p (t c) -> p t c", c=T)[:, :, 0:P]
            sqc = scratch[:, 0, 0:256].rearrange("p (t c) -> p t c", t=NT)
            for t in range(NT):
                ps = full(dve, f"ckv{t}")
                v(V.tensor_copy(kvt[:, t * T:t * T + P], ps[:, 0:P]))
                last(V.tensor_copy(vtok[:, 2 + t, :], ps[:, P:2 * P]), f"ckv{t}")
            v(V.tensor_tensor(sqc, kk, kk, ALU.mult))
            v(V.tensor_reduce(stat("ck_ss", 4), scratch[:, 0, 0:256].rearrange("p (a d) -> p a d", d=HD), AX.X, ALU.add), "ck_ss")
            dve.wait_ge(ev("ck_sd"), 1)
            v(V.reciprocal(stat("ck_r", 4), stat("ck_sd", 4)))
            for t in range(NT):
                k3 = kvt[:, t * T:t * T + P].rearrange("p (h d) -> p h d", h=KV)
                v(V.tensor_tensor(k3, k3, rep_(stat("ck_r", 4)[:, 2 * t:2 * t + 2], 2, [P, KV, HD]), ALU.mult))
                v(V.tensor_tensor(k3, k3, rep_(qkg[:, 1, :], 1, [P, KV, HD]), ALU.mult), "ck_ready" if t else None)

            def keys_dup(name, c0, done=None):
                ps = full(dve, name)
                for g in range(KV):
                    for half in range(2):
                        ins = V.tensor_copy(kdup[half * HD:(half + 1) * HD, g, c0:c0 + T], ps[g * HD:(g + 1) * HD, 0:T])
                        if g == KV - 1 and half == 1:
                            last(ins, name)
                        else:
                            v(ins)

            keys_dup("ckT", T)
            v(V.tensor_copy(stat("dummy", 1), epscol[:, 0:1]), "ck_sq_done")
            dve.wait_ge(dec_in, 16)
            dve.wait_ge(ev("tables_in"), 16 * 6)
            for t in range(NT):
                for m in range(4):
                    last(V.tensor_tensor(filt[:, t, m, :], full(dve, f"h{t}{m}"), decay[:, t, m % 2, :], ALU.mult), f"h{t}{m}")
            rn = arena2[:, 3584:4096]
            for o in range(2):
                if o:
                    full(dve, "habs0")
                for t in range(NT):
                    f, g = filt[:, t, 2 * o, :], filt[:, t, 2 * o + 1, :]
                    v(V.scalar_tensor_tensor(absb[:, t, :], f, -1.0, f, ALU.mult, ALU.max))
                    v(V.scalar_tensor_tensor(rn, g, -1.0, g, ALU.mult, ALU.max))
                    v(V.tensor_tensor(absb[:, t, :], absb[:, t, :], rn, ALU.add), "abs_ready")
                for t in range(NT):
                    f, g = filt[:, t, 2 * o, :], filt[:, t, 2 * o + 1, :]
                    v(V.tensor_tensor(rn, f, g, ALU.add))
                    v(V.tensor_tensor(g, f, g, ALU.subtract))
                    v(V.tensor_copy(f, rn), "ed_ready" if t else None)
                last(V.tensor_scalar(rn, full(dve, f"habs{o}"), EPS, None, ALU.add), f"habs{o}")
                v(V.reciprocal(rn, rn))
                for part in range(2):
                    for fr in range(NT):
                        last(V.tensor_tensor(spec[:, o, part, fr, :], full(dve, f"sp{o}{part}{fr}"), rn, ALU.mult), f"sp{o}{part}{fr}")
            v(V.tensor_copy(stat("dummy", 1), epscol[:, 0:1]), "filters_ready")

            norm_rows("xn", resid, "xn_ready")
            v(V.memset(vpad[:, :, 0:30], 0.0))
            for g in range(2):
                emptied(dve, f"wa{g}")
                emptied(dve, f"wg{g}")
            v(V.tensor_tensor(vpad[:, :, 30:30 + T], aT, sgT, ALU.mult))
            n = 0
            for j in range(TAPS):
                for c in range(KC):
                    w = colsB[:, j * KC + c:j * KC + c + 1]
                    if n >= KC:
                        dve.wait_ge(ev("tap"), n - KC + 1)
                    if j == 0:
                        V.tensor_scalar(yT[:, c, :], vpad[:, c, 0:T], w, colsA[:, 8 + c:9 + c], ALU.mult, ALU.add).then_inc(ev("tap"), 1)
                    else:
                        V.scalar_tensor_tensor(yT[:, c, :], vpad[:, c, j:j + T], w, yT[:, c, :], ALU.mult, ALU.add).then_inc(ev("tap"), 1)
                    n += 1
            dve.wait_ge(ev("tap"), n)
            keys_dup("k1", 0)
            v(V.tensor_copy(stat("dummy", 1), epscol[:, 0:1]), "k1_ready")
            for par in range(2):
                emptied(dve, f"s0{par}")
            m, sm, es = stat("p1_m", 16), stat("p1_sm", 16), stat("p1_es", 16)
            for t in range(NT):
                w = P * (t + 1)
                if t:
                    for par in range(2):
                        for pr in range(2):
                            emptied(dve, f"s1{par}{pr}")
                for h in range(HEADS):
                    p = prob1[:, t, h, 0:w]
                    v(V.scalar_tensor_tensor(p, rel[:, 2 * P - w:2 * P], -SLOPES[h], p, ALU.mult, ALU.add))
                mt = m[:, 8 * t:8 * t + 8]
                v(V.tensor_reduce(mt, prob1[:, t, :, 0:w], AX.X, ALU.max))
                v(V.tensor_tensor(mt, mt, sinkrow[:, :], ALU.max))
                v(V.tensor_tensor(sm[:, 8 * t:8 * t + 8], sinkrow[:, :], mt, ALU.subtract))
                v(V.tensor_tensor(prob1[:, t, :, 0:w], prob1[:, t, :, 0:w], rep_(mt, 2, [P, HEADS, w]), ALU.subtract), "p1_shift")
            for t in range(NT):
                w = P * (t + 1)
                mt = m[:, 8 * t:8 * t + 8]
                dve.wait_ge(ev("p1_exp"), t + 1)
                v(V.tensor_reduce(mt, prob1[:, t, :, 0:w], AX.X, ALU.add))
                v(V.tensor_tensor(mt, mt, es[:, 8 * t:8 * t + 8], ALU.add))
                v(V.reciprocal(mt, mt))
                v(V.tensor_tensor(prob1[:, t, :, 0:w], prob1[:, t, :, 0:w], rep_(mt, 2, [P, HEADS, w]), ALU.mult), "p1_ready")
            v(V.tensor_copy(stat("dummy", 1), epscol[:, 0:1]), "conv_ready")
            for t in range(NT):
                v(V.bn_stats(stat("bn", 12)[:, 6 * t:6 * t + 6], full(dve, f"yt{t}")))
                v(V.bn_aggr(stat("mv", 4)[:, 2 * t:2 * t + 2], stat("bn", 12)[:, 6 * t:6 * t + 6]))
                v(V.tensor_copy(stat("ln_v")[:, t:t + 1], stat("mv", 4)[:, 2 * t + 1:2 * t + 2]), "ln_var" if t else None)
            dve.wait_ge(ev("ln_sd"), 1)
            v(V.reciprocal(stat("ln_r"), stat("ln_sd")))
            for t in range(NT):
                last(V.tensor_scalar(ytok[:, t, :], full(dve, f"yt{t}"), stat("mv", 4)[:, 2 * t:2 * t + 1], stat("ln_r")[:, t:t + 1],
                                     ALU.subtract, ALU.mult), f"yt{t}")

            def merge(tag):
                for j in range(8):
                    br, i = j // 4, j % 4
                    emptied(dve, f"{tag}g{br}{i}")
                    ps = full(dve, f"{tag}o{br}{i}")
                    dst = mergedT[:, 2 * i:2 * i + 2, :].rearrange("p c t -> p (c t)")
                    if br == 0:
                        last(V.tensor_tensor(dst, sgate[:, j % 2, :], ps, ALU.mult), f"{tag}o{br}{i}")
                    else:
                        last(V.tensor_tensor(mtmp[:, j % 2, :], sgate[:, j % 2, :], ps, ALU.mult), f"{tag}o{br}{i}")
                        v(V.tensor_tensor(dst, dst, mtmp[:, j % 2, :], ALU.add), f"{tag}merged" if i == 3 else None)

            merge("a")
            for n in range(2):
                for t in range(NT):
                    r = resid[:, t, n * 512:(n + 1) * 512]
                    last(V.tensor_tensor(r, r, full(dve, f"ax{t}{n}"), ALU.add), f"ax{t}{n}")
            v(V.tensor_copy(stat("dummy", 1), epscol[:, 0:1]), "ah_ready")

            norm_rows("rn", resid, "rn_ready")
            lg = rt[:, 72:144].rearrange("p (t e) -> p t e", t=NT)
            ps = full(dve, "route")
            last(V.tensor_tensor(lg, ps[:, 0:128].rearrange("p (t e) -> p t e", t=NT)[:, :, 0:36], rep_(rbias[:, :], 1, [P, NT, 36]), ALU.add), "route")
            g8 = rt[:, 0:16].rearrange("p (t e) -> p t e", t=NT)
            gm = rt[:, 16:32]
            gi = rt[:, 32:48].bitcast(U32)
            gf = stat("gf")
            og = rt[:, 64:72].rearrange("p (t e) -> p t e", t=NT)
            v(V.memset(g8, -3.0e38))
            v(V.tensor_copy(g8[:, :, 0:GROUPS], lg[:, :, 0:GROUPS]))
            for t in range(NT):
                v(V.max(gm[:, 8 * t:8 * t + 8], g8[:, t, :]))
                v(V.max_index(gi[:, 8 * t:8 * t + 8], gm[:, 8 * t:8 * t + 8], g8[:, t, :]))
                v(V.tensor_copy(gf[:, t:t + 1], gi[:, 8 * t:8 * t + 1]))
                v(V.tensor_scalar(og[:, t, :], iota[:, 0:GROUPS], gf[:, t:t + 1], None, ALU.is_equal))
                v(V.tensor_scalar(stat("rt_ng")[:, t:t + 1], gm[:, 8 * t:8 * t + 1], -1.0, None, ALU.mult), "rt_gmax" if t else None)
            em = rt[:, 144:160]
            e8 = rt[:, 160:176].rearrange("p (t e) -> p t e", t=NT)
            ei = rt[:, 176:192].bitcast(U32)
            ef = stat("ef", 4)
            tmp = rt[:, 192:224].rearrange("p (g e) -> p g e", g=GROUPS)
            for t in range(NT):
                el = lg[:, t, GROUPS:].rearrange("p (g e) -> p g e", g=GROUPS)
                v(V.tensor_tensor(tmp, el, rep_(og[:, t, :], 2, [P, GROUPS, PER_GROUP]), ALU.mult))
                v(V.tensor_reduce(e8[:, t, :], rt[:, 192:224].rearrange("p (g e) -> p e g", g=GROUPS), AX.X, ALU.add))
                v(V.max(em[:, 8 * t:8 * t + 8], e8[:, t, :]))
                v(V.max_index(ei[:, 8 * t:8 * t + 8], em[:, 8 * t:8 * t + 8], e8[:, t, :]))
                v(V.tensor_copy(ef[:, 2 * t:2 * t + 2], ei[:, 8 * t:8 * t + 2]))
                v(V.tensor_scalar(stat("rt_nv")[:, t:t + 1], em[:, 8 * t:8 * t + 1], -1.0, None, ALU.mult), "rt_top" if t else None)
            oh = rt[:, 256:384].rearrange("p (j e) -> p j e", j=4)
            asg = arena2[:, 512:576].rearrange("p (t e) -> p t e", t=NT)
            for t in range(NT):
                for k in range(2):
                    j = 2 * t + k
                    v(V.scalar_tensor_tensor(ef[:, j:j + 1], gf[:, t:t + 1], float(PER_GROUP), ef[:, j:j + 1], ALU.mult, ALU.add))
                    v(V.tensor_scalar(oh[:, j, :], iota[:, :], ef[:, j:j + 1], None, ALU.is_equal))
                v(V.tensor_tensor(asg[:, t, :], oh[:, 2 * t, :], oh[:, 2 * t + 1, :], ALU.add), "assign_ready" if t else None)
            dve.wait_ge(ev("rt_gsum"), 2)
            dve.wait_ge(ev("rt_e1"), 2)
            pk = picks[:, :].rearrange("p (t k) -> p t k", k=2)
            wa_, wb_ = stat("wa_"), stat("wb_")
            v(V.tensor_scalar(wa_, stat("rt_e1"), 1.0, None, ALU.add))
            v(V.tensor_tensor(wa_, wa_, stat("rt_gs"), ALU.mult))
            v(V.reciprocal(wb_, wa_))
            v(V.tensor_copy(pk[:, :, 0], wb_))
            v(V.tensor_tensor(pk[:, :, 1], wb_, stat("rt_e1"), ALU.mult))
            posb = rt[:, 384:480]
            last(V.tensor_copy(posb, full(dve, "pos")[:, 0:96]), "pos")
            cnt = posb[:, 64:96]
            sums = rt[:, 640:896].rearrange("p (r n) -> p r n", r=2)
            ext, ext0 = sums[:, 0, 32:64], rt[:, 896:928]
            v(V.memset(rt[:, 640:896], 0.0))
            v(V.tensor_scalar(ext, cnt, float(CAP), None, ALU.is_gt))
            for r in range(2, BLOCKS):
                v(V.scalar_tensor_tensor(ext, cnt, float(CAP * r), ext, ALU.is_gt, ALU.add))
            v(V.tensor_copy(ext0, ext))
            side, d = 0, 1
            while d < EXPERTS:
                v(V.tensor_tensor(sums[:, 1 - side, 32:64], sums[:, side, 32:64], sums[:, side, 32 - d:64 - d], ALU.add))
                side, d = 1 - side, 2 * d
            upto = sums[:, side, 32:64]
            v(V.tensor_tensor(ext0, upto, ext0, ALU.subtract))
            pc, pp, po, pg = stat("pc", 4), stat("pp", 4), stat("po", 4), stat("pg", 4)
            for j in range(4):
                t = j // 2
                for row, dst in ((posb[:, 32 * t:32 * t + 32], pc), (ext0, po)):
                    v(V.tensor_tensor(rt[:, 480:512], oh[:, j, :], row, ALU.mult))
                    v(V.tensor_reduce(dst[:, j:j + 1], rt[:, 480:512], AX.X, ALU.add))
            v(V.tensor_scalar(pp, pc, float(CAP), None, ALU.is_ge))
            for r in range(2, BLOCKS):
                v(V.scalar_tensor_tensor(pp, pc, float(CAP * r), pp, ALU.is_ge, ALU.add))
            v(V.scalar_tensor_tensor(pc, pp, -float(CAP), pc, ALU.mult, ALU.add))
            v(V.tensor_scalar(pg, pp, 1.0, None, ALU.is_ge))
            v(V.scalar_tensor_tensor(po, po, float(EXPERTS - 1), pp, ALU.add, ALU.add))
            v(V.tensor_tensor(po, po, ef, ALU.subtract))
            v(V.tensor_tensor(po, po, pg, ALU.mult))
            v(V.tensor_tensor(po, po, ef, ALU.add))
            v(V.scalar_tensor_tensor(slotf[:, :], po, float(CAP), pc, ALU.mult, ALU.add))
            v(V.tensor_copy(sloti[:, :], slotf[:, :]))
            xe = rt[:, 928:1024]
            big = arena2[:, 1024:1280].rearrange("p (x e) -> p x e", x=EXTRA)
            v(V.tensor_tensor(big, rep_(iota[:, 0:EXTRA], 2, [P, EXTRA, EXPERTS]), rep_(upto, 1, [P, EXTRA, EXPERTS]), ALU.is_ge))
            v(V.tensor_copy(xe[:, 0:EXPERTS], iota[:, :]))
            v(V.tensor_reduce(xe[:, EXPERTS:EXPERTS + EXTRA], big, AX.X, ALU.add))
            v(V.tensor_scalar(xe[:, EXPERTS:EXPERTS + EXTRA], xe[:, EXPERTS:EXPERTS + EXTRA], float(EXPERTS - 1), None, ALU.min))
            v(V.tensor_copy(elist[:, :], xe[0:1, 0:EXPERTS + EXTRA]))
            np_ = stat("np", 1)
            v(V.tensor_scalar(np_, upto[:, EXPERTS - 1:EXPERTS], 0.0, float(STEPS), ALU.is_gt, ALU.add))
            for r in range(2, EXTRA, 2):
                v(V.scalar_tensor_tensor(np_, upto[:, EXPERTS - 1:EXPERTS], float(r), np_, ALU.is_gt, ALU.add))
            v(V.tensor_copy(trips[:, :], np_[0:1, :]), "trips_ready")

            n_iter = dve.value_load(trips[0:1, 0:1], min_val=STEPS, max_val=MAXSTEPS)
            dve.sem_inc(ev("down_read1"), 1)

            def rows_out(h, n):
                dve.wait_ge(ev(f"rowsT_full{h}"), n)
                V.tensor_tensor(xT[:, h, :, :], psum[:, 0, :].rearrange("p (k c) -> p k c", k=KD),
                                rep_(colsA[:, 36:44], 2, [P, KD, CAP]), ALU.mult).then_inc(ev(f"rowsT_ready{h}"), 1)

            rows_out(0, 1)
            with dve.Fori(0, n_iter) as i:
                rows_out(1, i + 2)
                for h in range(2):
                    dve.wait_ge(ev(f"silu_ready{h}"), i + 1)
                    dve.wait_ge(ev(f"up_full{h}"), i + 1)
                    V.tensor_tensor(hrow[:, h, :], silu[:, h, :], psum[0:CAP, 3 + 2 * h, :], ALU.mult).then_inc(ev(f"hid_ready{h}"), 1)
                for h in range(2):
                    dve.wait_ge(ev("down_full1"), 2 * i + h + 2)
                    dve.wait_ge(ev(f"stored{h}"), 16 * i + 1)
                    V.tensor_copy(yrow[:, h, 512:1024], psum[0:CAP, 7, :]).then_inc(ev("down_read1"), 1)
                    if h == 0:
                        rows_out(0, i + 2)

            dve.wait_ge(ev("fetched"), 64)
            for j in range(4):
                r = resid[:, j // 2, :]
                v(V.scalar_tensor_tensor(r, back[:, j, :], picks[:, j:j + 1], r, ALU.mult, ALU.add), "moe_added" if j == 3 else None)
            norm_rows("fn", resid, None)
            dve.wait_ge(ev("gf_in"), 16)
            for t in range(NT):
                v(V.tensor_tensor(resid[:, t, :], scratch[:, t, :], gfrow, ALU.mult), "x2_ready" if t else None)

            norm_rows("zn", resid, "zn_ready")
            v(V.memset(hpad[:, :, :, 0:1], 0.0))
            v(V.memset(hpad[:, :, :, T + 1:T + 2], 0.0), "pads_zero")
            for t in range(NT):
                ps = full(dve, f"kv{t}")
                v(V.tensor_copy(ktok[:, t, :], ps[:, 0:P]))
                last(V.tensor_copy(vtok[:, t, :], ps[:, P:2 * P]), f"kv{t}")
            for t in range(NT):
                emptied(dve, f"q{t}")
            ss = stat("qk_ss", 20)
            v(V.tensor_tensor(sq, qtok, qtok, ALU.mult))
            v(V.tensor_reduce(ss[:, 0:16], arena2[:, 1280:2304].rearrange("p (a d) -> p a d", d=HD), AX.X, ALU.add))
            v(V.tensor_tensor(arena2[:, 1280:1536], arena2[:, 1024:1280], arena2[:, 1024:1280], ALU.mult))
            v(V.tensor_reduce(ss[:, 16:20], arena2[:, 1280:1536].rearrange("p (a d) -> p a d", d=HD), AX.X, ALU.add), "qk_ss")
            dve.wait_ge(ev("qk_sd"), 1)
            v(V.reciprocal(stat("qk_r", 20), stat("qk_sd", 20)))
            for rows_, heads, r0, gi_ in ((qtok, HEADS, 0, 0), (ktok, KV, 16, 1)):
                for t in range(NT):
                    x3 = rows_[:, t, :].rearrange("p (h d) -> p h d", h=heads)
                    v(V.tensor_tensor(x3, x3, rep_(stat("qk_r", 20)[:, r0 + heads * t:r0 + heads * (t + 1)], 2, [P, heads, HD]), ALU.mult))
                    v(V.tensor_tensor(x3, x3, rep_(qkg[:, gi_, :], 1, [P, heads, HD]), ALU.mult))
                    x5 = rows_[:, t, :].rearrange("p (h a s j) -> p h a s j", a=2, s=2, j=16)
                    r5 = rtmp[:, t, 0:heads * HD].rearrange("p (h a s j) -> p h a s j", a=2, s=2, j=16)
                    s4 = rope[:, 1, t, :].rearrange("p (a s j) -> p a s j", a=2, s=2)
                    for half in range(2):
                        v(V.tensor_tensor(r5[:, :, :, half, :], x5[:, :, :, 1 - half, :],
                                          rep_(s4[:, :, half, :], 1, [P, heads, 2, 16]), ALU.mult))
                    v(V.tensor_tensor(x3, x3, rep_(rope[:, 0, t, :], 1, [P, heads, HD]), ALU.mult))
                    x2 = rows_[:, t, :]
                    fin = rows_ is ktok and t == NT - 1
                    v(V.tensor_tensor(x2, x2, rtmp[:, t, 0:heads * HD], ALU.add), "qk2_ready" if fin else None)
            for j in range(6):
                emptied(dve, f"hy{j // 2}{j % 2}")
                for c in range(2):
                    k = 2 * j + c
                    x = hpad[:, j % 2, c, :]
                    v(V.tensor_scalar(zs[:, k, :], x[:, 0:T], colsA[:, 44 + k:45 + k], colsA[:, 80 + k:81 + k], ALU.mult, ALU.add))
                    v(V.scalar_tensor_tensor(zs[:, k, :], x[:, 1:T + 1], colsA[:, 56 + k:57 + k], zs[:, k, :], ALU.mult, ALU.add))
                    v(V.scalar_tensor_tensor(zs[:, k, :], x[:, 2:T + 2], colsA[:, 68 + k:69 + k], zs[:, k, :], ALU.mult, ALU.add),
                      "short_done" if c else None)
            v(V.tensor_copy(stat("dummy", 1), epscol[:, 0:1]), "short_ready")
            keys_dup("kT", 0)
            v(V.tensor_copy(stat("dummy", 1), epscol[:, 0:1]), "k2_ready")

            def unit_max(u):
                v(V.tensor_reduce(stat("m2", 16)[:, u:u + 1], full(dve, f"sc{u}"), AX.X, ALU.max))
                v(V.tensor_scalar(stat("nm2", 16)[:, u:u + 1], stat("m2", 16)[:, u:u + 1], -HD ** -0.5, None, ALU.mult), "nmax")

            unit_max(0)
            for u in range(16):
                if u + 1 < 16:
                    unit_max(u + 1)
                emptied(dve, f"sc{u}")
                v(V.reciprocal(stat("m2", 16)[:, u:u + 1], stat("sum2", 16)[:, u:u + 1]))
                v(V.tensor_scalar(prob2[:, u % 8, :], prob2[:, u % 8, :], stat("m2", 16)[:, u:u + 1], None, ALU.mult), "p2_ready")
            half_ = lambda ap: ap.rearrange("p k c -> p (k c)")
            for o in range(2):
                for part in range(2):
                    for f in range(NT):
                        emptied(dve, f"U{o}{part}{f}")
                Uc, Us = half_(Usb[:, 0:2, :]), half_(Usb[:, 2:4, :])
                Kc, Ks = half_(spec[:, o, 0, :, :]), half_(spec[:, o, 1, :, :])
                v(V.tensor_tensor(prod[:, 0, :], Uc, Kc, ALU.mult))
                v(V.tensor_tensor(prod[:, 1, :], Us, Ks, ALU.mult))
                v(V.tensor_tensor(half_(Y[:, 0:2, :]), prod[:, 0, :], prod[:, 1, :], ALU.subtract))
                v(V.tensor_tensor(prod[:, 0, :], Uc, Ks, ALU.mult))
                v(V.tensor_tensor(prod[:, 1, :], Us, Kc, ALU.mult))
                v(V.tensor_tensor(half_(Y[:, 2:4, :]), prod[:, 0, :], prod[:, 1, :], ALU.add), "Y_ready")
                src = (zs[:, 0:4, :], y1T)[o]
                gate = (zs[:, 4:8, :], zs[:, 8:12, :])[o]
                for g in range(2):
                    ps = full(dve, f"I{o}{g}")
                    for c in range(2):
                        k = 2 * g + c
                        ins = V.scalar_tensor_tensor(prod[:, 0, k * T:(k + 1) * T], src[:, k, :], colsA[:, 92 + 4 * o + k:93 + 4 * o + k],
                                                     ps[:, c * T:(c + 1) * T], ALU.mult, ALU.add)
                        if c:
                            last(ins, f"I{o}{g}")
                        else:
                            v(ins)
                v(V.tensor_tensor(gate.rearrange("p c t -> p (c t)"), gate.rearrange("p c t -> p (c t)"), prod[:, 0, :], ALU.mult),
                  ("y1_ready", "hy_ready")[o])
            merge("b")
            dve.wait_ge(ev("g1_in"), 16)
            for j in range(2):
                r = g1row[:, j * 512:(j + 1) * 512]
                last(V.tensor_tensor(r, r, full(dve, f"G1{j}"), ALU.add), f"G1{j}")
            for n in range(2):
                for t in range(NT):
                    r = resid[:, t, n * 512:(n + 1) * 512]
                    last(V.tensor_tensor(scratch[:, t, 0:512], g1row[:, n * 512:(n + 1) * 512], full(dve, f"bx{t}{n}"), ALU.mult), f"bx{t}{n}")
                    v(V.tensor_tensor(r, r, scratch[:, t, 0:512], ALU.add), "bh_ready" if n and t else None)
            norm_rows("pn", resid, "pn_ready")
            dve.wait_ge(ev("g2_in"), 32)
            def top16(vals, idx, src):
                for r in range(2):
                    a, b = vals[:, 8 * r:8 * r + 8], idx[:, 8 * r:8 * r + 8]
                    v(V.max(a, src))
                    v(V.max_index(b, a, src))
                    if r == 0:
                        v(V.match_replace(src, a, src, -3.0e38))

            for t in range(NT):
                for g in range(4):
                    emptied(dve, f"ks{t}{g}")
                for c in range(2 * PH):
                    top16(top_v[:, t, c, :], top_i[:, t, c, :], S[:, t, c, :])
                v(V.tensor_copy(top_f[:, t, :, :], top_i[:, t, :, :]))
                for h in range(PH):
                    c3 = cand[:, h * 256:(h + 1) * 256].rearrange("p (a b) -> p a b", a=PTOP)
                    v(V.tensor_tensor(c3, rep_(top_v[:, t, 2 * h, :], 2, [P, PTOP, PTOP]), rep_(top_v[:, t, 2 * h + 1, :], 1, [P, PTOP, PTOP]), ALU.add))
                    top16(best[:, t, h, :], where[:, t, h * PTOP:(h + 1) * PTOP], cand[:, h * 256:(h + 1) * 256])
                g3 = gates[:, t, :].rearrange("p (h k) -> p h k", k=PTOP)
                v(V.tensor_tensor(g3, best[:, t, :, :], best[:, t, :, 0:1].to_broadcast([P, PH, PTOP]), ALU.subtract), "best_shift")
                dve.wait_ge(ev("best_exp"), t + 1)
                v(V.tensor_reduce(stat("gsum", 8), g3, AX.X, ALU.add))
                v(V.reciprocal(stat("gsum", 8), stat("gsum", 8)))
                v(V.tensor_tensor(g3, g3, rep_(stat("gsum", 8), 2, [P, PH, PTOP]), ALU.mult))
                oh4 = cand.rearrange("p (h k a) -> p h k a", h=PH, k=PTOP)
                for half, (op, arg) in enumerate(((ALU.logical_shift_right, 4), (ALU.bitwise_and, 15))):
                    v(V.tensor_scalar(wi[:, t, :], where[:, t, :], arg, None, op))
                    v(V.tensor_copy(wf[:, t, :], wi[:, t, :]))
                    v(V.tensor_tensor(cand.rearrange("p (n a) -> p n a", a=PTOP), rep_(wf[:, t, :], 2, [P, PICKS, PTOP]),
                                      rep_(iota[:, 0:PTOP], 1, [P, PICKS, PTOP]), ALU.is_equal))
                    tf = top_f[:, t, :, :].rearrange("p (h s) k -> p h s k", s=2)[:, :, half, :]
                    v(V.tensor_tensor(oh4, oh4, rep_(tf, 2, [P, PH, PTOP, PTOP]), ALU.mult))
                    dst = rowf[:, t, :] if half == 0 else wf[:, t, :]
                    v(V.tensor_reduce(dst, cand.rearrange("p (n a) -> p n a", a=PTOP), AX.X, ALU.add))
                v(V.scalar_tensor_tensor(rowf[:, t, :], rowf[:, t, :], float(PKEYS), wf[:, t, :], ALU.mult, ALU.add))
                v(V.tensor_copy(rowid[:, t, :], rowf[:, t, :]), "rowid_ready")
            for j in range(2):
                r = g2row[:, j * 512:(j + 1) * 512]
                last(V.tensor_tensor(r, r, full(dve, f"G2{j}"), ALU.add), f"G2{j}")
            for t in range(NT):
                for n in range(2):
                    emptied(dve, f"xp{t}{n}")

            dve.sem_inc(ev("row_used"), ROWBUFS)
            per = PICKS // ROWBUFS
            for t in range(NT):
                with dve.Fori(0, per) as i:
                    for b in range(ROWBUFS):
                        dve.wait_ge(ev(f"row_in{b}"), (i + (t * per + 1)) * 16)
                        V.tensor_tensor_reduce(dotjunk, rows[:, b, :], tok2[:, t, :], 1.0, 0.0, ALU.mult, ALU.add,
                                               dot8[:, b:b + 1]).then_inc(ev("row_used"), 1)
                        dve.wait_ge(ev("row_used"), (i + t * per) * ROWBUFS + (ROWBUFS + b + 1))
                    V.tensor_copy(dots[:, t, bass.ds(i * ROWBUFS, ROWBUFS)], dot8[:, :]).then_inc(ev("dots_kept"), 1)
                    dve.wait_ge(ev("dots_kept"), i + (t * per + 1))
                v(V.tensor_copy(stat("dummy", 1), epscol[:, 0:1]), "dots_ready")
            for t in range(NT):
                dve.wait_ge(ev("gelu_done"), t + 1)
                v(V.tensor_tensor(gates[:, t, :], gates[:, t, :], dots[:, t, :], ALU.mult))
                v(V.memset(scratch[:, t, :], 0.0))
            for t in range(NT):
                with dve.Fori(0, per) as i:
                    for b in range(ROWBUFS):
                        dve.wait_ge(ev(f"row_in{b}"), (i + ((NT + t) * per + 1)) * 16)
                        V.scalar_tensor_tensor(scratch[:, t, :], rows[:, b, :], gates[:, t, bass.ds(i * ROWBUFS + b, 1)], scratch[:, t, :],
                                               ALU.mult, ALU.add).then_inc(ev("row_used"), 1)
                        dve.wait_ge(ev("row_used"), (i + (NT + t) * per) * ROWBUFS + (ROWBUFS + b + 1))
                v(V.tensor_tensor(scratch[:, t, :], scratch[:, t, :], g2row, ALU.mult))
                v(V.tensor_tensor(resid[:, t, :], resid[:, t, :], scratch[:, t, :], ALU.add), "x3_ready")
            for t in range(NT):
                dve.wait_ge(ev("ff_sd"), t + 1)
                v(V.reciprocal(stat("ff_r")[:, t:t + 1], stat("ff_sd")[:, t:t + 1]))
                v(V.tensor_scalar(resid[:, t, :], resid[:, t, :], stat("ff_r")[:, t:t + 1], None, ALU.mult))
                v(V.tensor_tensor(resid[:, t, :], resid[:, t, :], flrow, ALU.mult), "final_ready")


_INS = ['x', 'g_mix', 'w_in', 'w_dw', 'b_dw', 'ln_conv_g', 'ln_conv_b', 'sinks', 'w_conv_out', 'w_attn_out', 'w_out', 'g_ffn',
        'w_group', 'b_group', 'w_expert', 'b_expert', 'w_gate', 'w_up', 'w_down', 'g_final', 'c_2', 'ctx_2', 'c_ctx_2',
        'ada_w_2', 'ada_b_2', 'norm_mix_g_2', 'norm_ffn_g_2', 'w_in_2', 'q_norm_g_2', 'k_norm_g_2', 'hy_conv_w_2',
        'hy_conv_b_2', 'hf_w1_2', 'hf_b1_2', 'hf_w2_2', 'hf_b2_2', 'hf_w3_2', 'hf_b3_2', 'hf_w4_2', 'hf_freq_2', 'hy_skip_2',
        'w_attn_out_2', 'w_hy_out_2', 'w_out_2', 'peer_wq_2', 'peer_keys1_2', 'peer_keys2_2', 'peer_u_2', 'peer_v_2',
        'final_norm_g_2']


def kernel(**inputs):
    import numpy as _np
    import concourse.bacc as _bacc
    from concourse import mybir as _mybir
    from concourse.bass_utils import run_bass_kernel_spmd as _run

    nc = _bacc.Bacc("TRN2", target_bir_lowering=False, num_devices=1)
    arrays, aps = {}, {}
    named = {n: _np.ascontiguousarray(inputs[n]) for n in _INS}
    named.update(shape_constants())
    for name, a in named.items():
        arrays[f"in_{name}_dram"] = a
        aps[name] = nc.dram_tensor(f"in_{name}_dram", a.shape, _mybir.dt.from_np(a.dtype), kind="ExternalInput").ap()
    out = nc.dram_tensor("out_0_dram", (1, T, D), F32, kind="ExternalOutput").ap()
    build(nc, aps, out)
    r = _run(nc, [arrays], core_ids=[0])
    return r.results[0]["out_0_dram"]
```

```python
from contextlib import ExitStack

import numpy as np
import concourse.bass as bass
from concourse import mybir

P = 128
F32 = mybir.dt.float32
I32 = mybir.dt.int32
U32 = mybir.dt.uint32
ALU = mybir.AluOpType
ACT = mybir.ActivationFunctionType
AX = mybir.AxisListType

T = 256
NT = T // P
D = 1024
KD = D // P
CH = 512
KC = CH // P
TAPS = 31
HEADS, KV, HD = 8, 2, 64
EXPERTS, GROUPS, PER_GROUP = 32, 4, 8
FF = 512
CAP = 64
BLOCKS = T // CAP
EXTRA = 2 * T // CAP
SLOTS = 6
PIECE = 4096
STEPS = EXPERTS // 2
MAXSTEPS = (EXPERTS + EXTRA) // 2
ROWS = (EXPERTS + EXTRA) * CAP
PH, PKEYS, PTOP = 8, 128, 16
PICKS = PH * PTOP
ROWBUFS = 16
EPS = 1e-6
SLOPES = [2.0 ** (-8.0 * (h + 1) / HEADS) for h in range(HEADS)]
MASKED = 1.0e30


def shape_constants():
    c = {}
    c["c_ident"] = np.eye(P, dtype=np.float32)
    c["c_before"] = np.triu(np.ones((P, P), np.float32), 1)
    q = np.arange(P)[:, None]
    k = np.arange(2 * P)[None, :]
    rel = P + q - k
    c["c_rel"] = np.where((rel >= 0) & (rel < P), rel, MASKED).astype(np.float32)
    t = np.arange(T, dtype=np.float64)
    theta = 2 * np.pi * (t + 0.5) / (2 * T)
    ang = t[:, None] * theta[None, :]
    cs = np.stack([np.cos(ang), np.sin(ang)])
    c["c_dft"] = cs.reshape(2, NT, P, T).transpose(2, 0, 1, 3).astype(np.float32).copy()
    inv = (np.stack([np.cos(ang).T, np.sin(ang).T]) / T)
    c["c_idft"] = inv.reshape(2 * NT, P, T).transpose(1, 0, 2).astype(np.float32).copy()
    row, col = np.arange(T) // 64, np.arange(T) % 64
    f = (10000.0 ** (-np.arange(0, 32, 2) / 32)).astype(np.float32)
    ar, ac = row[:, None].astype(np.float32) * f, col[:, None].astype(np.float32) * f
    a = np.concatenate([ar, ar, ac, ac], -1)
    sign = np.tile(np.concatenate([-np.ones(16), np.ones(16)]), 2)
    c["c_rope"] = np.stack([np.cos(a), np.sin(a) * sign]).reshape(2, NT, P, HD).transpose(2, 0, 1, 3).astype(np.float32).copy()
    t01 = np.linspace(0.0, 1.0, T, dtype=np.float32)[:, None]
    w = (2.0 * np.pi * np.arange(T, dtype=np.float32)[:, None] / T).astype(np.float32)
    fr = np.linspace(1e-4, 15, 16, dtype=np.float32)[None]
    z = np.concatenate([t01, np.cos(fr * w), -np.sin(fr * w)], -1)
    c["c_feat"] = z.T.astype(np.float32).copy()
    deltas = np.abs(np.linspace(np.log(1e-2) / 1.5, np.log(1e-2) / 0.3, CH, dtype=np.float32))
    decay = np.exp(-t01 * deltas)
    back = decay.copy()
    back[0] = 0.0
    c["c_decay"] = np.stack([decay, back]).reshape(2, NT, P, CH).transpose(2, 1, 0, 3).astype(np.float32).copy()
    c["c_iota"] = np.tile(np.arange(EXPERTS, dtype=np.float32), (P, 1))
    return c


def build(nc, A, out):
    ctx = ExitStack()
    with ctx:
        def sb(name, shape, dt=F32):
            return ctx.enter_context(nc.sbuf_tensor(name, shape, dt))

        def sem(name):
            return ctx.enter_context(nc.semaphore(name))

        psum = ctx.enter_context(nc.psum_tensor("psum", [P, 8, 512], F32))
        ring = sb("ring", [P, SLOTS, PIECE])
        resid = sb("resid", [P, NT, D])
        scratch = sb("scratch", [P, NT, D])
        tok2 = sb("tok2", [P, NT, D])
        actT = sb("actT", [P, KD, T])
        spec = sb("spec", [P, 2, 2, NT, CH])
        dft = sb("dft", [P, 2, NT, T])
        idft = sb("idft", [P, 2 * NT, T])
        arena1 = sb("arena1", [P, 4224])
        arena2 = sb("arena2", [P, 4096])
        qT = sb("qT", [P, KC, T])
        kdup = sb("kdup", [P, KV, 2 * T])
        vtok = sb("vtok", [P, 2 * NT, KV * HD])
        attnT = sb("attnT", [P, KC, T])
        ident = sb("ident", [P, P])
        ones = sb("ones", [P, P])
        before = sb("before", [P, P])
        rel = sb("rel", [P, 2 * P])
        rope = sb("rope", [P, 2, NT, HD])
        iota = sb("iota", [P, EXPERTS])
        colsA = sb("colsA", [P, 104])
        colsB = sb("colsB", [P, 124])
        colsC = sb("colsC", [P, 48])
        colsD = sb("colsD", [64, 4])
        mod = sb("mod", [P, 6 * KD, 2])
        modsc = sb("modsc", [P, 3, KD])
        scT = sb("scT", [P, KD, 2])
        rbias = sb("rbias", [P, GROUPS + EXPERTS])
        sinkrow = sb("sinkrow", [P, HEADS])
        qkg = sb("qkg", [P, 2, HD])
        wroute = sb("wroute", [P, KD, GROUPS + EXPERTS])
        st = sb("st", [P, 400])
        epscol = sb("epscol", [P, 1])
        picks = sb("picks", [P, 4])
        slotf = sb("slotf", [P, 4])
        sloti = sb("sloti", [P, 4], I32)
        trips = sb("trips", [1, 1], I32)
        elist = sb("elist", [1, EXPERTS + EXTRA], I32)

        aT = arena1[:, 0:1024].rearrange("p (c t) -> p c t", c=KC)
        sgT = arena1[:, 1024:2048].rearrange("p (c t) -> p c t", c=KC)
        vpad = arena1[:, 2048:2048 + KC * (T + 30)].rearrange("p (c t) -> p c t", c=KC)
        yT = arena1[:, 3200:4224].rearrange("p (c t) -> p c t", c=KC)
        ytok = arena1[:, 0:1024].rearrange("p (a c) -> p a c", a=NT)
        yactT = arena1[:, 1024:2048].rearrange("p (c t) -> p c t", c=KC)
        prob1 = arena2[:, :].rearrange("p (t h k) -> p t h k", t=NT, h=HEADS)
        pTbuf = scratch[:, :, :].rearrange("p a (s c) -> p (a s) c", c=512)
        sgate = {"a": arena1[:, 3200:4224].rearrange("p (b c) -> p b c", b=2), "b": arena2[:, 0:1024].rearrange("p (b c) -> p b c", b=2)}
        mtmp = {"a": arena1[:, 0:1024].rearrange("p (b c) -> p b c", b=2), "b": arena2[:, 1024:2048].rearrange("p (b c) -> p b c", b=2)}
        normjunk = arena1[:, 0:2 * D].rearrange("p (a d) -> p a d", d=D)
        qjunk = qT[:, :, :].rearrange("p c t -> p (c t)").unsqueeze(1).to_broadcast([P, NT, D])
        mergedT = tok2[:, :, :].rearrange("p a (c t) -> p (a c) t", t=T)
        filt = spec[:, :, :, :, :].rearrange("p o m a c -> p a (o m) c")
        decay = tok2[:, :, :].rearrange("p a (m c) -> p a m c", m=2)
        fsmall = arena2[0:64, 0:2048].rearrange("p (a t) -> p a t", t=T)
        feat = arena2[0:33, 2048:2304]
        w1s = arena2[0:33, 2304:2368]
        w23 = arena2[0:64, 2368:2496].rearrange("p (a n) -> p a n", a=2)
        absb = arena2[:, 2560:3584].rearrange("p (a c) -> p a c", a=2)
        ctxr = arena2[:, 2048:4096].rearrange("p (a d) -> p a d", d=D)
        mrow = tok2[0:2, :, :].rearrange("p a (b n) -> p (a b) n", n=512)
        kvt = qT[:, :, :].rearrange("p c t -> p (c t)")

        kflat = kdup[:, :, :].rearrange("p a t -> p (a t)")
        prm = kflat[:, 0:384].rearrange("p (a t) -> p a t", t=P)
        prmD = kflat[0:4, 384:448]
        crow = kflat[0:16, 512:640]
        zeros = kdup[:, 0, T:2 * T]
        rt = arena2[:, 0:1024]
        xrow = scratch[0:CAP, :, :]
        yrow = tok2[0:CAP, :, :]
        xT = arena1[:, 0:1024].rearrange("p (h k c) -> p h k c", h=2, k=KD)
        hidT = arena1[:, 1024:1536].rearrange("p (h k c) -> p h k c", h=2, k=4)
        silu = arena1[0:CAP, 1536:2560].rearrange("p (h c) -> p h c", h=2)
        hrow = arena1[0:CAP, 2560:3584].rearrange("p (h c) -> p h c", h=2)
        back = arena2[:, :].rearrange("p (a d) -> p a d", d=D)
        zs = arena1[:, 0:3072].rearrange("p (c t) -> p c t", t=T)
        y1T, hyoT = zs[:, 4:8, :], zs[:, 8:12, :]
        hpad = arena1[:, 3072:3072 + 4 * (T + 2)].rearrange("p (b c t) -> p b c t", b=2, c=2)
        qtok = arena2[:, 0:1024].rearrange("p (a c) -> p a c", a=NT)
        ktok = arena2[:, 1024:1280].rearrange("p (a c) -> p a c", a=NT)
        sq = arena2[:, 1280:2304].rearrange("p (a c) -> p a c", a=NT)
        rtmp = arena2[:, 2304:3328].rearrange("p (a c) -> p a c", a=NT)
        prob2 = arena2[:, 2048:4096].rearrange("p (u c) -> p u c", c=512)
        pT2 = scratch[:, 0, :].rearrange("p (u c) -> p u c", c=512)
        vtime = arena2[:, 0:1024].rearrange("p (a c) -> p a c", a=NT)
        Usb = ring[:, 3, 0:2048].rearrange("p (k c) -> p k c", c=CH)
        Y = ring[:, 3, 2048:4096].rearrange("p (k c) -> p k c", c=CH)
        prod = scratch[:, 1, :]
        g1row = kflat
        grow = tok2[0:1, :, :].rearrange("p a (b n) -> p (a b) n", n=512)
        gbias = actT[0:1, :, :].rearrange("p (a k) t -> p a (k t)", a=4)
        gfrow = attnT[:, :, :].rearrange("p c t -> p (c t)")
        pqT = arena2[:, :].rearrange("p (c t) -> p c t", t=T)
        keysT = spec[:, 0, :, :, :].rearrange("p a b c -> p (a b c)").rearrange("p (c n) -> p c n", n=P)
        cand = spec[:, 1, :, :, :].rearrange("p a b c -> p (a b c)")
        S = arena1[:, 0:4096].rearrange("p (t c n) -> p t c n", t=NT, n=P)
        qflat = qT[:, :, :].rearrange("p c t -> p (c t)")
        vflat = vtok[:, :, :].rearrange("p c t -> p (c t)")
        aflat = attnT[:, :, :].rearrange("p c t -> p (c t)")
        top_v = qflat[:, 0:512].rearrange("p (t c k) -> p t c k", t=NT, k=PTOP)
        top_i = qflat[:, 512:1024].bitcast(U32).rearrange("p (t c k) -> p t c k", t=NT, k=PTOP)
        top_f = kflat[:, 0:512].rearrange("p (t c k) -> p t c k", t=NT, k=PTOP)
        best = kflat[:, 512:768].rearrange("p (t h k) -> p t h k", t=NT, k=PTOP)
        where = kflat[:, 768:1024].bitcast(U32).rearrange("p (t n) -> p t n", t=NT)
        wi = vflat[:, 0:256].bitcast(U32).rearrange("p (t n) -> p t n", t=NT)
        wf = vflat[:, 256:512].rearrange("p (t n) -> p t n", t=NT)
        dots = aflat[:, 0:256].rearrange("p (t n) -> p t n", t=NT)
        gates = aflat[:, 256:512].rearrange("p (t n) -> p t n", t=NT)
        rowid = aflat[:, 512:768].bitcast(I32).rearrange("p (t n) -> p t n", t=NT)
        rowf = aflat[:, 768:1024].rearrange("p (t n) -> p t n", t=NT)
        rows = ring[:, 0:4, :].rearrange("p s (b d) -> p (s b) d", d=D)
        g2row, flrow = ring[:, 5, 0:D], ring[:, 5, D:2 * D]
        dotjunk = actT[:, :, :].rearrange("p (a c) t -> p a (c t)", a=2)
        cur = sb("cur", [P, ROWBUFS], I32)
        dotcols = sb("dotcols", [P, ROWBUFS])

        gate_rows = nc.dram_tensor("gate_rows", (1, 2 * D), F32, kind="Internal").ap()
        xs = nc.dram_tensor("moe_rows_in", (ROWS + P, D), F32, kind="Internal").ap()
        ys = nc.dram_tensor("moe_rows_out", (ROWS, D), F32, kind="Internal").ap()

        bank_full = [sem(f"bank_full{b}") for b in range(8)]
        bank_read = [sem(f"bank_read{b}") for b in range(8)]
        piece_in = [sem(f"piece_in{s}") for s in range(SLOTS)]
        piece2_in = [sem(f"piece2_in{s}") for s in range(SLOTS)]
        prm_in = sem("prm_in")
        const_in = sem("const_in")
        ctx_in = sem("ctx_in")
        grow_in = sem("grow_in")
        dec_in = sem("dec_in")
        act_step = sem("act_step")
        dve_step = sem("dve_step")
        pool_step = sem("pool_step")
        pe_step = sem("pe_step")
        events = {}

        def ev(name):
            if name not in events:
                events[name] = sem(name)
            return events[name]

        def kpiece(w, c0, n=512):
            return w[:, c0:c0 + n].rearrange("(k p) n -> p k n", p=P)

        w_in, w_in2, ada = A["w_in"][0], A["w_in_2"][0], A["ada_w_2"][0]
        pieces = [("wa", kpiece(w_in, 0)), ("wg", kpiece(w_in, CH)), ("filt4", A["hf_w4_2"][0]),
                  ("wq", kpiece(w_in, 2 * CH)), ("wkv", kpiece(w_in, 3 * CH, 2 * KV * HD))]
        mod_pieces = (0, 1, 2, 3, 6, 7, 8, 9)
        for j in mod_pieces:
            pieces.append((f"ada{j}", kpiece(ada, 512 * j)))
        g0 = 3 * CH + 2 * KV * HD
        pieces += [("o0", A["w_conv_out"][0].rearrange("(k p) n -> p k n", p=P)),
                   ("g00", kpiece(w_in, g0)), ("g01", kpiece(w_in, g0 + 512)),
                   ("o1", A["w_attn_out"][0].rearrange("(k p) n -> p k n", p=P)),
                   ("g10", kpiece(w_in, g0 + D)), ("g11", kpiece(w_in, g0 + D + 512)),
                   ("wo0", kpiece(A["w_out"][0], 0)), ("wo1", kpiece(A["w_out"][0], 512)),
                   ("ctxkv", kpiece(w_in2, CH, 2 * KV * HD))]
        place1 = {n: (i % SLOTS, i // SLOTS + 1) for i, (n, _) in enumerate(pieces)}
        base_use = [len([1 for i in range(len(pieces)) if i % SLOTS == s]) for s in range(SLOTS)]
        h0 = CH + 2 * KV * HD
        g2 = h0 + 3 * CH
        pieces2 = [("m4", kpiece(ada, 2048)), ("m5", kpiece(ada, 2560)),
                   ("m10", kpiece(ada, 5120)), ("m11", kpiece(ada, 5632)),
                   ("q", kpiece(w_in2, 0)), ("kv", kpiece(w_in2, CH, 2 * KV * HD)),
                   ("hy0", kpiece(w_in2, h0)), ("hy1", kpiece(w_in2, h0 + CH)), ("hy2", kpiece(w_in2, h0 + 2 * CH)),
                   ("room", None),
                   ("o0", A["w_attn_out_2"][0].rearrange("(k p) n -> p k n", p=P)),
                   ("g00", kpiece(w_in2, g2)), ("g01", kpiece(w_in2, g2 + 512)),
                   ("o1", A["w_hy_out_2"][0].rearrange("(k p) n -> p k n", p=P)),
                   ("g10", kpiece(w_in2, g2 + D)), ("g11", kpiece(w_in2, g2 + D + 512)),
                   ("wo0", kpiece(A["w_out_2"][0], 0)), ("wo1", kpiece(A["w_out_2"][0], 512)),
                   ("keys", None),
                   ("pq0", kpiece(A["peer_wq_2"][0], 0)), ("pq1", kpiece(A["peer_wq_2"][0], 512)),
                   ("pq2", kpiece(A["peer_wq_2"][0], 1024)), ("pq3", kpiece(A["peer_wq_2"][0], 1536))]
        room = [n for n, _ in pieces2].index("room") % SLOTS
        place2 = {n: (i % SLOTS, i // SLOTS + 1 - (i % SLOTS == room and i >= SLOTS)) for i, (n, _) in enumerate(pieces2)}

        def view(slot, src):
            k, n = src.shape[1], src.shape[2]
            return ring[:, slot, 0:k * n].rearrange("p (k n) -> p k n", k=k)

        def pview(places, name, n=512):
            s = places[name][0]
            k = PIECE // n if n != 256 else KD
            return ring[:, s, 0:k * n].rearrange("p (k n) -> p k n", k=k)

        A_cols = dict(g_mix=0, b_dw=8, ln_g=12, ln_b=16, mixg=20, ffng2=28, g_ffn=36, hyw=44, hyb=80, skip=92)

        N_CONST, N_PRM = 3, 18
        ZEROED = ROWS // P + 1 + EXTRA * CAP // P
        stat_cols = {}

        def stat(name, n=NT):
            if name not in stat_cols:
                a = sum(w for _, w in stat_cols.values())
                assert a + n <= 400
                stat_cols[name] = (a, n)
            a, w = stat_cols[name]
            assert w == n
            return st[:, a:a + n]

        def rep_(ap, axis, shape):
            return ap.unsqueeze(axis).to_broadcast(shape)

        groups = {}

        def full(eng, name):
            b, n = groups[name]
            eng.wait_ge(bank_full[b], n)
            return psum[:, b, :]

        def emptied(eng, name):
            b, n = groups[name]
            eng.wait_ge(bank_read[b], n)

        block = ctx.enter_context(nc.Block())

        @block.tensor
        def _(pe):
            fills = [0] * 8
            turns = {}
            everyday = [tuple(range(7))]

            def bank(name, among=None):
                among = among or everyday[-1]
                turns[among] = turns.get(among, 0) + 1
                b = among[turns[among] % len(among)]
                if fills[b]:
                    pe.wait_ge(bank_read[b], fills[b])
                fills[b] += 1
                groups[name] = (b, fills[b])
                return b

            def mm(o, lhsT, rhs, k, n):
                return nc.tensor.matmul(o, lhsT, rhs, start=(k == 0), stop=(k == n - 1))

            def to_T(name, rows, ev_name):
                banks = [bank(f"{name}{g}") for g in range(4)]
                for t in range(NT):
                    pe.wait_ge(ev(ev_name), t + 1)
                    for g, b in enumerate(banks):
                        for c in range(2):
                            last = nc.tensor.transpose(psum[:, b, c * T + t * P:c * T + t * P + P],
                                                       rows[:, t, (2 * g + c) * P:(2 * g + c + 1) * P], ident[:, :])
                        if t == NT - 1:
                            last.then_inc(bank_full[b], 1)

            def proj_T(name, w, src, nk, chunks, first=0):
                for g in range(first // 2, chunks // 2):
                    b = bank(f"{name}{g}")
                    for c in range(2):
                        m = (2 * g + c) * P
                        for k in range(nk):
                            last = mm(psum[:, b, c * T:(c + 1) * T], w[:, k, m:m + P], src[:, k, :], k, nk)
                    last.then_inc(bank_full[b], 1)

            def landed(places, name):
                s, n = places[name]
                pe.wait_ge((piece_in if places is place1 else piece2_in)[s], 16 * n)

            pe.wait_ge(const_in, 16 * N_CONST)
            to_T("xn", scratch, "xn_ready")
            pe.wait_ge(prm_in, 16 * N_PRM)
            b = bank("prm")
            nc.tensor.transpose(psum[:, b, 0:100], prm[0:100, 0, :], ident[0:100, 0:100])
            nc.tensor.transpose(psum[:, b, 104:228], prm[0:124, 1, :], ident[0:124, 0:124])
            nc.tensor.transpose(psum[:, b, 228:276], prm[0:48, 2, :], ident[0:48, 0:48])
            nc.tensor.transpose(psum[0:64, b, 276:280], prmD[:, :], ident[0:4, 0:4])
            nc.tensor.transpose(psum[:, b, 280:296], crow[:, :], ident[0:16, 0:16]).then_inc(bank_full[b], 1)

            def sine_layer(i):
                b = bank(f"f{i}")
                if i == 0:
                    pe.wait_ge(ev("filt_in"), 16 * 4)
                    last = mm(psum[0:64, b, 0:T], w1s, feat, 0, 1)
                else:
                    pe.wait_ge(ev("sine_done"), i)
                    last = mm(psum[0:64, b, 0:T], w23[:, i - 1, :], fsmall[:, 2 * (i - 1), :], 0, 1)
                last.then_inc(bank_full[b], 1)

            def filter_spectra(o):
                b = bank(f"habs{o}")
                for t in range(NT):
                    pe.wait_ge(ev("abs_ready"), NT * o + t + 1)
                    last = mm(psum[:, b, :], ones[:, :], absb[:, t, :], t, NT)
                last.then_inc(bank_full[b], 1)
                pe.wait_ge(ev("ed_ready"), o + 1)
                for part in range(2):
                    for f in range(NT):
                        b = bank(f"sp{o}{part}{f}")
                        for t in range(NT):
                            last = mm(psum[:, b, :], dft[:, part, t, f * P:(f + 1) * P], filt[:, t, 2 * o + part, :], t, NT)
                        last.then_inc(bank_full[b], 1)

            sine_layer(0)
            for g in range(4):
                emptied(pe, f"xn{g}")
            landed(place1, "wa")
            proj_T("wa", pview(place1, "wa"), actT, KD, 2)
            sine_layer(1)
            proj_T("wa", pview(place1, "wa"), actT, KD, 4, 2)
            sine_layer(2)
            landed(place1, "wg")
            proj_T("wg", pview(place1, "wg"), actT, KD, 2)
            pe.wait_ge(ev("sine_done"), 3)
            landed(place1, "filt4")
            w4 = ring[0:64, place1["filt4"][0], 0:2048]
            for t in range(NT):
                for m in range(4):
                    b = bank(f"h{t}{m}")
                    mm(psum[:, b, :], fsmall[:, 4, t * P:(t + 1) * P], w4[:, m * CH:(m + 1) * CH], 0, 1) \
                        .then_inc(bank_full[b], 1)
            proj_T("wg", pview(place1, "wg"), actT, KD, 4, 2)
            landed(place1, "wq")
            proj_T("wq", pview(place1, "wq"), actT, KD, 4)
            pe.wait_ge(ev("tables_in"), 16 * 6)
            filter_spectra(0)
            landed(place1, "wkv")
            w = pview(place1, "wkv", 256)
            b = bank("k1")
            for k in range(KD):
                last = mm(psum[:, b, 0:T], w[:, k, 0:P], actT[:, k, :], k, KD)
            last.then_inc(bank_full[b], 1)
            b = bank("v1")
            for t in range(NT):
                for k in range(KD):
                    last = mm(psum[:, b, t * P:(t + 1) * P], actT[:, k, t * P:(t + 1) * P], w[:, k, P:2 * P], k, KD)
            last.then_inc(bank_full[b], 1)
            filter_spectra(1)
            emptied(pe, "wq0")
            emptied(pe, "wq1")
            emptied(pe, "k1")

            def score(b, col, h, t, k0, k1):
                r = slice((h % 2) * HD, (h % 2) * HD + HD)
                return mm(psum[:, b, col:col + k1 - k0], qT[r, h // 2, t * P:(t + 1) * P], kdup[r, h // 4, k0:k1], 0, 1)

            for par in range(2):
                b = bank(f"s0{par}")
                for i in range(4):
                    last = score(b, i * P, 2 * i + par, 0, 0, P)
                last.then_inc(bank_full[b], 1)
            for par in range(2):
                for pr in range(2):
                    b = bank(f"s1{par}{pr}")
                    for i in range(2):
                        last = score(b, i * T, 4 * pr + 2 * i + par, 1, 0, T)
                    last.then_inc(bank_full[b], 1)

            mod_bank = bank("mod", (7,))
            emptied(pe, "prm")

            def turn(i):
                emptied(pe, f"mr{i}")
                for m in range(4):
                    o = 2 * (4 * i + m)
                    last = nc.tensor.transpose(psum[:, mod_bank, o:o + 2], mrow[:, i % 4, m * P:(m + 1) * P], ident[0:2, 0:2])
                if i < len(mod_pieces) - 1:
                    last.then_inc(ev("mod_turned"), 1)
                else:
                    last.then_inc(bank_full[mod_bank], 1)

            for i, j in enumerate(mod_pieces):
                landed(place1, f"ada{j}")
                w = pview(place1, f"ada{j}")
                b = bank(f"mr{i}")
                for k in range(KD):
                    last = mm(psum[0:2, b, :], scT[:, k, :], w[:, k, :], k, KD)
                last.then_inc(bank_full[b], 1)
                if i:
                    turn(i - 1)
            turn(len(mod_pieces) - 1)

            def pv1(h):
                r = slice((h % 2) * HD, (h % 2) * HD + HD)
                emptied(pe, f"pt{h}")
                if h % 2 == 0:
                    bank(f"pv{h // 2}")
                b = groups[f"pv{h // 2}"][0]
                g = (h // 4) * HD
                s = pTbuf[:, h % 4, :]
                mm(psum[r, b, 0:P], vtok[:, 0, g:g + HD], s[:, 0:P], 0, 1)
                mm(psum[r, b, P:T], vtok[:, 0, g:g + HD], s[:, P:2 * P], 0, 2)
                last = mm(psum[r, b, P:T], vtok[:, 1, g:g + HD], s[:, 2 * P:3 * P], 1, 2)
                if h % 2:
                    last.then_inc(bank_full[b], 1)
                return last

            def attend1():
                pe.wait_ge(ev("p1_ready"), 2)
                emptied(pe, "v1")
                for h in range(HEADS):
                    b = bank(f"pt{h}")
                    for i, (t, kc) in enumerate(((0, 0), (1, 0), (1, 1))):
                        last = nc.tensor.transpose(psum[:, b, i * P:(i + 1) * P], prob1[:, t, h, kc * P:(kc + 1) * P], ident[:, :])
                    last.then_inc(bank_full[b], 1)
                    if h:
                        pv1(h - 1)
                pv1(HEADS - 1)

            pe.wait_ge(ev("conv_ready"), 1)
            for t in range(NT):
                b = bank(f"yt{t}")
                for c in range(KC):
                    last = nc.tensor.transpose(psum[:, b, c * P:(c + 1) * P], yT[:, c, t * P:(t + 1) * P], ident[:, :])
                last.then_inc(bank_full[b], 1)
            for g in range(2):
                emptied(pe, "yt0")
                emptied(pe, "yt1")
                b = bank(f"yb{g}")
                for c in range(2):
                    for t in range(NT):
                        last = nc.tensor.transpose(psum[:, b, c * T + t * P:c * T + t * P + P],
                                                   ytok[:, t, (2 * g + c) * P:(2 * g + c + 1) * P], ident[:, :])
                last.then_inc(bank_full[b], 1)

            def merge(pl, tag, branches, only=(0, 1)):
                for br in only:
                    src, need = branches[br]
                    landed(pl, f"o{br}")
                    wo = ring[:, pl[f"o{br}"][0], :].rearrange("p (k n) -> p k n", k=KC)
                    for half in range(2):
                        landed(pl, f"g{br}{half}")
                        wg = pview(pl, f"g{br}{half}")
                        for g in range(2):
                            i = 2 * half + g
                            b = bank(f"{tag}g{br}{i}")
                            for c in range(2):
                                for k in range(KD):
                                    last = mm(psum[:, b, c * T:(c + 1) * T], wg[:, k, (2 * g + c) * P:(2 * g + c + 1) * P],
                                              actT[:, k, :], k, KD)
                            last.then_inc(bank_full[b], 1)
                            if i == 0:
                                for nm in need:
                                    emptied(pe, nm)
                                if tag == "b" and br == 1:
                                    pe.wait_ge(ev("hy_ready"), 1)
                            b = bank(f"{tag}o{br}{i}")
                            for c in range(2):
                                m = (2 * i + c) * P
                                for k in range(KC):
                                    last = mm(psum[:, b, c * T:(c + 1) * T], wo[:, k, m:m + P], src[:, k, :], k, KC)
                            last.then_inc(bank_full[b], 1)

            def out_proj(pl, tag):
                pe.wait_ge(ev(f"{tag}merged"), 1)
                for t in range(NT):
                    for n in range(2):
                        landed(pl, f"wo{n}")
                        w = pview(pl, f"wo{n}")
                        b = bank(f"{tag}x{t}{n}")
                        for k in range(KD):
                            last = mm(psum[:, b, :], mergedT[:, k, t * P:(t + 1) * P], w[:, k, :], k, KD)
                        last.then_inc(bank_full[b], 1)

            branches = [(yactT, ("yb0", "yb1")), (attnT, tuple(f"pv{i}" for i in range(4)))]
            merge(place1, "a", branches, (0,))
            attend1()
            merge(place1, "a", branches, (1,))
            out_proj(place1, "a")
            to_T("rn", scratch, "rn_ready")
            for g in range(4):
                emptied(pe, f"rn{g}")
            b = bank("route")
            for t in range(NT):
                for k in range(KD):
                    last = mm(psum[:, b, t * 64:t * 64 + 36], actT[:, k, t * P:(t + 1) * P], wroute[:, k, :], k, KD)
            last.then_inc(bank_full[b], 1)
            to_T("cx", ctxr, "ctxn_ready")
            landed(place1, "ctxkv")
            for g in range(4):
                emptied(pe, f"cx{g}")
            w = pview(place1, "ctxkv", 256)
            for t in range(NT):
                b = bank(f"ckv{t}")
                for k in range(KD):
                    last = mm(psum[:, b, 0:256], actT[:, k, t * P:(t + 1) * P], w[:, k, :], k, KD)
                last.then_inc(bank_full[b], 1)
            pe.wait_ge(ev("assign_ready"), 1)
            asg = arena2[:, 512:576].rearrange("p (t e) -> p t e", t=NT)
            b = bank("pos")
            mm(psum[:, b, 0:32], before[:, :], asg[:, 0, :], 0, 1)
            mm(psum[:, b, 32:64], ones[:, :], asg[:, 0, :], 0, 2)
            mm(psum[:, b, 32:64], before[:, :], asg[:, 1, :], 1, 2)
            mm(psum[:, b, 64:96], ones[:, :], asg[:, 0, :], 0, 2)
            mm(psum[:, b, 64:96], ones[:, :], asg[:, 1, :], 1, 2).then_inc(bank_full[b], 1)
            b = bank("ckT")
            pe.wait_ge(ev("ck_ready"), 1)
            for t in range(NT):
                last = nc.tensor.transpose(psum[:, b, t * P:(t + 1) * P], kvt[:, t * 256:t * 256 + P], ident[:, :])
            last.then_inc(bank_full[b], 1)
            for b in range(8):
                pe.wait_ge(bank_read[b], fills[b])

            pe.wait_ge(ev("trips_ready"), 1)
            n_iter = pe.value_load(trips[0:1, 0:1], min_val=STEPS, max_val=MAXSTEPS)
            pe.sem_inc(ev("rowsT_full1"), 1)
            pe.sem_inc(ev("down_full1"), 1)

            def rows_T(h, n):
                pe.wait_ge(ev(f"rows_in{h}"), 16 * n)
                pe.sem_inc(pe_step, 1)
                for c in range(KD):
                    last = nc.tensor.transpose(psum[:, 0, c * CAP:(c + 1) * CAP], xrow[:, h, c * P:(c + 1) * P],
                                               ident[0:CAP, 0:CAP])
                last.then_inc(ev(f"rowsT_full{h}"), 1)

            pe.wait_ge(ev("rows_in0"), 16)
            rows_T(0, 1)
            with pe.Fori(0, n_iter) as i:
                def up(h, j):
                    s = 3 * h + j
                    pe.wait_ge(piece_in[s], 16 * i + 16 * (base_use[s] + 1))
                    if j == 0:
                        pe.wait_ge(ev(f"rowsT_ready{h}"), i + 1)
                    w = ring[:, s, :].rearrange("p (k n) -> p k n", k=KD)
                    for k in range(KD):
                        last = mm(psum[0:CAP, 2 + 2 * h + j, :], xT[:, h, k, :], w[:, k, :], k, KD)
                    last.then_inc(ev(("gate_full", "up_full")[j] + str(h)), 1)

                def hid_T(h):
                    pe.wait_ge(ev(f"hid_ready{h}"), i + 1)
                    pe.sem_inc(pe_step, 1)
                    for k in range(4):
                        last = nc.tensor.transpose(psum[:, 1, (4 * h + k) * CAP:(4 * h + k + 1) * CAP],
                                                   hrow[:, h, k * P:(k + 1) * P], ident[0:CAP, 0:CAP])
                    last.then_inc(ev(f"hidT_full{h}"), 1)

                def down(h, n):
                    s = 3 * h + 2
                    if n == 0:
                        pe.wait_ge(piece_in[s], 16 * i + 16 * (base_use[s] + 1))
                        pe.wait_ge(ev(f"hidT_ready{h}"), i + 1)
                    w = ring[:, s, :].rearrange("p (k n) -> p k n", k=4)
                    pe.wait_ge(ev(f"down_read{n}"), 2 * i + h + 1)
                    for k in range(4):
                        last = mm(psum[0:CAP, 6 + n, :], hidT[:, h, k, :], w[:, k, n * 512:(n + 1) * 512], k, 4)
                    last.then_inc(ev(f"down_full{n}"), 1)

                up(0, 0)
                rows_T(1, i + 1)
                up(0, 1)
                up(1, 0)
                hid_T(0)
                up(1, 1)
                down(0, 0)
                hid_T(1)
                down(0, 1)
                rows_T(0, i + 2)
                down(1, 0)
                down(1, 1)

            pe.wait_ge(ev("down_read0"), n_iter * 2 + 1)
            pe.wait_ge(ev("down_read1"), n_iter * 2 + 1)
            pe.sem_inc(pe_step, 1)
            everyday.append(tuple(range(8)))
            for j, nm in enumerate(("m4", "m5", "m10", "m11")):
                landed(place2, nm)
                if j == 0:
                    pe.wait_ge(ev("gbias_in"), 16 * 2)
                w = pview(place2, nm)
                b = bank(f"G{j}")
                mm(psum[0:1, b, :], ones[0:1, 0:1], gbias[:, j, :], 0, KD + 1)
                for k in range(KD):
                    last = mm(psum[0:1, b, :], scT[:, k, 0:1], w[:, k, :], k + 1, KD + 1)
                last.then_inc(bank_full[b], 1)
            to_T("zn", scratch, "zn_ready")
            for g in range(4):
                emptied(pe, f"zn{g}")
            landed(place2, "q")
            w = pview(place2, "q")
            for t in range(NT):
                b = bank(f"q{t}")
                for k in range(KD):
                    last = mm(psum[:, b, :], actT[:, k, t * P:(t + 1) * P], w[:, k, :], k, KD)
                last.then_inc(bank_full[b], 1)
            landed(place2, "kv")
            w = pview(place2, "kv", 256)
            for t in range(NT):
                b = bank(f"kv{t}")
                for k in range(KD):
                    last = mm(psum[:, b, 0:256], actT[:, k, t * P:(t + 1) * P], w[:, k, :], k, KD)
                last.then_inc(bank_full[b], 1)
            for j in range(3):
                landed(place2, f"hy{j}")
                proj_T(f"hy{j}", pview(place2, f"hy{j}"), actT, KD, 4)
            pe.wait_ge(ev("qk2_ready"), 1)
            for g in range(2):
                b = bank(f"qT{g}")
                for c in range(2):
                    for t in range(NT):
                        last = nc.tensor.transpose(psum[:, b, c * T + t * P:c * T + t * P + P],
                                                   qtok[:, t, (2 * g + c) * P:(2 * g + c + 1) * P], ident[:, :])
                last.then_inc(bank_full[b], 1)
            b = bank("kT")
            for t in range(NT):
                last = nc.tensor.transpose(psum[:, b, t * P:(t + 1) * P], ktok[:, t, :], ident[:, :])
            last.then_inc(bank_full[b], 1)
            emptied(pe, "qT0")
            emptied(pe, "qT1")
            pe.wait_ge(ev("k2_ready"), 1)
            units = [(h, t) for h in range(HEADS) for t in range(NT)]

            def score2(u):
                h, t = units[u]
                b = bank(f"sc{u}", (0, 1, 2, 3))
                score(b, 0, h, t, 0, 2 * T).then_inc(bank_full[b], 1)

            def pt2(u):
                pe.wait_ge(ev("p2_ready"), u + 1)
                b = bank(f"qt{u}", (0, 1, 2, 3))
                for kc in range(4):
                    last = nc.tensor.transpose(psum[:, b, kc * P:(kc + 1) * P], prob2[:, u % 4, kc * P:(kc + 1) * P], ident[:, :])
                last.then_inc(bank_full[b], 1)

            def pv2(u):
                h, t = units[u]
                emptied(pe, f"qt{u}")
                if u % 4 == 0:
                    bank(f"pw{h // 2}", (6, 7))
                b = groups[f"pw{h // 2}"][0]
                r = slice((h % 2) * HD, (h % 2) * HD + HD)
                for kc in range(4):
                    last = mm(psum[r, b, t * P:(t + 1) * P], vtok[:, kc, (h // 4) * HD:(h // 4 + 1) * HD],
                              pT2[:, u % 2, kc * P:(kc + 1) * P], kc, 4)
                if u % 4 == 3:
                    last.then_inc(bank_full[b], 1)

            def hy_rows(o):
                src = (zs[:, 0:4, :], y1T)[o]
                pe.wait_ge(ev(("short_ready", "y1_ready")[o]), 1)
                for t in range(NT):
                    b = bank(f"vt{o}{t}", (4, 5))
                    for c in range(KC):
                        last = nc.tensor.transpose(psum[:, b, c * P:(c + 1) * P], src[:, c, t * P:(t + 1) * P], ident[:, :])
                    last.then_inc(bank_full[b], 1)

            def hy_spectrum(o, part):
                for t in range(NT):
                    emptied(pe, f"vt{o}{t}")
                for f in range(NT):
                    b = bank(f"U{o}{part}{f}", (4, 5))
                    for t in range(NT):
                        last = mm(psum[:, b, :], dft[:, part, t, f * P:(f + 1) * P], vtime[:, t, :], t, NT)
                    last.then_inc(bank_full[b], 1)

            def hy_back(o, g):
                pe.wait_ge(ev("Y_ready"), o + 1)
                b = bank(f"I{o}{g}", (4, 5))
                for c in range(2):
                    for k in range(4):
                        last = mm(psum[:, b, c * T:(c + 1) * T], Y[:, k, (2 * g + c) * P:(2 * g + c + 1) * P], idft[:, k, :], k, 4)
                last.then_inc(bank_full[b], 1)

            hy_parts = {0: (hy_rows, 0), 1: (hy_spectrum, 0, 0), 2: (hy_spectrum, 0, 1), 6: (hy_back, 0, 0), 7: (hy_back, 0, 1),
                        9: (hy_rows, 1), 10: (hy_spectrum, 1, 0), 11: (hy_spectrum, 1, 1), 15: (hy_back, 1, 0)}
            score2(0)
            score2(1)
            for u in range(16):
                if u + 2 < 16:
                    score2(u + 2)
                if u in hy_parts:
                    hy_parts[u][0](*hy_parts[u][1:])
                pt2(u)
                if u:
                    pv2(u - 1)
            pv2(15)
            hy_back(1, 1)
            merge(place2, "b", [(attnT, tuple(f"pw{i}" for i in range(4))), (hyoT, ())])

            out_proj(place2, "b")
            pe.wait_ge(ev("keys1_in"), 16)
            landed(place2, "keys")
            kp = ring[:, place2["keys"][0], 0:2048].rearrange("p (c d) -> p c d", d=P)
            for g in range(4):
                b = bank(f"keyT{g}")
                for c in range(4):
                    last = nc.tensor.transpose(psum[:, b, c * P:(c + 1) * P], kp[:, 4 * g + c, :], ident[:, :])
                last.then_inc(bank_full[b], 1)
            to_T("pn", scratch, "pn_ready")
            for g in range(4):
                emptied(pe, f"pn{g}")
                emptied(pe, f"keyT{g}")
            for t in range(NT):
                for n in range(2):
                    b = bank(f"xp{t}{n}")
                    for c in range(4):
                        last = nc.tensor.transpose(psum[:, b, c * P:(c + 1) * P], actT[:, 4 * n + c, t * P:(t + 1) * P], ident[:, :])
                    last.then_inc(bank_full[b], 1)

            def key_scores(t, g):
                for pair in range(2):
                    emptied(pe, f"pq{g}{pair}")
                b = bank(f"ks{t}{g}")
                for i in range(4):
                    h, half = (4 * g + i) // 2, (4 * g + i) % 2
                    last = mm(psum[:, b, i * P:(i + 1) * P], pqT[:, 2 * h + half, t * P:(t + 1) * P],
                              keysT[:, half * 8 + h, :], 0, 1)
                last.then_inc(bank_full[b], 1)

            for j in range(4):
                landed(place2, f"pq{j}")
                proj_T(f"pq{j}", pview(place2, f"pq{j}"), actT, KD, 4)
                if j:
                    key_scores(0, j - 1)
            key_scores(0, 3)
            for g in range(4):
                key_scores(1, g)

        @block.sync
        def _(sp):
            for t in range(NT):
                sp.dma_start(resid[:, t, :], A["x"][0, t * P:(t + 1) * P, :]).then_inc(ev(f"x_in{t}"), 16)
            sp.dma_start(ident[:, :], A["c_ident"]).then_inc(const_in, 16)
            rows_A = [("g_mix", 8), ("b_dw", 4), ("ln_conv_g", 4), ("ln_conv_b", 4), ("norm_mix_g_2", 8),
                      ("norm_ffn_g_2", 8), ("g_ffn", 8)]
            r = 0
            for nm, n in rows_A:
                sp.dma_start(prm[r:r + n, 0, :], A[nm][0].rearrange("(r c) -> r c", c=P)).then_inc(prm_in, 16)
                r += n
            sp.dma_start(prm[r:r + 36, 0, :], A["hy_conv_w_2"][0].rearrange("j (r c) -> (j r) c", c=P)).then_inc(prm_in, 16)
            r += 36
            sp.dma_start(prm[r:r + 12, 0, :], A["hy_conv_b_2"][0].rearrange("(r c) -> r c", c=P)).then_inc(prm_in, 16)
            r += 12
            sp.dma_start(prm[r:r + 8, 0, :], A["hy_skip_2"][0].rearrange("j (r c) -> (j r) c", c=P)).then_inc(prm_in, 16)
            assert r + 8 == 100
            sp.dma_start(prm[0:124, 1, :], A["w_dw"][0, :, 0, :].rearrange("j (r c) -> (j r) c", c=P)).then_inc(prm_in, 16)
            sp.dma_start(prm[0:48, 2, :], A["ada_b_2"][0].rearrange("(r c) -> r c", c=P)).then_inc(prm_in, 16)
            for i, nm in enumerate(("hf_b1_2", "hf_b2_2", "hf_b3_2", "hf_freq_2")):
                sp.dma_start(prmD[i:i + 1, :], A[nm]).then_inc(prm_in, 16)
            sp.dma_start(crow[0:8, :], A["c_2"][0].rearrange("(r c) -> r c", c=P)).then_inc(prm_in, 16)
            sp.dma_start(crow[8:16, :], A["c_ctx_2"].rearrange("(r c) -> r c", c=P)).then_inc(prm_in, 16)
            sp.dma_start(w1s, A["hf_w1_2"][0]).then_inc(ev("filt_in"), 16)
            sp.dma_start(feat, A["c_feat"]).then_inc(ev("filt_in"), 16)
            sp.dma_start(w23[:, 0, :], A["hf_w2_2"][0]).then_inc(ev("filt_in"), 16)
            sp.dma_start(w23[:, 1, :], A["hf_w3_2"][0]).then_inc(ev("filt_in"), 16)

            last_reader = {**{f"ada{j}": f"mr{i}" for i, j in enumerate(mod_pieces)}, "ctxkv": "ckv1", "filt4": "h13", "wa": "wa1", "wg": "wg1",
                           "wq": "wq1", "wkv": "v1", "o0": "ao03", "g00": "ag01", "g01": "ag03", "o1": "ao13",
                           "g10": "ag11", "g11": "ag13", "wo0": "ax10", "wo1": "ax11"}

            def filled(name):
                b, n = groups[name]
                sp.wait_ge(bank_full[b], n)

            for i, (nm, src) in enumerate(pieces):
                s = i % SLOTS
                if i >= SLOTS:
                    filled(last_reader[pieces[i - SLOTS][0]])
                dst = ring[0:64, s, 0:2048] if nm == "filt4" else view(s, src)
                sp.dma_start(dst, src).then_inc(piece_in[s], 16)
                if nm == "filt4":
                    for dstt, cn in ((before, "c_before"), (rel, "c_rel"), (iota, "c_iota")):
                        sp.dma_start(dstt[:, :], A[cn]).then_inc(ev("tables_in"), 16)
                    sp.dma_start(tok2[:, :, :], A["c_decay"].rearrange("p a m c -> p a (m c)")).then_inc(dec_in, 16)
                if nm == "wq":
                    sp.dma_start(dft[:, :, :, :], A["c_dft"]).then_inc(ev("tables_in"), 16)
                    sp.dma_start(idft[:, :, :], A["c_idft"]).then_inc(ev("tables_in"), 16)
                    sp.dma_start(rope[:, :, :, :], A["c_rope"]).then_inc(ev("tables_in"), 16)
                if nm == "wo0":
                    filled("pt7")
                    sp.dma_start(ctxr, A["ctx_2"][0].rearrange("(t p) d -> p t d", p=P)).then_inc(ctx_in, 16)

            def expert_piece(s, e):
                h, j = s // 3, s % 3
                w = (A["w_gate"], A["w_up"], A["w_down"])[j][0]
                src = w[e, :, :] if isinstance(e, int) else w[bass.ds(e, 1), :, :].rearrange("e k n -> (e k) n")
                k = 4 if j == 2 else KD
                sp.dma_start(ring[:, s, :].rearrange("p (k n) -> p k n", k=k),
                             src.rearrange("(k p) n -> p k n", p=P)).then_inc(piece_in[s], 16)

            for s in range(SLOTS):
                prev = [nm for i, (nm, _) in enumerate(pieces) if i % SLOTS == s][-1]
                filled(last_reader[prev])
                expert_piece(s, s // 3)

            filled("ckv1")
            sp.dma_start(actT[0:1, 0:4, :].rearrange("p k t -> p (k t)"), A["ada_b_2"][:, 2 * D:3 * D]).then_inc(ev("gbias_in"), 16)
            sp.dma_start(actT[0:1, 4:8, :].rearrange("p k t -> p (k t)"), A["ada_b_2"][:, 5 * D:6 * D]).then_inc(ev("gbias_in"), 16)

            def expert_step(i, experts):
                for s in range(SLOTS):
                    h = s // 3
                    if s % 3 < 2:
                        sp.wait_ge(ev(("gate_full", "up_full")[s % 3] + str(h)), i)
                    else:
                        sp.wait_ge(ev("down_full1"), 2 * i + h)
                    expert_piece(s, experts[h])

            with sp.Fori(1, STEPS - 1) as i:
                expert_step(i, (2 * i, 2 * i + 1))
            sp.wait_ge(ev("trips_ready"), 1)
            n_iter = sp.value_load(trips[0:1, 0:1], min_val=STEPS, max_val=MAXSTEPS)
            with sp.Fori(STEPS - 1, n_iter) as i:
                expert_step(i, [sp.value_load(elist[0:1, bass.ds(i * 2 + h, 1)], min_val=0, max_val=EXPERTS - 1) for h in range(2)])

            last2 = {"q": "q1", "kv": "kv1", "hy0": "hy01", "hy1": "hy11", "hy2": "hy21", "room": "I11", "o0": "bo03", "g00": "bg01",
                     "g01": "bg03", "o1": "bo13", "g10": "bg11", "g11": "bg13", "m4": "G0", "m5": "G1", "m10": "G2", "m11": "G3",
                     "wo0": "bx10", "wo1": "bx11", "keys": "keyT3", "pq0": "pq01", "pq1": "pq11", "pq2": "pq21",
                     "pq3": "pq31"}
            for i, (nm, src) in enumerate(pieces2):
                s = i % SLOTS
                if i < SLOTS:
                    if s % 3 < 2:
                        sp.wait_ge(ev(("gate_full", "up_full")[s % 3] + str(s // 3)), n_iter)
                    else:
                        sp.wait_ge(ev("down_full1"), 2 * n_iter + s // 3)
                else:
                    filled(last2[pieces2[i - SLOTS][0]])
                if nm == "hy1":
                    sp.wait_ge(ev("fetched"), 16 * 4)
                if nm == "room":
                    continue
                if nm == "keys":
                    kp = ring[:, s, 0:2048].rearrange("p (a h d) -> p a h d", a=2, d=P)
                    for half, knm in enumerate(("peer_keys1_2", "peer_keys2_2")):
                        sp.dma_start(kp[:, half, :, :], A[knm][0].rearrange("h n d -> n h d")).then_inc(
                            (ev("keys1_in"), piece2_in[s])[half], 16)
                    continue
                sp.dma_start(view(s, src), src).then_inc(piece2_in[s], 16)
                if nm == "q":
                    sp.wait_ge(ev("amerged"), 1)
                    sp.dma_start(gfrow, A["g_final"].rearrange("(a n) -> a n", a=1).to_broadcast([P, D])).then_inc(ev("gf_in"), 16)
                if nm == "g11":
                    filled("pw3")
                    sp.wait_ge(ev("grow_sent"), 16)
                    sp.dma_start(g1row, gate_rows[0:1, 0:D].to_broadcast([P, D])).then_inc(ev("g1_in"), 16)
                if nm == "pq3":
                    filled("bx11")
                    sp.dma_start(g2row, gate_rows[0:1, D:2 * D].to_broadcast([P, D])).then_inc(ev("g2_in"), 16)
                    sp.dma_start(flrow, A["final_norm_g_2"].rearrange("(a n) -> a n", a=1).to_broadcast([P, D])).then_inc(ev("g2_in"), 16)
            for t in range(NT):
                sp.wait_ge(ev("final_ready"), t + 1)
                sp.dma_start(out[0, t * P:(t + 1) * P, :], resid[:, t, :]).then_inc(ev("out_sent"), 16)
            sp.wait_ge(ev("out_sent"), 16 * NT)

        @block.gpsimd
        def _(pool):
            steps = [0]

            def own(ins):
                steps[0] += 1
                ins.then_inc(pool_step, 1)
                pool.wait_ge(pool_step, steps[0])

            nc.gpsimd.memset(ones[:, :], 1.0).then_inc(const_in, 16)
            nc.gpsimd.memset(epscol[:, :], EPS).then_inc(const_in, 16)
            for dst, nm in ((rbias[:, 0:GROUPS], "b_group"), (rbias[:, GROUPS:], "b_expert"), (sinkrow[:, :], "sinks"),
                            (qkg[:, 0, :], "q_norm_g_2"), (qkg[:, 1, :], "k_norm_g_2")):
                pool.dma_start(dst, A[nm].to_broadcast([P, A[nm].shape[1]])).then_inc(ev("rows_in"), 16)
            pool.dma_start(wroute[:, :, 0:GROUPS], A["w_group"][0].rearrange("(k p) n -> p k n", p=P)).then_inc(ev("rows_in"), 16)
            pool.dma_start(wroute[:, :, GROUPS:], A["w_expert"][0].rearrange("(k p) n -> p k n", p=P)).then_inc(ev("rows_in"), 16)
            b, n = groups["prm"]
            pool.wait_ge(bank_full[b], n)
            own(nc.gpsimd.memset(zeros, 0.0))
            pool.wait_ge(ev("conv_ready"), 1)
            z4 = zeros.unsqueeze(1).to_broadcast([P, 4, T])
            for b in range(ROWS // P + 1):
                pool.dma_start(xs[b * P:(b + 1) * P, :].rearrange("r (q c) -> r q c", q=4), z4).then_inc(ev("zeroed"), 16)
            for b in range(EXPERTS * CAP // P, ROWS // P):
                pool.dma_start(ys[b * P:(b + 1) * P, :].rearrange("r (q c) -> r q c", q=4), z4).then_inc(ev("zeroed"), 16)
            pool.wait_ge(ev("trips_ready"), 1)
            n_iter = pool.value_load(trips[0:1, 0:1], min_val=STEPS, max_val=MAXSTEPS)
            pool.wait_ge(ev("zeroed"), 16 * ZEROED)
            pool.wait_ge(ev("rn_ready"), NT)
            for t in range(NT):
                for k in range(2):
                    pool.indirect_dma_start(out=xs[:, :], out_offset=bass.IndirectOffsetOnAxis(ap=sloti[:, 2 * t + k:2 * t + k + 1], axis=0),
                                            in_=scratch[:, t, :], in_offset=None).then_inc(ev("sent"), 16)
            pool.wait_ge(ev("sent"), 16 * 2 * NT)
            pool.dma_start(xrow[:, 0, :], xs[0:CAP, :]).then_inc(ev("rows_in0"), 16)
            with pool.Fori(0, n_iter) as i:
                pool.wait_ge(ev("rowsT_full1"), i + 1)
                pool.sem_inc(pool_step, 1)
                pool.dma_start(xrow[:, 1, :], xs[bass.ds((i * 2 + 1) * CAP, CAP), :]).then_inc(ev("rows_in1"), 16)
                pool.wait_ge(ev("rowsT_full0"), i + 1)
                pool.sem_inc(pool_step, 1)
                pool.dma_start(xrow[:, 0, :], xs[bass.ds((i * 2 + 2) * CAP, CAP), :]).then_inc(ev("rows_in0"), 16)
            pool.wait_ge(ev("stored0"), n_iter * 16 + 1)
            pool.sem_inc(pool_step, 1)
            pool.wait_ge(ev("stored1"), n_iter * 16 + 1)
            pool.sem_inc(pool_step, 1)
            for j in range(4):
                pool.indirect_dma_start(out=back[:, j, :], out_offset=None, in_=ys[:, :],
                                        in_offset=bass.IndirectOffsetOnAxis(ap=sloti[:, j:j + 1], axis=0)).then_inc(ev("fetched"), 16)

            filled_b, filled_n = groups["pq31"]
            pool.wait_ge(bank_full[filled_b], filled_n)
            per = PICKS // ROWBUFS
            for r, tab in enumerate(("peer_u_2", "peer_v_2")):
                for t in range(NT):
                    if r == 0:
                        pool.wait_ge(ev("rowid_ready"), t + 1)
                    with pool.Fori(0, per) as i:
                        for b in range(ROWBUFS):
                            pool.wait_ge(ev("row_used"), (i + (2 * r + t) * per) * ROWBUFS + b + 1)
                            pool.sem_inc(pool_step, 1)
                            nc.gpsimd.tensor_copy(cur[:, b:b + 1], rowid[:, t, bass.ds(i * ROWBUFS + b, 1)]).then_inc(ev("cur_set"), 1)
                            pool.wait_ge(ev("cur_set"), (i + (2 * r + t) * per) * ROWBUFS + b + 1)
                            pool.sem_inc(pool_step, 1)
                            pool.indirect_dma_start(out=rows[:, b, :], out_offset=None, in_=A[tab][0],
                                                    in_offset=bass.IndirectOffsetOnAxis(ap=cur[:, b:b + 1], axis=0)).then_inc(ev(f"row_in{b}"), 16)

        @block.scalar
        def _(act):
            counts = {}

            def a(ins, name=None):
                s = ev(name) if name else act_step
                counts[s.name] = counts.get(s.name, 0) + 1
                ins.then_inc(s, 1)
                act.wait_ge(s, counts[s.name])

            def last(ins, name):
                b, n = groups[name]
                ins.then_inc(bank_read[b], 1)
                act.wait_ge(bank_read[b], n)

            def squares(tag, src, ready=None, junk=scratch):
                for t in range(NT):
                    if ready:
                        act.wait_ge(ev(ready), t + 1)
                    if tag == "xn":
                        act.wait_ge(ev(f"x_in{t}"), 16)
                    a(nc.scalar.activation(junk[:, t, :], src[:, t, :], ACT.Square, accum_out=stat(f"{tag}_ss")[:, t:t + 1]))
                    a(nc.scalar.activation(stat(f"{tag}_sd")[:, t:t + 1], stat(f"{tag}_ss")[:, t:t + 1], ACT.Sqrt, bias=epscol[:, 0:1], scale=1.0 / D), f"{tag}_sd")

            def take_T(name, scale, bias=None):
                for g in range(4):
                    ps = full(act, f"{name}{g}")
                    for c in range(2):
                        k = 2 * g + c
                        kw = {} if bias is None else {"bias": bias[:, k:k + 1]}
                        ins = nc.scalar.activation(actT[:, k, :], ps[:, c * T:(c + 1) * T], ACT.Identity, scale=scale[:, k:k + 1], **kw)
                    last(ins, f"{name}{g}")

            def copy_out(name, dst, w=512, func=ACT.Copy, **kw):
                last(nc.scalar.activation(dst, full(act, name)[:, 0:w], func, **kw), name)

            act.wait_ge(const_in, 16 * N_CONST)
            squares("xn", resid)
            act.wait_ge(ev("cols_ready"), 1)
            take_T("xn", colsA[:, 0:8])

            def sine(i):
                act.wait_ge(ev("sine_arg"), i + 1)
                a(nc.scalar.activation(fsmall[:, 2 * i, :], fsmall[:, 2 * i + 1, :], ACT.Sin), "sine_done")

            def pair(dst, g):
                return dst[:, 2 * g:2 * g + 2, :].rearrange("p c t -> p (c t)")

            sine(0)
            copy_out("wa0", pair(aT, 0))
            sine(1)
            copy_out("wa1", pair(aT, 1))
            sine(2)
            ps = full(act, "prm")
            last(nc.scalar.activation(scT[:, :, :].rearrange("p k j -> p j k"), ps[:, 280:296].rearrange("p (j k) -> p j k", j=2), ACT.Silu), "prm")
            for g in range(2):
                copy_out(f"wg{g}", pair(sgT, g), func=ACT.Sigmoid)
            for g in range(2):
                copy_out(f"wq{g}", pair(qT, g))
            ps = full(act, "k1")
            for g in range(KV):
                for half in range(2):
                    ins = nc.scalar.activation(kdup[half * HD:(half + 1) * HD, g, 0:T], ps[g * HD:(g + 1) * HD, 0:T], ACT.Copy)
            last(ins, "k1")
            copy_out("v1", vtok[:, 0:2, :].rearrange("p t c -> p (t c)"), 256)
            act.wait_ge(ev("filters_ready"), 1)
            for par in range(2):
                ps = full(act, f"s0{par}").rearrange("p (i k) -> p i k", i=4)
                dst = prob1[:, 0, :, 0:P].rearrange("p (i r) k -> p r i k", r=2)[:, par, :, :]
                last(nc.scalar.activation(dst, ps, ACT.Copy, scale=HD ** -0.5), f"s0{par}")
            for par in range(2):
                for pr in range(2):
                    ps = full(act, f"s1{par}{pr}").rearrange("p (i k) -> p i k", i=2)
                    dst = prob1[:, 1, 4 * pr:4 * pr + 4, :].rearrange("p (i r) k -> p r i k", r=2)[:, par, :, :]
                    last(nc.scalar.activation(dst, ps, ACT.Copy, scale=HD ** -0.5), f"s1{par}{pr}")
            emptied(act, "h13")
            for i in range(len(mod_pieces)):
                if i >= 4:
                    act.wait_ge(ev("mod_turned"), i - 3)
                last(nc.scalar.activation(mrow[:, i % 4, :], full(act, f"mr{i}")[0:2, :], ACT.Copy), f"mr{i}")
            for t in range(NT):
                act.wait_ge(ev("ln_var"), t + 1)
                a(nc.scalar.activation(stat("ln_sd")[:, t:t + 1], stat("ln_v")[:, t:t + 1], ACT.Sqrt, bias=epscol[:, 0:1]), "ln_sd")
            for g in range(2):
                ps = full(act, f"yb{g}")
                for c in range(2):
                    k = 2 * g + c
                    ins = nc.scalar.activation(yactT[:, k, :], ps[:, c * T:(c + 1) * T], ACT.Silu, scale=colsA[:, 12 + k:13 + k], bias=colsA[:, 16 + k:17 + k])
                last(ins, f"yb{g}")

            def gate_of(tag, j):
                br, i = j // 4, j % 4
                if j >= 2:
                    emptied(act, f"{tag}o{(j - 2) // 4}{(j - 2) % 4}")
                copy_out(f"{tag}g{br}{i}", sgate[tag][:, j % 2, :], func=ACT.Sigmoid)

            for t in range(NT):
                act.wait_ge(ev("p1_shift"), t + 1)
                w = P * (t + 1)
                a(nc.scalar.activation(prob1[:, t, :, 0:w], prob1[:, t, :, 0:w], ACT.Exp))
                a(nc.scalar.activation(stat("p1_es", 16)[:, 8 * t:8 * t + 8], stat("p1_sm", 16)[:, 8 * t:8 * t + 8], ACT.Exp), "p1_exp")
                gate_of("a", t)
            gate_of("a", 2)
            gate_of("a", 3)
            for h in range(HEADS):
                copy_out(f"pt{h}", pTbuf[:, h % 4, 0:384], 384)
                if h % 2 == 0 and h:
                    copy_out(f"pv{h // 2 - 1}", attnT[:, h // 2 - 1, :], T)
            copy_out("pv3", attnT[:, 3, :], T)
            for j in range(4, 8):
                gate_of("a", j)
            act.wait_ge(ctx_in, 16)
            squares("cx", ctxr, None, qjunk)
            squares("rn", resid, "ah_ready")
            take_T("rn", colsA[:, 36:44])
            take_T("cx", modsc[:, 1, :], mod[:, 0:KD, 1])
            act.wait_ge(ev("rt_gmax"), 1)
            for t in range(NT):
                a(nc.scalar.activation(rt[:, 600 + 4 * t:604 + 4 * t], rt[:, 72 + 36 * t:76 + 36 * t], ACT.Exp, bias=stat("rt_ng")[:, t:t + 1],
                                       accum_out=stat("rt_gs")[:, t:t + 1]), "rt_gsum")
            act.wait_ge(ev("rt_top"), 1)
            for t in range(NT):
                a(nc.scalar.activation(stat("rt_e1")[:, t:t + 1], rt[:, 144 + 8 * t + 1:144 + 8 * t + 2], ACT.Exp, bias=stat("rt_nv")[:, t:t + 1]), "rt_e1")

            act.wait_ge(ev("ck_ss"), 1)
            a(nc.scalar.activation(stat("ck_sd", 4), stat("ck_ss", 4), ACT.Sqrt, bias=epscol[:, 0:1], scale=1.0 / HD), "ck_sd")

            act.wait_ge(ev("trips_ready"), 1)
            n_iter = act.value_load(trips[0:1, 0:1], min_val=STEPS, max_val=MAXSTEPS)
            act.sem_inc(ev("down_read0"), 1)
            act.sem_inc(ev("stored0"), 1)
            act.sem_inc(ev("stored1"), 1)
            with act.Fori(0, n_iter) as i:
                for h in range(2):
                    act.wait_ge(ev(f"gate_full{h}"), i + 1)
                    nc.scalar.activation(silu[:, h, :], psum[0:CAP, 2 + 2 * h, :], ACT.Silu).then_inc(ev(f"silu_ready{h}"), 1)

                def hid_out(h):
                    act.wait_ge(ev(f"hidT_full{h}"), i + 1)
                    nc.scalar.activation(hidT[:, h, :, :].rearrange("p k c -> p (k c)"), psum[:, 1, h * 256:(h + 1) * 256],
                                         ACT.Copy).then_inc(ev(f"hidT_ready{h}"), 1)

                def down_out(h):
                    act.wait_ge(ev("down_full0"), 2 * i + h + 1)
                    act.wait_ge(ev(f"stored{h}"), 16 * i + 1)
                    nc.scalar.activation(yrow[:, h, 0:512], psum[0:CAP, 6, :], ACT.Copy).then_inc(ev("down_read0"), 1)

                def store(h):
                    act.wait_ge(ev("down_read0"), 2 * i + h + 2)
                    act.wait_ge(ev("down_read1"), 2 * i + h + 2)
                    act.dma_start(ys[bass.ds((i * 2 + h) * CAP, CAP), :], yrow[:, h, :]).then_inc(ev(f"stored{h}"), 16)

                hid_out(0)
                down_out(0)
                hid_out(1)
                store(0)
                down_out(1)
                store(1)

            def gate_row(j):
                last(nc.scalar.activation(grow[:, j, :], full(act, f"G{j}")[0:1, :], ACT.Copy), f"G{j}")

            for h in range(2):
                act.wait_ge(ev(f"stored{h}"), n_iter * 16 + 1)
            gate_row(0)
            gate_row(1)
            squares("fn", resid, "moe_added", normjunk)
            squares("zn", resid, "x2_ready", normjunk)
            gate_row(2)
            gate_row(3)
            act.dma_start(gate_rows, tok2[0:1, :, :].rearrange("p a d -> p (a d)")).then_inc(ev("grow_sent"), 16)
            take_T("zn", modsc[:, 0, :], mod[:, 0:KD, 0])
            for t in range(NT):
                copy_out(f"q{t}", qtok[:, t, :])
            act.wait_ge(ev("qk_ss"), 1)
            a(nc.scalar.activation(stat("qk_sd", 20), stat("qk_ss", 20), ACT.Sqrt, bias=epscol[:, 0:1], scale=1.0 / HD), "qk_sd")
            for j in range(6):
                if j == 0:
                    act.wait_ge(ev("pads_zero"), 1)
                if j >= 2:
                    act.wait_ge(ev("short_done"), j - 1)
                ps = full(act, f"hy{j // 2}{j % 2}").rearrange("p (c t) -> p c t", c=2)
                last(nc.scalar.activation(hpad[:, j % 2, :, 1:T + 1], ps, ACT.Copy), f"hy{j // 2}{j % 2}")
            for g in range(2):
                copy_out(f"qT{g}", qT[:, 2 * g:2 * g + 2, :].rearrange("p c t -> p (c t)"))

            def exp_unit(u):
                act.wait_ge(ev("nmax"), u + 1)
                if u >= 4:
                    full(act, f"qt{u - 4}")
                else:
                    full(act, "kT")
                last(nc.scalar.activation(prob2[:, u % 4, :], full(act, f"sc{u}"), ACT.Exp, bias=stat("nm2", 16)[:, u:u + 1], scale=HD ** -0.5,
                                          accum_out=stat("sum2", 16)[:, u:u + 1]), f"sc{u}")

            def hy_rows(o):
                for t in range(NT):
                    copy_out(f"vt{o}{t}", vtime[:, t, :])

            def hy_spectrum(o, part):
                if o == 0 and part == 0:
                    act.wait_ge(ev("down_read1"), n_iter * 2 + 1)
                for f in range(NT):
                    copy_out(f"U{o}{part}{f}", Usb[:, 2 * part + f, :])

            hy_parts = {0: (hy_rows, 0), 1: (hy_spectrum, 0, 0), 2: (hy_spectrum, 0, 1),
                        9: (hy_rows, 1), 10: (hy_spectrum, 1, 0), 11: (hy_spectrum, 1, 1)}
            exp_unit(0)
            for u in range(16):
                if u + 1 < 16:
                    exp_unit(u + 1)
                if u in hy_parts:
                    hy_parts[u][0](*hy_parts[u][1:])
                copy_out(f"qt{u}", pT2[:, u % 2, :])
                if u % 4 == 0 and u:
                    copy_out(f"pw{u // 4 - 1}", attnT[:, u // 4 - 1, :], T)
            copy_out("pw3", attnT[:, 3, :], T)
            for j in range(8):
                gate_of("b", j)
            for g in range(4):
                copy_out(f"keyT{g}", keysT[:, 4 * g:4 * g + 4, :].rearrange("p c n -> p (c n)"))
            squares("pn", resid, "bh_ready")
            take_T("pn", modsc[:, 2, :], mod[:, 24:32, 0])
            for t in range(NT):
                for n in range(2):
                    copy_out(f"xp{t}{n}", tok2[:, t, n * 512:(n + 1) * 512])

            def scores_out(t, g):
                copy_out(f"ks{t}{g}", S[:, t, 4 * g:4 * g + 4, :].rearrange("p c n -> p (c n)"))

            for j in range(4):
                for g in range(2):
                    k = 4 * j + 2 * g
                    copy_out(f"pq{j}{g}", pqT[:, k:k + 2, :].rearrange("p c t -> p (c t)"))
                if j:
                    scores_out(0, j - 1)
            scores_out(0, 3)
            for g in range(4):
                scores_out(1, g)
            for t in range(NT):
                act.wait_ge(ev("best_shift"), t + 1)
                a(nc.scalar.activation(gates[:, t, :], gates[:, t, :], ACT.Exp), "best_exp")
            for t in range(NT):
                act.wait_ge(ev("dots_ready"), t + 1)
                a(nc.scalar.activation(dots[:, t, :], dots[:, t, :], ACT.Gelu_apprx_tanh), "gelu_done")
            for t in range(NT):
                act.wait_ge(ev("x3_ready"), t + 1)
                a(nc.scalar.activation(tok2[:, t, :], resid[:, t, :], ACT.Square, accum_out=stat("ff_ss")[:, t:t + 1]))
                a(nc.scalar.activation(stat("ff_sd")[:, t:t + 1], stat("ff_ss")[:, t:t + 1], ACT.Sqrt, bias=epscol[:, 0:1], scale=1.0 / D), "ff_sd")

        @block.vector
        def _(dve):
            counts = {}
            V = nc.vector

            def v(ins, name=None):
                s = ev(name) if name else dve_step
                counts[s.name] = counts.get(s.name, 0) + 1
                ins.then_inc(s, 1)
                dve.wait_ge(s, counts[s.name])

            def v_pair(ins):
                counts[dve_step.name] = counts.get(dve_step.name, 0) + 1
                ins.then_inc(dve_step, 1)
                dve.wait_ge(dve_step, counts[dve_step.name] - 1)

            def v_done():
                dve.wait_ge(dve_step, counts[dve_step.name])

            def last(ins, name):
                b, n = groups[name]
                ins.then_inc(bank_read[b], 1)
                dve.wait_ge(bank_read[b], n)

            def norm_rows(tag, src, name, gain=None):
                for t in range(NT):
                    dve.wait_ge(ev(f"{tag}_sd"), t + 1)
                    r = stat(f"{tag}_r")[:, t:t + 1]
                    v(V.reciprocal(r, stat(f"{tag}_sd")[:, t:t + 1]))
                    if gain is None:
                        v(V.tensor_scalar(scratch[:, t, :], src[:, t, :], r, None, ALU.mult), name)
                    else:
                        v(V.scalar_tensor_tensor(src[:, t, :], src[:, t, :], r, gain, ALU.mult, ALU.mult), name)

            dve.wait_ge(const_in, 16 * N_CONST)
            norm_rows("xn", resid, "xn_ready")
            ps = full(dve, "prm")
            v(V.tensor_copy(colsA[:, 0:100], ps[:, 0:100]))
            v(V.tensor_copy(colsB[:, :], ps[:, 104:228]))
            v(V.tensor_copy(colsC[:, :], ps[:, 228:276]))
            v(V.tensor_copy(colsD[:, :], ps[0:64, 276:280]), "cols_ready")
            C1 = 6.28125
            C2 = 2 * np.pi - C1
            MAGIC = 12582912.0
            for i in range(3):
                x, n = fsmall[:, 2 * i + 1, :], fsmall[:, 6, :]
                ps = full(dve, f"f{i}")
                last(V.tensor_scalar(x, ps[0:64, 0:T], colsD[:, i:i + 1], colsD[:, 3:4], ALU.add, ALU.mult), f"f{i}")
                v(V.tensor_scalar(n, x, 1.0 / (2 * np.pi), MAGIC, ALU.mult, ALU.add))
                v(V.tensor_scalar(n, n, MAGIC, None, ALU.subtract))
                v(V.scalar_tensor_tensor(x, n, -C1, x, ALU.mult, ALU.add))
                v(V.scalar_tensor_tensor(x, n, -C2, x, ALU.mult, ALU.add))
                v(V.tensor_scalar(x, x, 3.1415925, -3.1415925, ALU.min, ALU.max), "sine_arg")
            def keys_dup(name, c0, done=None):
                ps = full(dve, name)
                for g in range(KV):
                    for half in range(2):
                        ins = V.tensor_copy(kdup[half * HD:(half + 1) * HD, g, c0:c0 + T], ps[g * HD:(g + 1) * HD, 0:T])
                        if g == KV - 1 and half == 1:
                            last(ins, name)
                        else:
                            v(ins)

            dve.wait_ge(dec_in, 16)
            dve.wait_ge(ev("tables_in"), 16 * 6)
            for t in range(NT):
                for m in range(4):
                    last(V.tensor_tensor(filt[:, t, m, :], full(dve, f"h{t}{m}"), decay[:, t, m % 2, :], ALU.mult), f"h{t}{m}")
            rn = arena2[:, 3584:4096]
            for o in range(2):
                if o:
                    full(dve, "habs0")
                for t in range(NT):
                    f, g = filt[:, t, 2 * o, :], filt[:, t, 2 * o + 1, :]
                    v(V.scalar_tensor_tensor(absb[:, t, :], f, -1.0, f, ALU.mult, ALU.max))
                    v(V.scalar_tensor_tensor(rn, g, -1.0, g, ALU.mult, ALU.max))
                    v(V.tensor_tensor(absb[:, t, :], absb[:, t, :], rn, ALU.add), "abs_ready")
                for t in range(NT):
                    f, g = filt[:, t, 2 * o, :], filt[:, t, 2 * o + 1, :]
                    v(V.tensor_tensor(rn, f, g, ALU.add))
                    v(V.tensor_tensor(g, f, g, ALU.subtract))
                    v(V.tensor_copy(f, rn), "ed_ready" if t else None)
                last(V.tensor_scalar(rn, full(dve, f"habs{o}"), EPS, None, ALU.add), f"habs{o}")
                v(V.reciprocal(rn, rn))
                for part in range(2):
                    full(dve, f"sp{o}{part}1")
                    for fr in range(NT):
                        last(V.tensor_tensor(spec[:, o, part, fr, :], full(dve, f"sp{o}{part}{fr}"), rn, ALU.mult), f"sp{o}{part}{fr}")
            v(V.tensor_copy(stat("dummy", 1), epscol[:, 0:1]), "filters_ready")

            v(V.memset(vpad[:, :, 0:30], 0.0))
            for g in range(2):
                emptied(dve, f"wa{g}")
                emptied(dve, f"wg{g}")
            v(V.tensor_tensor(vpad[:, :, 30:30 + T], aT, sgT, ALU.mult))
            n = 0
            for j in range(TAPS):
                for c in range(KC):
                    w = colsB[:, j * KC + c:j * KC + c + 1]
                    if n >= KC:
                        dve.wait_ge(ev("tap"), n - KC + 1)
                    if j == 0:
                        V.tensor_scalar(yT[:, c, :], vpad[:, c, 0:T], w, colsA[:, 8 + c:9 + c], ALU.mult, ALU.add).then_inc(ev("tap"), 1)
                    else:
                        V.scalar_tensor_tensor(yT[:, c, :], vpad[:, c, j:j + T], w, yT[:, c, :], ALU.mult, ALU.add).then_inc(ev("tap"), 1)
                    n += 1
            dve.wait_ge(ev("tap"), n)
            v(V.tensor_copy(stat("dummy", 1), epscol[:, 0:1]), "conv_ready")
            for t in range(NT):
                v(V.bn_stats(stat("bn", 12)[:, 6 * t:6 * t + 6], full(dve, f"yt{t}")))
                v(V.bn_aggr(stat("mv", 4)[:, 2 * t:2 * t + 2], stat("bn", 12)[:, 6 * t:6 * t + 6]))
                v(V.tensor_copy(stat("ln_v")[:, t:t + 1], stat("mv", 4)[:, 2 * t + 1:2 * t + 2]), "ln_var")
            for t in range(NT):
                dve.wait_ge(ev("ln_sd"), t + 1)
                v(V.reciprocal(stat("ln_r")[:, t:t + 1], stat("ln_sd")[:, t:t + 1]))
                last(V.tensor_scalar(ytok[:, t, :], full(dve, f"yt{t}"), stat("mv", 4)[:, 2 * t:2 * t + 1], stat("ln_r")[:, t:t + 1],
                                     ALU.subtract, ALU.mult), f"yt{t}")

            dve.wait_ge(ev("rows_in"), 16 * 7)
            for par in range(2):
                emptied(dve, f"s0{par}")
            m, sm, es = stat("p1_m", 16), stat("p1_sm", 16), stat("p1_es", 16)
            for t in range(NT):
                w = P * (t + 1)
                if t:
                    for par in range(2):
                        for pr in range(2):
                            emptied(dve, f"s1{par}{pr}")
                for h in range(HEADS):
                    p = prob1[:, t, h, 0:w]
                    v(V.scalar_tensor_tensor(p, rel[:, 2 * P - w:2 * P], -SLOPES[h], p, ALU.mult, ALU.add))
                mt = m[:, 8 * t:8 * t + 8]
                v(V.tensor_reduce(mt, prob1[:, t, :, 0:w], AX.X, ALU.max))
                v(V.tensor_tensor(mt, mt, sinkrow[:, :], ALU.max))
                v(V.tensor_tensor(sm[:, 8 * t:8 * t + 8], sinkrow[:, :], mt, ALU.subtract))
                v(V.tensor_tensor(prob1[:, t, :, 0:w], prob1[:, t, :, 0:w], rep_(mt, 2, [P, HEADS, w]), ALU.subtract), "p1_shift")
            for t in range(NT):
                w = P * (t + 1)
                mt = m[:, 8 * t:8 * t + 8]
                dve.wait_ge(ev("p1_exp"), t + 1)
                v(V.tensor_reduce(mt, prob1[:, t, :, 0:w], AX.X, ALU.add))
                v(V.tensor_tensor(mt, mt, es[:, 8 * t:8 * t + 8], ALU.add))
                v(V.reciprocal(mt, mt))
                v(V.tensor_tensor(prob1[:, t, :, 0:w], prob1[:, t, :, 0:w], rep_(mt, 2, [P, HEADS, w]), ALU.mult), "p1_ready")
            ps = full(dve, "mod")
            for q in range(4):
                j = (0, 1, 3, 4)[q]
                ins = V.tensor_tensor(mod[:, 8 * j:8 * j + 8, :], ps[:, 16 * q:16 * q + 16].rearrange("p (k j) -> p k j", j=2),
                                      rep_(colsC[:, 8 * j:8 * j + 8], 2, [P, 8, 2]), ALU.add)
                if q < 3:
                    v(ins)
                else:
                    last(ins, "mod")
            for r, (c, j, g) in enumerate(((8, 0, 20), (8, 1, 20), (32, 0, 28))):
                v(V.scalar_tensor_tensor(modsc[:, r, :], mod[:, c:c + 8, j], 1.0, colsA[:, g:g + 8], ALU.add, ALU.mult),
                  "modsc_ready" if r == 2 else None)

            def merge(tag):
                for j in range(8):
                    br, i = j // 4, j % 4
                    emptied(dve, f"{tag}g{br}{i}")
                    ps = full(dve, f"{tag}o{br}{i}")
                    dst = mergedT[:, 2 * i:2 * i + 2, :].rearrange("p c t -> p (c t)")
                    if br == 0:
                        last(V.tensor_tensor(dst, sgate[tag][:, j % 2, :], ps, ALU.mult), f"{tag}o{br}{i}")
                    else:
                        last(V.tensor_tensor(mtmp[tag][:, j % 2, :], sgate[tag][:, j % 2, :], ps, ALU.mult), f"{tag}o{br}{i}")
                        v(V.tensor_tensor(dst, dst, mtmp[tag][:, j % 2, :], ALU.add), f"{tag}merged" if i == 3 else None)

            merge("a")
            for t in range(NT):
                for n in range(2):
                    r = resid[:, t, n * 512:(n + 1) * 512]
                    last(V.tensor_tensor(r, r, full(dve, f"ax{t}{n}"), ALU.add), f"ax{t}{n}")
                v(V.tensor_copy(stat("dummy", 1), epscol[:, 0:1]), "ah_ready")

            norm_rows("rn", resid, "rn_ready")
            for t in range(NT):
                dve.wait_ge(ev("cx_sd"), t + 1)
                v(V.reciprocal(stat("cx_r")[:, t:t + 1], stat("cx_sd")[:, t:t + 1]))
                v(V.tensor_scalar(ctxr[:, t, :], ctxr[:, t, :], stat("cx_r")[:, t:t + 1], None, ALU.mult), "ctxn_ready")
            lg = rt[:, 72:144].rearrange("p (t e) -> p t e", t=NT)
            ps = full(dve, "route")
            last(V.tensor_tensor(lg, ps[:, 0:128].rearrange("p (t e) -> p t e", t=NT)[:, :, 0:36], rep_(rbias[:, :], 1, [P, NT, 36]), ALU.add), "route")
            g8 = rt[:, 0:16].rearrange("p (t e) -> p t e", t=NT)
            gm = rt[:, 16:32]
            gi = rt[:, 32:48].bitcast(U32)
            gf = stat("gf")
            og = rt[:, 64:72].rearrange("p (t e) -> p t e", t=NT)
            v(V.memset(g8, -3.0e38))
            v(V.tensor_copy(g8[:, :, 0:GROUPS], lg[:, :, 0:GROUPS]))
            for t in range(NT):
                v(V.max(gm[:, 8 * t:8 * t + 8], g8[:, t, :]))
                v(V.max_index(gi[:, 8 * t:8 * t + 8], gm[:, 8 * t:8 * t + 8], g8[:, t, :]))
                v(V.tensor_copy(gf[:, t:t + 1], gi[:, 8 * t:8 * t + 1]))
                v(V.tensor_scalar(og[:, t, :], iota[:, 0:GROUPS], gf[:, t:t + 1], None, ALU.is_equal))
                v(V.tensor_scalar(stat("rt_ng")[:, t:t + 1], gm[:, 8 * t:8 * t + 1], -1.0, None, ALU.mult), "rt_gmax" if t else None)
            em = rt[:, 144:160]
            e8 = rt[:, 160:176].rearrange("p (t e) -> p t e", t=NT)
            ei = rt[:, 176:192].bitcast(U32)
            ef = stat("ef", 4)
            tmp = rt[:, 192:224].rearrange("p (g e) -> p g e", g=GROUPS)
            for t in range(NT):
                el = lg[:, t, GROUPS:].rearrange("p (g e) -> p g e", g=GROUPS)
                v(V.tensor_tensor(tmp, el, rep_(og[:, t, :], 2, [P, GROUPS, PER_GROUP]), ALU.mult))
                v(V.tensor_reduce(e8[:, t, :], rt[:, 192:224].rearrange("p (g e) -> p e g", g=GROUPS), AX.X, ALU.add))
                v(V.max(em[:, 8 * t:8 * t + 8], e8[:, t, :]))
                v(V.max_index(ei[:, 8 * t:8 * t + 8], em[:, 8 * t:8 * t + 8], e8[:, t, :]))
                v(V.tensor_copy(ef[:, 2 * t:2 * t + 2], ei[:, 8 * t:8 * t + 2]))
                v(V.tensor_scalar(stat("rt_nv")[:, t:t + 1], em[:, 8 * t:8 * t + 1], -1.0, None, ALU.mult), "rt_top" if t else None)
            oh = rt[:, 256:384].rearrange("p (j e) -> p j e", j=4)
            asg = arena2[:, 512:576].rearrange("p (t e) -> p t e", t=NT)
            for t in range(NT):
                for k in range(2):
                    j = 2 * t + k
                    v(V.scalar_tensor_tensor(ef[:, j:j + 1], gf[:, t:t + 1], float(PER_GROUP), ef[:, j:j + 1], ALU.mult, ALU.add))
                    v(V.tensor_scalar(oh[:, j, :], iota[:, :], ef[:, j:j + 1], None, ALU.is_equal))
                v(V.tensor_tensor(asg[:, t, :], oh[:, 2 * t, :], oh[:, 2 * t + 1, :], ALU.add), "assign_ready" if t else None)
            dve.wait_ge(ev("rt_gsum"), 2)
            dve.wait_ge(ev("rt_e1"), 2)
            pk = picks[:, :].rearrange("p (t k) -> p t k", k=2)
            wa_, wb_ = stat("wa_"), stat("wb_")
            v(V.tensor_scalar(wa_, stat("rt_e1"), 1.0, None, ALU.add))
            v(V.tensor_tensor(wa_, wa_, stat("rt_gs"), ALU.mult))
            v(V.reciprocal(wb_, wa_))
            v(V.tensor_copy(pk[:, :, 0], wb_))
            v(V.tensor_tensor(pk[:, :, 1], wb_, stat("rt_e1"), ALU.mult))
            posb = rt[:, 384:480]
            last(V.tensor_copy(posb, full(dve, "pos")[:, 0:96]), "pos")
            cnt = posb[:, 64:96]
            sums = rt[:, 640:896].rearrange("p (r n) -> p r n", r=2)
            ext, ext0 = sums[:, 0, 32:64], rt[:, 896:928]
            v(V.memset(rt[:, 640:896], 0.0))
            v(V.tensor_scalar(ext, cnt, float(CAP), None, ALU.is_gt))
            for r in range(2, BLOCKS):
                v(V.scalar_tensor_tensor(ext, cnt, float(CAP * r), ext, ALU.is_gt, ALU.add))
            v(V.tensor_copy(ext0, ext))
            side, d = 0, 1
            while d < EXPERTS:
                v(V.tensor_tensor(sums[:, 1 - side, 32:64], sums[:, side, 32:64], sums[:, side, 32 - d:64 - d], ALU.add))
                side, d = 1 - side, 2 * d
            upto = sums[:, side, 32:64]
            v(V.tensor_tensor(ext0, upto, ext0, ALU.subtract))
            pc, pp, po, pg = stat("pc", 4), stat("pp", 4), stat("po", 4), stat("pg", 4)
            for j in range(4):
                t = j // 2
                for row, dst in ((posb[:, 32 * t:32 * t + 32], pc), (ext0, po)):
                    v(V.tensor_tensor(rt[:, 480:512], oh[:, j, :], row, ALU.mult))
                    v(V.tensor_reduce(dst[:, j:j + 1], rt[:, 480:512], AX.X, ALU.add))
            v(V.tensor_scalar(pp, pc, float(CAP), None, ALU.is_ge))
            for r in range(2, BLOCKS):
                v(V.scalar_tensor_tensor(pp, pc, float(CAP * r), pp, ALU.is_ge, ALU.add))
            v(V.scalar_tensor_tensor(pc, pp, -float(CAP), pc, ALU.mult, ALU.add))
            v(V.tensor_scalar(pg, pp, 1.0, None, ALU.is_ge))
            v(V.scalar_tensor_tensor(po, po, float(EXPERTS - 1), pp, ALU.add, ALU.add))
            v(V.tensor_tensor(po, po, ef, ALU.subtract))
            v(V.tensor_tensor(po, po, pg, ALU.mult))
            v(V.tensor_tensor(po, po, ef, ALU.add))
            v(V.scalar_tensor_tensor(slotf[:, :], po, float(CAP), pc, ALU.mult, ALU.add))
            v(V.tensor_copy(sloti[:, :], slotf[:, :]))
            xe = rt[:, 928:1024]
            big = arena2[:, 1024:1280].rearrange("p (x e) -> p x e", x=EXTRA)
            v(V.tensor_tensor(big, rep_(iota[:, 0:EXTRA], 2, [P, EXTRA, EXPERTS]), rep_(upto, 1, [P, EXTRA, EXPERTS]), ALU.is_ge))
            v(V.tensor_copy(xe[:, 0:EXPERTS], iota[:, :]))
            v(V.tensor_reduce(xe[:, EXPERTS:EXPERTS + EXTRA], big, AX.X, ALU.add))
            v(V.tensor_scalar(xe[:, EXPERTS:EXPERTS + EXTRA], xe[:, EXPERTS:EXPERTS + EXTRA], float(EXPERTS - 1), None, ALU.min))
            v(V.tensor_copy(elist[:, :], xe[0:1, 0:EXPERTS + EXTRA]))
            np_ = stat("np", 1)
            v(V.tensor_scalar(np_, upto[:, EXPERTS - 1:EXPERTS], 0.0, float(STEPS), ALU.is_gt, ALU.add))
            for r in range(2, EXTRA, 2):
                v(V.scalar_tensor_tensor(np_, upto[:, EXPERTS - 1:EXPERTS], float(r), np_, ALU.is_gt, ALU.add))
            v(V.tensor_copy(trips[:, :], np_[0:1, :]), "trips_ready")

            kk = kvt[:, 0:512].rearrange("p (t c) -> p t c", c=T)[:, :, 0:P]
            sqc = arena1[:, 3600:3856].rearrange("p (t c) -> p t c", t=NT)
            for t in range(NT):
                ps = full(dve, f"ckv{t}")
                v(V.tensor_copy(kvt[:, t * T:t * T + P], ps[:, 0:P]))
                last(V.tensor_copy(vtok[:, 2 + t, :], ps[:, P:2 * P]), f"ckv{t}")
            v(V.tensor_tensor(sqc, kk, kk, ALU.mult))
            v(V.tensor_reduce(stat("ck_ss", 4), arena1[:, 3600:3856].rearrange("p (a d) -> p a d", d=HD), AX.X, ALU.add), "ck_ss")
            dve.wait_ge(ev("ck_sd"), 1)
            v(V.reciprocal(stat("ck_r", 4), stat("ck_sd", 4)))
            for t in range(NT):
                k3 = kvt[:, t * T:t * T + P].rearrange("p (h d) -> p h d", h=KV)
                v(V.tensor_tensor(k3, k3, rep_(stat("ck_r", 4)[:, 2 * t:2 * t + 2], 2, [P, KV, HD]), ALU.mult))
                v(V.tensor_tensor(k3, k3, rep_(qkg[:, 1, :], 1, [P, KV, HD]), ALU.mult), "ck_ready" if t else None)

            dve.wait_ge(ev("zeroed"), 16 * ZEROED)
            keys_dup("ckT", T)

            n_iter = dve.value_load(trips[0:1, 0:1], min_val=STEPS, max_val=MAXSTEPS)
            dve.sem_inc(ev("down_read1"), 1)

            def rows_out(h, n):
                dve.wait_ge(ev(f"rowsT_full{h}"), n)
                V.tensor_tensor(xT[:, h, :, :], psum[:, 0, :].rearrange("p (k c) -> p k c", k=KD),
                                rep_(colsA[:, 36:44], 2, [P, KD, CAP]), ALU.mult).then_inc(ev(f"rowsT_ready{h}"), 1)

            rows_out(0, 1)
            with dve.Fori(0, n_iter) as i:
                rows_out(1, i + 2)
                for h in range(2):
                    dve.wait_ge(ev(f"silu_ready{h}"), i + 1)
                    dve.wait_ge(ev(f"up_full{h}"), i + 1)
                    V.tensor_tensor(hrow[:, h, :], silu[:, h, :], psum[0:CAP, 3 + 2 * h, :], ALU.mult).then_inc(ev(f"hid_ready{h}"), 1)
                for h in range(2):
                    dve.wait_ge(ev("down_full1"), 2 * i + h + 2)
                    dve.wait_ge(ev(f"stored{h}"), 16 * i + 1)
                    V.tensor_copy(yrow[:, h, 512:1024], psum[0:CAP, 7, :]).then_inc(ev("down_read1"), 1)
                    if h == 0:
                        rows_out(0, i + 2)

            for j in range(4):
                dve.wait_ge(ev("fetched"), 16 * 4)
                r = resid[:, j // 2, :]
                v(V.scalar_tensor_tensor(r, back[:, j, :], picks[:, j:j + 1], r, ALU.mult, ALU.add), "moe_added" if j % 2 else None)
            dve.wait_ge(ev("gf_in"), 16)
            norm_rows("fn", resid, "x2_ready", gfrow)

            norm_rows("zn", resid, "zn_ready")
            v(V.memset(hpad[:, :, :, 0:1], 0.0))
            v(V.memset(hpad[:, :, :, T + 1:T + 2], 0.0), "pads_zero")
            for t in range(NT):
                ps = full(dve, f"kv{t}")
                v(V.tensor_copy(ktok[:, t, :], ps[:, 0:P]))
                last(V.tensor_copy(vtok[:, t, :], ps[:, P:2 * P]), f"kv{t}")
            for t in range(NT):
                emptied(dve, f"q{t}")
            ss = stat("qk_ss", 20)
            v(V.tensor_tensor(sq, qtok, qtok, ALU.mult))
            v(V.tensor_reduce(ss[:, 0:16], arena2[:, 1280:2304].rearrange("p (a d) -> p a d", d=HD), AX.X, ALU.add))
            v(V.tensor_tensor(arena2[:, 1280:1536], arena2[:, 1024:1280], arena2[:, 1024:1280], ALU.mult))
            v(V.tensor_reduce(ss[:, 16:20], arena2[:, 1280:1536].rearrange("p (a d) -> p a d", d=HD), AX.X, ALU.add), "qk_ss")
            dve.wait_ge(ev("qk_sd"), 1)
            v(V.reciprocal(stat("qk_r", 20), stat("qk_sd", 20)))
            for rows_, heads, r0, gi_ in ((qtok, HEADS, 0, 0), (ktok, KV, 16, 1)):
                for t in range(NT):
                    x3 = rows_[:, t, :].rearrange("p (h d) -> p h d", h=heads)
                    v(V.tensor_tensor(x3, x3, rep_(stat("qk_r", 20)[:, r0 + heads * t:r0 + heads * (t + 1)], 2, [P, heads, HD]), ALU.mult))
                    v(V.tensor_tensor(x3, x3, rep_(qkg[:, gi_, :], 1, [P, heads, HD]), ALU.mult))
                    x5 = rows_[:, t, :].rearrange("p (h a s j) -> p h a s j", a=2, s=2, j=16)
                    r5 = rtmp[:, t, 0:heads * HD].rearrange("p (h a s j) -> p h a s j", a=2, s=2, j=16)
                    s4 = rope[:, 1, t, :].rearrange("p (a s j) -> p a s j", a=2, s=2)
                    for half in range(2):
                        v(V.tensor_tensor(r5[:, :, :, half, :], x5[:, :, :, 1 - half, :],
                                          rep_(s4[:, :, half, :], 1, [P, heads, 2, 16]), ALU.mult))
                    v(V.tensor_tensor(x3, x3, rep_(rope[:, 0, t, :], 1, [P, heads, HD]), ALU.mult))
                    x2 = rows_[:, t, :]
                    fin = rows_ is ktok and t == NT - 1
                    v(V.tensor_tensor(x2, x2, rtmp[:, t, 0:heads * HD], ALU.add), "qk2_ready" if fin else None)
            for j in range(6):
                emptied(dve, f"hy{j // 2}{j % 2}")
                for c in range(2):
                    k = 2 * j + c
                    x = hpad[:, j % 2, c, :]
                    v(V.tensor_scalar(zs[:, k, :], x[:, 0:T], colsA[:, 44 + k:45 + k], colsA[:, 80 + k:81 + k], ALU.mult, ALU.add))
                    v(V.scalar_tensor_tensor(zs[:, k, :], x[:, 1:T + 1], colsA[:, 56 + k:57 + k], zs[:, k, :], ALU.mult, ALU.add))
                    v(V.scalar_tensor_tensor(zs[:, k, :], x[:, 2:T + 2], colsA[:, 68 + k:69 + k], zs[:, k, :], ALU.mult, ALU.add),
                      "short_done" if c else None)
            v(V.tensor_copy(stat("dummy", 1), epscol[:, 0:1]), "short_ready")
            keys_dup("kT", 0)
            v(V.tensor_copy(stat("dummy", 1), epscol[:, 0:1]), "k2_ready")

            def unit_max(u):
                v(V.tensor_reduce(stat("m2", 16)[:, u:u + 1], full(dve, f"sc{u}"), AX.X, ALU.max))
                v(V.tensor_scalar(stat("nm2", 16)[:, u:u + 1], stat("m2", 16)[:, u:u + 1], -HD ** -0.5, None, ALU.mult), "nmax")

            half_ = lambda ap: ap.rearrange("p k c -> p (k c)")
            Uc, Us = half_(Usb[:, 0:2, :]), half_(Usb[:, 2:4, :])

            def hy_product(o, part):
                for p_ in range(2):
                    for f in range(NT):
                        emptied(dve, f"U{o}{p_}{f}")
                Kc, Ks = half_(spec[:, o, 0, :, :]), half_(spec[:, o, 1, :, :])
                y = half_(Y[:, 2 * part:2 * part + 2, :])
                v(V.tensor_tensor(y, Uc, (Kc, Ks)[part], ALU.mult))
                v(V.tensor_tensor(prod, Us, (Ks, Kc)[part], ALU.mult))
                v(V.tensor_tensor(y, y, prod, (ALU.subtract, ALU.add)[part]), "Y_ready" if part else None)

            def hy_gate(o, g):
                src = (zs[:, 0:4, :], y1T)[o]
                gate = (zs[:, 4:8, :], zs[:, 8:12, :])[o]
                ps = full(dve, f"I{o}{g}")
                for c in range(2):
                    k = 2 * g + c
                    ins = V.scalar_tensor_tensor(prod[:, k * T:(k + 1) * T], src[:, k, :], colsA[:, 92 + 4 * o + k:93 + 4 * o + k],
                                                 ps[:, c * T:(c + 1) * T], ALU.mult, ALU.add)
                    if c:
                        last(ins, f"I{o}{g}")
                    else:
                        v(ins)
                if g:
                    v(V.tensor_tensor(gate.rearrange("p c t -> p (c t)"), gate.rearrange("p c t -> p (c t)"), prod, ALU.mult),
                      ("y1_ready", "hy_ready")[o])

            hy_parts = {3: (hy_product, 0, 0), 4: (hy_product, 0, 1), 7: (hy_gate, 0, 0), 8: (hy_gate, 0, 1),
                        12: (hy_product, 1, 0), 13: (hy_product, 1, 1)}
            unit_max(0)
            for u in range(16):
                if u + 1 < 16:
                    unit_max(u + 1)
                emptied(dve, f"sc{u}")
                v(V.reciprocal(stat("m2", 16)[:, u:u + 1], stat("sum2", 16)[:, u:u + 1]))
                v(V.tensor_scalar(prob2[:, u % 4, :], prob2[:, u % 4, :], stat("m2", 16)[:, u:u + 1], None, ALU.mult), "p2_ready")
                if u in hy_parts:
                    hy_parts[u][0](*hy_parts[u][1:])
            hy_gate(1, 0)
            hy_gate(1, 1)
            dve.wait_ge(ev("grow_sent"), 16)
            merge("b")
            dve.wait_ge(ev("g1_in"), 16)
            for t in range(NT):
                for n in range(2):
                    r = resid[:, t, n * 512:(n + 1) * 512]
                    last(V.tensor_tensor(scratch[:, t, 0:512], g1row[:, n * 512:(n + 1) * 512], full(dve, f"bx{t}{n}"), ALU.mult), f"bx{t}{n}")
                    v(V.tensor_tensor(r, r, scratch[:, t, 0:512], ALU.add), "bh_ready" if n else None)
            norm_rows("pn", resid, "pn_ready")
            def top16(chains):
                for r in range(2):
                    for vals, idx, src in chains:
                        v_pair(V.max(vals[:, 8 * r:8 * r + 8], src))
                    for vals, idx, src in chains:
                        v_pair(V.max_index(idx[:, 8 * r:8 * r + 8], vals[:, 8 * r:8 * r + 8], src))
                    if r == 0:
                        for vals, idx, src in chains:
                            v_pair(V.match_replace(src, vals[:, 0:8], src, -3.0e38))

            def best_of(t, g):
                emptied(dve, f"ks{t}{g}")
                for h in (2 * g, 2 * g + 1):
                    top16([(top_v[:, t, c, :], top_i[:, t, c, :], S[:, t, c, :]) for c in (2 * h, 2 * h + 1)])
                v_done()
                sums = [(best[:, t, h, :], where[:, t, h * PTOP:(h + 1) * PTOP], cand[:, h * 256:(h + 1) * 256]) for h in (2 * g, 2 * g + 1)]
                for h, (_, _, c) in zip((2 * g, 2 * g + 1), sums):
                    v_pair(V.tensor_tensor(c.rearrange("p (a b) -> p a b", a=PTOP), rep_(top_v[:, t, 2 * h, :], 2, [P, PTOP, PTOP]),
                                           rep_(top_v[:, t, 2 * h + 1, :], 1, [P, PTOP, PTOP]), ALU.add))
                top16(sums)
                v_done()

            def rows_of_table(t):
                v(V.tensor_copy(top_f[:, t, :, :], top_i[:, t, :, :]))
                g3 = gates[:, t, :].rearrange("p (h k) -> p h k", k=PTOP)
                v(V.tensor_tensor(g3, best[:, t, :, :], best[:, t, :, 0:1].to_broadcast([P, PH, PTOP]), ALU.subtract), "best_shift")
                dve.wait_ge(ev("best_exp"), t + 1)
                v(V.tensor_reduce(stat("gsum", 8), g3, AX.X, ALU.add))
                v(V.reciprocal(stat("gsum", 8), stat("gsum", 8)))
                v(V.tensor_tensor(g3, g3, rep_(stat("gsum", 8), 2, [P, PH, PTOP]), ALU.mult))
                oh4 = cand.rearrange("p (h k a) -> p h k a", h=PH, k=PTOP)
                for half, (op, arg) in enumerate(((ALU.logical_shift_right, 4), (ALU.bitwise_and, 15))):
                    v(V.tensor_scalar(wi[:, t, :], where[:, t, :], arg, None, op))
                    v(V.tensor_copy(wf[:, t, :], wi[:, t, :]))
                    v(V.tensor_tensor(cand.rearrange("p (n a) -> p n a", a=PTOP), rep_(wf[:, t, :], 2, [P, PICKS, PTOP]),
                                      rep_(iota[:, 0:PTOP], 1, [P, PICKS, PTOP]), ALU.is_equal))
                    tf = top_f[:, t, :, :].rearrange("p (h s) k -> p h s k", s=2)[:, :, half, :]
                    v(V.tensor_tensor(oh4, oh4, rep_(tf, 2, [P, PH, PTOP, PTOP]), ALU.mult))
                    dst = rowf[:, t, :] if half == 0 else wf[:, t, :]
                    v(V.tensor_reduce(dst, cand.rearrange("p (n a) -> p n a", a=PTOP), AX.X, ALU.add))
                v(V.scalar_tensor_tensor(rowf[:, t, :], rowf[:, t, :], float(PKEYS), wf[:, t, :], ALU.mult, ALU.add))
                v(V.tensor_copy(rowid[:, t, :], rowf[:, t, :]), "rowid_ready")

            per = PICKS // ROWBUFS

            def row_dots(t, i0, i1):
                with dve.Fori(i0, i1) as i:
                    for b in range(ROWBUFS):
                        dve.wait_ge(ev(f"row_in{b}"), (i + (t * per + 1)) * 16)
                        V.tensor_tensor_reduce(dotjunk[:, b % 2, :], rows[:, b, :], tok2[:, t, :], 1.0, 0.0, ALU.mult, ALU.add,
                                               dotcols[:, b:b + 1]).then_inc(ev("row_used"), 1)
                        dve.wait_ge(ev("row_used"), (i + t * per) * ROWBUFS + (ROWBUFS + b))
                    dve.wait_ge(ev("row_used"), (i + t * per) * ROWBUFS + 2 * ROWBUFS)
                    V.tensor_copy(dots[:, t, bass.ds(i * ROWBUFS, ROWBUFS)], dotcols[:, :]).then_inc(ev("dots_kept"), 1)
                    dve.wait_ge(ev("dots_kept"), i + (t * per + 1))

            for g in range(4):
                best_of(0, g)
            dve.sem_inc(ev("row_used"), ROWBUFS)
            rows_of_table(0)
            for t in range(NT):
                for n in range(2):
                    emptied(dve, f"xp{t}{n}")
            for g in range(4):
                best_of(1, g)
                row_dots(0, g * per // 5, (g + 1) * per // 5)
            rows_of_table(1)
            row_dots(0, 4 * per // 5, per)
            v(V.tensor_copy(stat("dummy", 1), epscol[:, 0:1]), "dots_ready")
            row_dots(1, 0, per)
            v(V.tensor_copy(stat("dummy", 1), epscol[:, 0:1]), "dots_ready")
            for t in range(NT):
                dve.wait_ge(ev("gelu_done"), t + 1)
                v(V.tensor_tensor(gates[:, t, :], gates[:, t, :], dots[:, t, :], ALU.mult))
                v(V.memset(scratch[:, t, :], 0.0))
            for t in range(NT):
                with dve.Fori(0, per) as i:
                    for b in range(ROWBUFS):
                        dve.wait_ge(ev(f"row_in{b}"), (i + ((NT + t) * per + 1)) * 16)
                        V.scalar_tensor_tensor(scratch[:, t, :], rows[:, b, :], gates[:, t, bass.ds(i * ROWBUFS + b, 1)], scratch[:, t, :],
                                               ALU.mult, ALU.add).then_inc(ev("row_used"), 1)
                        dve.wait_ge(ev("row_used"), (i + (NT + t) * per) * ROWBUFS + (ROWBUFS + b + 1))
                dve.wait_ge(ev("g2_in"), 32)
                v(V.tensor_tensor(scratch[:, t, :], scratch[:, t, :], g2row, ALU.mult))
                v(V.tensor_tensor(resid[:, t, :], resid[:, t, :], scratch[:, t, :], ALU.add), "x3_ready")
            for t in range(NT):
                dve.wait_ge(ev("ff_sd"), t + 1)
                v(V.reciprocal(stat("ff_r")[:, t:t + 1], stat("ff_sd")[:, t:t + 1]))
                v(V.scalar_tensor_tensor(resid[:, t, :], resid[:, t, :], stat("ff_r")[:, t:t + 1], flrow, ALU.mult, ALU.mult), "final_ready")


_INS = ['x', 'g_mix', 'w_in', 'w_dw', 'b_dw', 'ln_conv_g', 'ln_conv_b', 'sinks', 'w_conv_out', 'w_attn_out', 'w_out', 'g_ffn',
        'w_group', 'b_group', 'w_expert', 'b_expert', 'w_gate', 'w_up', 'w_down', 'g_final', 'c_2', 'ctx_2', 'c_ctx_2',
        'ada_w_2', 'ada_b_2', 'norm_mix_g_2', 'norm_ffn_g_2', 'w_in_2', 'q_norm_g_2', 'k_norm_g_2', 'hy_conv_w_2',
        'hy_conv_b_2', 'hf_w1_2', 'hf_b1_2', 'hf_w2_2', 'hf_b2_2', 'hf_w3_2', 'hf_b3_2', 'hf_w4_2', 'hf_freq_2', 'hy_skip_2',
        'w_attn_out_2', 'w_hy_out_2', 'w_out_2', 'peer_wq_2', 'peer_keys1_2', 'peer_keys2_2', 'peer_u_2', 'peer_v_2',
        'final_norm_g_2']


def kernel(**inputs):
    import numpy as _np
    import concourse.bacc as _bacc
    from concourse import mybir as _mybir
    from concourse.bass_utils import run_bass_kernel_spmd as _run

    nc = _bacc.Bacc("TRN2", target_bir_lowering=False, num_devices=1)
    arrays, aps = {}, {}
    named = {n: _np.ascontiguousarray(inputs[n]) for n in _INS}
    named.update(shape_constants())
    for name, a in named.items():
        arrays[f"in_{name}_dram"] = a
        aps[name] = nc.dram_tensor(f"in_{name}_dram", a.shape, _mybir.dt.from_np(a.dtype), kind="ExternalInput").ap()
    out = nc.dram_tensor("out_0_dram", (1, T, D), F32, kind="ExternalOutput").ap()
    build(nc, aps, out)
    r = _run(nc, [arrays], core_ids=[0])
    return r.results[0]["out_0_dram"]
```

```python
from contextlib import ExitStack

import numpy as np
import concourse.bass as bass
from concourse import mybir

P = 128
F32 = mybir.dt.float32
I32 = mybir.dt.int32
U32 = mybir.dt.uint32
ALU = mybir.AluOpType
ACT = mybir.ActivationFunctionType
AX = mybir.AxisListType

T = 256
NT = T // P
D = 1024
KD = D // P
CH = 512
KC = CH // P
TAPS = 31
HEADS, KV, HD = 8, 2, 64
EXPERTS, GROUPS, PER_GROUP = 32, 4, 8
FF = 512
CAP = 64
BLOCKS = T // CAP
EXTRA = 2 * T // CAP
BOTH = 2 * CAP
SLOTS = 6
PIECE = 4096
STEPS = EXPERTS // 2
MAXSTEPS = (EXPERTS + EXTRA) // 2
ROWS = (EXPERTS + EXTRA) * CAP
PH, PKEYS, PTOP = 8, 128, 16
PICKS = PH * PTOP
ROWBUFS = 16
EPS = 1e-6
SLOPES = [2.0 ** (-8.0 * (h + 1) / HEADS) for h in range(HEADS)]
MASKED = 1.0e30


def shape_constants():
    c = {}
    c["c_ident"] = np.eye(P, dtype=np.float32)
    c["c_before"] = np.triu(np.ones((P, P), np.float32), 1)
    q = np.arange(P)[:, None]
    k = np.arange(2 * P)[None, :]
    rel = P + q - k
    c["c_rel"] = np.where((rel >= 0) & (rel < P), rel, MASKED).astype(np.float32)
    t = np.arange(T, dtype=np.float64)
    theta = 2 * np.pi * (t + 0.5) / (2 * T)
    ang = t[:, None] * theta[None, :]
    cs = np.stack([np.cos(ang), np.sin(ang)])
    c["c_dft"] = cs.reshape(2, NT, P, T).transpose(2, 0, 1, 3).astype(np.float32).copy()
    inv = (np.stack([np.cos(ang).T, np.sin(ang).T]) / T)
    c["c_idft"] = inv.reshape(2 * NT, P, T).transpose(1, 0, 2).astype(np.float32).copy()
    row, col = np.arange(T) // 64, np.arange(T) % 64
    f = (10000.0 ** (-np.arange(0, 32, 2) / 32)).astype(np.float32)
    ar, ac = row[:, None].astype(np.float32) * f, col[:, None].astype(np.float32) * f
    a = np.concatenate([ar, ar, ac, ac], -1)
    sign = np.tile(np.concatenate([-np.ones(16), np.ones(16)]), 2)
    c["c_rope"] = np.stack([np.cos(a), np.sin(a) * sign]).reshape(2, NT, P, HD).transpose(2, 0, 1, 3).astype(np.float32).copy()
    t01 = np.linspace(0.0, 1.0, T, dtype=np.float32)[:, None]
    w = (2.0 * np.pi * np.arange(T, dtype=np.float32)[:, None] / T).astype(np.float32)
    fr = np.linspace(1e-4, 15, 16, dtype=np.float32)[None]
    z = np.concatenate([t01, np.cos(fr * w), -np.sin(fr * w)], -1)
    c["c_feat"] = z.T.astype(np.float32).copy()
    deltas = np.abs(np.linspace(np.log(1e-2) / 1.5, np.log(1e-2) / 0.3, CH, dtype=np.float32))
    decay = np.exp(-t01 * deltas)
    back = decay.copy()
    back[0] = 0.0
    c["c_decay"] = np.stack([decay, back]).reshape(2, NT, P, CH).transpose(2, 1, 0, 3).astype(np.float32).copy()
    c["c_iota"] = np.tile(np.arange(EXPERTS, dtype=np.float32), (P, 1))
    return c


def build(nc, A, out):
    ctx = ExitStack()
    with ctx:
        def sb(name, shape, dt=F32):
            return ctx.enter_context(nc.sbuf_tensor(name, shape, dt))

        def sem(name):
            return ctx.enter_context(nc.semaphore(name))

        psum = ctx.enter_context(nc.psum_tensor("psum", [P, 8, 512], F32))
        ring = sb("ring", [P, SLOTS, PIECE])
        resid = sb("resid", [P, NT, D])
        scratch = sb("scratch", [P, NT, D])
        tok2 = sb("tok2", [P, NT, D])
        actT = sb("actT", [P, KD, T])
        spec = sb("spec", [P, 2, 2, NT, CH])
        dft = sb("dft", [P, 2, NT, T])
        idft = sb("idft", [P, 2 * NT, T])
        arena1 = sb("arena1", [P, 4224])
        arena2 = sb("arena2", [P, 4096])
        qT = sb("qT", [P, KC, T])
        kdup = sb("kdup", [P, KV, 2 * T])
        vtok = sb("vtok", [P, 2 * NT, KV * HD])
        attnT = sb("attnT", [P, KC, T])
        ident = sb("ident", [P, P])
        ones = sb("ones", [P, P])
        before = sb("before", [P, P])
        rel = sb("rel", [P, 2 * P])
        rope = sb("rope", [P, 2, NT, HD])
        iota = sb("iota", [P, EXPERTS])
        colsA = sb("colsA", [P, 104])
        colsB = sb("colsB", [P, 124])
        colsC = sb("colsC", [P, 48])
        colsD = sb("colsD", [64, 4])
        mod = sb("mod", [P, 6 * KD, 2])
        modsc = sb("modsc", [P, 3, KD])
        scT = sb("scT", [P, KD, 2])
        rbias = sb("rbias", [P, GROUPS + EXPERTS])
        sinkrow = sb("sinkrow", [P, HEADS])
        qkg = sb("qkg", [P, 2, HD])
        wroute = sb("wroute", [P, KD, GROUPS + EXPERTS])
        st = sb("st", [P, 400])
        epscol = sb("epscol", [P, 1])
        picks = sb("picks", [P, 4])
        slotf = sb("slotf", [P, 4])
        sloti = sb("sloti", [P, 4], I32)
        trips = sb("trips", [1, 1], I32)
        elist = sb("elist", [1, EXPERTS + EXTRA], I32)

        aT = arena1[:, 0:1024].rearrange("p (c t) -> p c t", c=KC)
        sgT = arena1[:, 1024:2048].rearrange("p (c t) -> p c t", c=KC)
        vpad = arena1[:, 2048:2048 + KC * (T + 30)].rearrange("p (c t) -> p c t", c=KC)
        yT = arena1[:, 3200:4224].rearrange("p (c t) -> p c t", c=KC)
        ytok = arena1[:, 0:1024].rearrange("p (a c) -> p a c", a=NT)
        yactT = arena1[:, 1024:2048].rearrange("p (c t) -> p c t", c=KC)
        prob1 = arena2[:, :].rearrange("p (t h k) -> p t h k", t=NT, h=HEADS)
        pTbuf = scratch[:, :, :].rearrange("p a (s c) -> p (a s) c", c=512)
        sgate = {"a": arena1[:, 3200:4224].rearrange("p (b c) -> p b c", b=2), "b": arena2[:, 0:1024].rearrange("p (b c) -> p b c", b=2)}
        mtmp = {"a": arena1[:, 0:1024].rearrange("p (b c) -> p b c", b=2), "b": arena2[:, 1024:2048].rearrange("p (b c) -> p b c", b=2)}
        normjunk = arena1[:, 0:2 * D].rearrange("p (a d) -> p a d", d=D)
        qjunk = qT[:, :, :].rearrange("p c t -> p (c t)").unsqueeze(1).to_broadcast([P, NT, D])
        mergedT = tok2[:, :, :].rearrange("p a (c t) -> p (a c) t", t=T)
        filt = spec[:, :, :, :, :].rearrange("p o m a c -> p a (o m) c")
        decay = tok2[:, :, :].rearrange("p a (m c) -> p a m c", m=2)
        fsmall = arena2[0:64, 0:2048].rearrange("p (a t) -> p a t", t=T)
        feat = arena2[0:33, 2048:2304]
        w1s = arena2[0:33, 2304:2368]
        w23 = arena2[0:64, 2368:2496].rearrange("p (a n) -> p a n", a=2)
        absb = arena2[:, 2560:3584].rearrange("p (a c) -> p a c", a=2)
        ctxr = arena2[:, 2048:4096].rearrange("p (a d) -> p a d", d=D)
        mrow = tok2[0:2, :, :].rearrange("p a (b n) -> p (a b) n", n=512)
        kvt = qT[:, :, :].rearrange("p c t -> p (c t)")

        kflat = kdup[:, :, :].rearrange("p a t -> p (a t)")
        prm = kflat[:, 0:384].rearrange("p (a t) -> p a t", t=P)
        prmD = kflat[0:4, 384:448]
        crow = kflat[0:16, 512:640]
        zeros = kdup[:, 0, T:2 * T]
        rt = arena2[:, 0:1024]
        xrow = scratch[0:BOTH, 0, :]
        yrow = tok2[0:BOTH, 0, :]
        xT = arena1[:, 0:KD * BOTH].rearrange("p (k c) -> p k c", k=KD)
        hidT = arena1[:, 1024:1024 + 4 * BOTH].rearrange("p (k c) -> p k c", k=4)
        silu = arena1[0:BOTH, 1536:2048]
        hrow = arena1[0:BOTH, 2048:2560]
        back = arena2[:, :].rearrange("p (a d) -> p a d", d=D)
        zs = arena1[:, 0:3072].rearrange("p (c t) -> p c t", t=T)
        y1T, hyoT = zs[:, 4:8, :], zs[:, 8:12, :]
        hpad = arena1[:, 3072:3072 + 4 * (T + 2)].rearrange("p (b c t) -> p b c t", b=2, c=2)
        qtok = arena2[:, 0:1024].rearrange("p (a c) -> p a c", a=NT)
        ktok = arena2[:, 1024:1280].rearrange("p (a c) -> p a c", a=NT)
        sq = arena2[:, 1280:2304].rearrange("p (a c) -> p a c", a=NT)
        rtmp = arena2[:, 2304:3328].rearrange("p (a c) -> p a c", a=NT)
        prob2 = arena2[:, 2048:4096].rearrange("p (u c) -> p u c", c=512)
        pT2 = scratch[:, 0, :].rearrange("p (u c) -> p u c", c=512)
        vtime = arena2[:, 0:1024].rearrange("p (a c) -> p a c", a=NT)
        Usb = ring[:, 5, 0:2048].rearrange("p (k c) -> p k c", c=CH)
        Y = ring[:, 5, 2048:4096].rearrange("p (k c) -> p k c", c=CH)
        prod = scratch[:, 1, :]
        g1row = kflat
        gbias = scratch[0:1, :, :].rearrange("p a (b n) -> p (a b) n", n=512)
        gfrow = attnT[:, :, :].rearrange("p c t -> p (c t)")
        pqT = arena2[:, :].rearrange("p (c t) -> p c t", t=T)
        keysT = spec[:, 0, :, :, :].rearrange("p a b c -> p (a b c)").rearrange("p (c n) -> p c n", n=P)
        cand = spec[:, 1, :, :, :].rearrange("p a b c -> p (a b c)")
        S = arena1[:, 0:4096].rearrange("p (t c n) -> p t c n", t=NT, n=P)
        qflat = qT[:, :, :].rearrange("p c t -> p (c t)")
        vflat = vtok[:, :, :].rearrange("p c t -> p (c t)")
        aflat = attnT[:, :, :].rearrange("p c t -> p (c t)")
        top_v = qflat[:, 0:512].rearrange("p (t c k) -> p t c k", t=NT, k=PTOP)
        top_i = qflat[:, 512:1024].bitcast(U32).rearrange("p (t c k) -> p t c k", t=NT, k=PTOP)
        top_f = kflat[:, 0:512].rearrange("p (t c k) -> p t c k", t=NT, k=PTOP)
        best = kflat[:, 512:768].rearrange("p (t h k) -> p t h k", t=NT, k=PTOP)
        where = kflat[:, 768:1024].bitcast(U32).rearrange("p (t n) -> p t n", t=NT)
        wi = vflat[:, 0:256].bitcast(U32).rearrange("p (t n) -> p t n", t=NT)
        wf = vflat[:, 256:512].rearrange("p (t n) -> p t n", t=NT)
        dots = aflat[:, 0:256].rearrange("p (t n) -> p t n", t=NT)
        gates = aflat[:, 256:512].rearrange("p (t n) -> p t n", t=NT)
        rowid = aflat[:, 512:768].bitcast(I32).rearrange("p (t n) -> p t n", t=NT)
        rowf = aflat[:, 768:1024].rearrange("p (t n) -> p t n", t=NT)
        rows = ring[:, 1:5, :].rearrange("p s (b d) -> p (s b) d", d=D)
        g2row, flrow = ring[:, 0, 0:D], ring[:, 0, D:2 * D]
        dotjunk = scratch
        cur = sb("cur", [P, ROWBUFS], I32)
        dotcols = sb("dotcols", [P, ROWBUFS])

        gate_rows = nc.dram_tensor("gate_rows", (1, 2 * D), F32, kind="Internal").ap()
        xs = nc.dram_tensor("moe_rows_in", (ROWS + P, D), F32, kind="Internal").ap()
        ys = nc.dram_tensor("moe_rows_out", (ROWS, D), F32, kind="Internal").ap()

        bank_full = [sem(f"bank_full{b}") for b in range(8)]
        bank_read = [sem(f"bank_read{b}") for b in range(8)]
        piece_in = [sem(f"piece_in{s}") for s in range(SLOTS)]
        piece2_in = [sem(f"piece2_in{s}") for s in range(SLOTS)]
        prm_in = sem("prm_in")
        const_in = sem("const_in")
        ctx_in = sem("ctx_in")
        grow_in = sem("grow_in")
        dec_in = sem("dec_in")
        act_step = sem("act_step")
        dve_step = sem("dve_step")
        pool_step = sem("pool_step")
        pe_step = sem("pe_step")
        events = {}

        def ev(name):
            if name not in events:
                events[name] = sem(name)
            return events[name]

        def kpiece(w, c0, n=512):
            return w[:, c0:c0 + n].rearrange("(k p) n -> p k n", p=P)

        w_in, w_in2, ada = A["w_in"][0], A["w_in_2"][0], A["ada_w_2"][0]
        pieces = [("wa", kpiece(w_in, 0)), ("wg", kpiece(w_in, CH)), ("filt4", A["hf_w4_2"][0]),
                  ("wq", kpiece(w_in, 2 * CH)), ("wkv", kpiece(w_in, 3 * CH, 2 * KV * HD))]
        mod_pairs = ((0, 1), (2, 3), (6, 7), (8, 9), (4, 5), (10, 11))
        COLUMN_PAIRS = 4
        for pair_ in mod_pairs:
            pieces += [(f"ada{j}", kpiece(ada, 512 * j)) for j in pair_]
        g0 = 3 * CH + 2 * KV * HD
        pieces += [("o0", A["w_conv_out"][0].rearrange("(k p) n -> p k n", p=P)),
                   ("g00", kpiece(w_in, g0)), ("g01", kpiece(w_in, g0 + 512)),
                   ("o1", A["w_attn_out"][0].rearrange("(k p) n -> p k n", p=P)),
                   ("g10", kpiece(w_in, g0 + D)), ("g11", kpiece(w_in, g0 + D + 512)),
                   ("wo0", kpiece(A["w_out"][0], 0)), ("wo1", kpiece(A["w_out"][0], 512)),
                   ("ctxkv", kpiece(w_in2, CH, 2 * KV * HD))]
        place1 = {n: (i % SLOTS, i // SLOTS + 1) for i, (n, _) in enumerate(pieces)}
        base_use = [len([1 for i in range(len(pieces)) if i % SLOTS == s]) for s in range(SLOTS)]
        h0 = CH + 2 * KV * HD
        g2 = h0 + 3 * CH
        pieces2 = [("q", kpiece(w_in2, 0)), ("kv", kpiece(w_in2, CH, 2 * KV * HD)),
                   ("hy0", kpiece(w_in2, h0)), ("hy1", kpiece(w_in2, h0 + CH)), ("hy2", kpiece(w_in2, h0 + 2 * CH)),
                   ("room", None),
                   ("o0", A["w_attn_out_2"][0].rearrange("(k p) n -> p k n", p=P)),
                   ("g00", kpiece(w_in2, g2)), ("g01", kpiece(w_in2, g2 + 512)),
                   ("o1", A["w_hy_out_2"][0].rearrange("(k p) n -> p k n", p=P)),
                   ("g10", kpiece(w_in2, g2 + D)), ("g11", kpiece(w_in2, g2 + D + 512)),
                   ("wo0", kpiece(A["w_out_2"][0], 0)), ("wo1", kpiece(A["w_out_2"][0], 512)),
                   ("keys", None),
                   ("pq0", kpiece(A["peer_wq_2"][0], 0)), ("pq1", kpiece(A["peer_wq_2"][0], 512)),
                   ("pq2", kpiece(A["peer_wq_2"][0], 1024)), ("pq3", kpiece(A["peer_wq_2"][0], 1536))]
        room = [n for n, _ in pieces2].index("room") % SLOTS
        place2 = {n: (i % SLOTS, i // SLOTS + 1 - (i % SLOTS == room and i >= SLOTS)) for i, (n, _) in enumerate(pieces2)}

        def view(slot, src):
            k, n = src.shape[1], src.shape[2]
            return ring[:, slot, 0:k * n].rearrange("p (k n) -> p k n", k=k)

        def pview(places, name, n=512):
            s = places[name][0]
            k = PIECE // n if n != 256 else KD
            return ring[:, s, 0:k * n].rearrange("p (k n) -> p k n", k=k)


        N_CONST, N_PRM = 3, 18
        ZEROED = ROWS // P + 1 + EXTRA * CAP // P
        stat_cols = {}

        def stat(name, n=NT):
            if name not in stat_cols:
                a = sum(w for _, w in stat_cols.values())
                assert a + n <= 400
                stat_cols[name] = (a, n)
            a, w = stat_cols[name]
            assert w == n
            return st[:, a:a + n]

        def rep_(ap, axis, shape):
            return ap.unsqueeze(axis).to_broadcast(shape)

        groups = {}

        def full(eng, name):
            b, n = groups[name]
            eng.wait_ge(bank_full[b], n)
            return psum[:, b, :]

        def emptied(eng, name):
            b, n = groups[name]
            eng.wait_ge(bank_read[b], n)

        block = ctx.enter_context(nc.Block())

        @block.tensor
        def _(pe):
            fills = [0] * 8
            turns = {}
            everyday = [tuple(range(7))]

            def bank(name, among=None):
                among = among or everyday[-1]
                turns[among] = turns.get(among, 0) + 1
                b = among[turns[among] % len(among)]
                if fills[b]:
                    pe.wait_ge(bank_read[b], fills[b])
                fills[b] += 1
                groups[name] = (b, fills[b])
                return b

            def mm(o, lhsT, rhs, k, n):
                return nc.tensor.matmul(o, lhsT, rhs, start=(k == 0), stop=(k == n - 1))

            def to_T(name, rows, ev_name):
                banks = [bank(f"{name}{g}") for g in range(4)]
                for t in range(NT):
                    pe.wait_ge(ev(ev_name), t + 1)
                    for g, b in enumerate(banks):
                        for c in range(2):
                            last = nc.tensor.transpose(psum[:, b, c * T + t * P:c * T + t * P + P],
                                                       rows[:, t, (2 * g + c) * P:(2 * g + c + 1) * P], ident[:, :])
                        if t == NT - 1:
                            last.then_inc(bank_full[b], 1)

            def proj_T(name, w, src, nk, chunks, first=0):
                for g in range(first // 2, chunks // 2):
                    b = bank(f"{name}{g}")
                    for c in range(2):
                        m = (2 * g + c) * P
                        for k in range(nk):
                            last = mm(psum[:, b, c * T:(c + 1) * T], w[:, k, m:m + P], src[:, k, :], k, nk)
                    last.then_inc(bank_full[b], 1)

            def landed(places, name):
                s, n = places[name]
                pe.wait_ge((piece_in if places is place1 else piece2_in)[s], 16 * n)

            pe.wait_ge(const_in, 16 * N_CONST)
            to_T("xn", scratch, "xn_ready")
            pe.wait_ge(prm_in, 16 * N_PRM)
            b = bank("prm")
            nc.tensor.transpose(psum[:, b, 0:100], prm[0:100, 0, :], ident[0:100, 0:100])
            nc.tensor.transpose(psum[:, b, 104:228], prm[0:124, 1, :], ident[0:124, 0:124])
            nc.tensor.transpose(psum[:, b, 228:276], prm[0:48, 2, :], ident[0:48, 0:48])
            nc.tensor.transpose(psum[0:64, b, 276:280], prmD[:, :], ident[0:4, 0:4])
            nc.tensor.transpose(psum[:, b, 280:296], crow[:, :], ident[0:16, 0:16]).then_inc(bank_full[b], 1)

            def sine_layer(i):
                b = bank(f"f{i}")
                if i == 0:
                    pe.wait_ge(ev("filt_in"), 16 * 4)
                    last = mm(psum[0:64, b, 0:T], w1s, feat, 0, 1)
                else:
                    pe.wait_ge(ev("sine_done"), i)
                    last = mm(psum[0:64, b, 0:T], w23[:, i - 1, :], fsmall[:, 2 * (i - 1), :], 0, 1)
                last.then_inc(bank_full[b], 1)

            def filter_spectra(o):
                b = bank(f"habs{o}")
                for t in range(NT):
                    pe.wait_ge(ev("abs_ready"), NT * o + t + 1)
                    last = mm(psum[:, b, :], ones[:, :], absb[:, t, :], t, NT)
                last.then_inc(bank_full[b], 1)
                pe.wait_ge(ev("ed_ready"), o + 1)
                for part in range(2):
                    for f in range(NT):
                        b = bank(f"sp{o}{part}{f}")
                        for t in range(NT):
                            last = mm(psum[:, b, :], dft[:, part, t, f * P:(f + 1) * P], filt[:, t, 2 * o + part, :], t, NT)
                        last.then_inc(bank_full[b], 1)

            sine_layer(0)
            for g in range(4):
                emptied(pe, f"xn{g}")
            landed(place1, "wa")
            proj_T("wa", pview(place1, "wa"), actT, KD, 2)
            sine_layer(1)
            proj_T("wa", pview(place1, "wa"), actT, KD, 4, 2)
            sine_layer(2)
            landed(place1, "wg")
            proj_T("wg", pview(place1, "wg"), actT, KD, 2)
            pe.wait_ge(ev("sine_done"), 3)
            landed(place1, "filt4")
            w4 = ring[0:64, place1["filt4"][0], 0:2048]
            for t in range(NT):
                for m in range(4):
                    b = bank(f"h{t}{m}")
                    mm(psum[:, b, :], fsmall[:, 4, t * P:(t + 1) * P], w4[:, m * CH:(m + 1) * CH], 0, 1) \
                        .then_inc(bank_full[b], 1)
            proj_T("wg", pview(place1, "wg"), actT, KD, 4, 2)
            landed(place1, "wq")
            proj_T("wq", pview(place1, "wq"), actT, KD, 4)
            pe.wait_ge(ev("tables_in"), 16 * 6)
            filter_spectra(0)
            landed(place1, "wkv")
            w = pview(place1, "wkv", 256)
            b = bank("k1")
            for k in range(KD):
                last = mm(psum[:, b, 0:T], w[:, k, 0:P], actT[:, k, :], k, KD)
            last.then_inc(bank_full[b], 1)
            b = bank("v1")
            for t in range(NT):
                for k in range(KD):
                    last = mm(psum[:, b, t * P:(t + 1) * P], actT[:, k, t * P:(t + 1) * P], w[:, k, P:2 * P], k, KD)
            last.then_inc(bank_full[b], 1)
            filter_spectra(1)
            emptied(pe, "wq0")
            emptied(pe, "wq1")
            emptied(pe, "k1")

            def score(b, col, h, t, k0, k1):
                r = slice((h % 2) * HD, (h % 2) * HD + HD)
                return mm(psum[:, b, col:col + k1 - k0], qT[r, h // 2, t * P:(t + 1) * P], kdup[r, h // 4, k0:k1], 0, 1)

            for par in range(2):
                b = bank(f"s0{par}")
                for i in range(4):
                    last = score(b, i * P, 2 * i + par, 0, 0, P)
                last.then_inc(bank_full[b], 1)
            for par in range(2):
                for pr in range(2):
                    b = bank(f"s1{par}{pr}")
                    for i in range(2):
                        last = score(b, i * T, 4 * pr + 2 * i + par, 1, 0, T)
                    last.then_inc(bank_full[b], 1)

            mod_bank = bank("mod", (7,))
            emptied(pe, "prm")

            def turn(p):
                for h in range(2):
                    i = 2 * p + h
                    for m in range(4):
                        o = 2 * (4 * i + m)
                        last = nc.tensor.transpose(psum[:, mod_bank, o:o + 2], mrow[:, i % 4, m * P:(m + 1) * P], ident[0:2, 0:2])
                if p < COLUMN_PAIRS - 1:
                    last.then_inc(ev("mod_turned"), 1)
                else:
                    last.then_inc(bank_full[mod_bank], 1)

            for p, pair_ in enumerate(mod_pairs):
                for j in pair_:
                    landed(place1, f"ada{j}")
                gate = p >= COLUMN_PAIRS
                if p == COLUMN_PAIRS:
                    pe.wait_ge(ev("gbias_in"), 16 * 2)
                b = bank(f"mr{p}")
                w = [pview(place1, f"ada{j}") for j in pair_]
                m = 1 if gate else 2
                n = KD + gate
                if gate:
                    for h in range(2):
                        mm(psum[64 * h:64 * h + 1, b, :], ones[0:1, 0:1], gbias[:, 2 * (p - COLUMN_PAIRS) + h, :], 0, n)
                for k in range(KD):
                    for h in range(2):
                        last = mm(psum[64 * h:64 * h + m, b, :], scT[:, k, 0:m], w[h][:, k, :], k + gate, n)
                last.then_inc(bank_full[b], 1)
                if 1 <= p <= COLUMN_PAIRS:
                    emptied(pe, f"mr{p - 1}")
                    turn(p - 1)

            def pv1(h):
                r = slice((h % 2) * HD, (h % 2) * HD + HD)
                emptied(pe, f"pt{h}")
                if h % 2 == 0:
                    bank(f"pv{h // 2}")
                b = groups[f"pv{h // 2}"][0]
                g = (h // 4) * HD
                s = pTbuf[:, h % 4, :]
                mm(psum[r, b, 0:P], vtok[:, 0, g:g + HD], s[:, 0:P], 0, 1)
                mm(psum[r, b, P:T], vtok[:, 0, g:g + HD], s[:, P:2 * P], 0, 2)
                last = mm(psum[r, b, P:T], vtok[:, 1, g:g + HD], s[:, 2 * P:3 * P], 1, 2)
                if h % 2:
                    last.then_inc(bank_full[b], 1)
                return last

            def attend1():
                pe.wait_ge(ev("p1_ready"), 2)
                emptied(pe, "v1")
                for h in range(HEADS):
                    b = bank(f"pt{h}")
                    for i, (t, kc) in enumerate(((0, 0), (1, 0), (1, 1))):
                        last = nc.tensor.transpose(psum[:, b, i * P:(i + 1) * P], prob1[:, t, h, kc * P:(kc + 1) * P], ident[:, :])
                    last.then_inc(bank_full[b], 1)
                    if h:
                        pv1(h - 1)
                pv1(HEADS - 1)

            pe.wait_ge(ev("conv_ready"), 1)
            for t in range(NT):
                b = bank(f"yt{t}")
                for c in range(KC):
                    last = nc.tensor.transpose(psum[:, b, c * P:(c + 1) * P], yT[:, c, t * P:(t + 1) * P], ident[:, :])
                last.then_inc(bank_full[b], 1)
            for g in range(2):
                emptied(pe, "yt0")
                emptied(pe, "yt1")
                b = bank(f"yb{g}")
                for c in range(2):
                    for t in range(NT):
                        last = nc.tensor.transpose(psum[:, b, c * T + t * P:c * T + t * P + P],
                                                   ytok[:, t, (2 * g + c) * P:(2 * g + c + 1) * P], ident[:, :])
                last.then_inc(bank_full[b], 1)

            def merge(pl, tag, branches, only=(0, 1)):
                for br in only:
                    src, need = branches[br]
                    landed(pl, f"o{br}")
                    wo = ring[:, pl[f"o{br}"][0], :].rearrange("p (k n) -> p k n", k=KC)
                    for half in range(2):
                        landed(pl, f"g{br}{half}")
                        wg = pview(pl, f"g{br}{half}")
                        for g in range(2):
                            i = 2 * half + g
                            b = bank(f"{tag}g{br}{i}")
                            for c in range(2):
                                for k in range(KD):
                                    last = mm(psum[:, b, c * T:(c + 1) * T], wg[:, k, (2 * g + c) * P:(2 * g + c + 1) * P],
                                              actT[:, k, :], k, KD)
                            last.then_inc(bank_full[b], 1)
                            if i == 0:
                                for nm in need:
                                    emptied(pe, nm)
                                if tag == "b" and br == 1:
                                    pe.wait_ge(ev("hy_ready"), 1)
                            b = bank(f"{tag}o{br}{i}")
                            for c in range(2):
                                m = (2 * i + c) * P
                                for k in range(KC):
                                    last = mm(psum[:, b, c * T:(c + 1) * T], wo[:, k, m:m + P], src[:, k, :], k, KC)
                            last.then_inc(bank_full[b], 1)

            def out_proj(pl, tag):
                pe.wait_ge(ev(f"{tag}merged"), 1)
                for t in range(NT):
                    for n in range(2):
                        landed(pl, f"wo{n}")
                        w = pview(pl, f"wo{n}")
                        b = bank(f"{tag}x{t}{n}")
                        for k in range(KD):
                            last = mm(psum[:, b, :], mergedT[:, k, t * P:(t + 1) * P], w[:, k, :], k, KD)
                        last.then_inc(bank_full[b], 1)

            branches = [(yactT, ("yb0", "yb1")), (attnT, tuple(f"pv{i}" for i in range(4)))]
            merge(place1, "a", branches, (0,))
            attend1()
            merge(place1, "a", branches, (1,))
            out_proj(place1, "a")
            to_T("rn", scratch, "rn_ready")
            for g in range(4):
                emptied(pe, f"rn{g}")
            b = bank("route")
            for t in range(NT):
                for k in range(KD):
                    last = mm(psum[:, b, t * 64:t * 64 + 36], actT[:, k, t * P:(t + 1) * P], wroute[:, k, :], k, KD)
            last.then_inc(bank_full[b], 1)
            to_T("cx", ctxr, "ctxn_ready")
            pe.wait_ge(ev("assign_ready"), 1)
            asg = arena2[:, 512:576].rearrange("p (t e) -> p t e", t=NT)
            b = bank("pos")
            mm(psum[:, b, 0:32], before[:, :], asg[:, 0, :], 0, 1)
            mm(psum[:, b, 32:64], ones[:, :], asg[:, 0, :], 0, 2)
            mm(psum[:, b, 32:64], before[:, :], asg[:, 1, :], 1, 2)
            mm(psum[:, b, 64:96], ones[:, :], asg[:, 0, :], 0, 2)
            mm(psum[:, b, 64:96], ones[:, :], asg[:, 1, :], 1, 2).then_inc(bank_full[b], 1)
            landed(place1, "ctxkv")
            for g in range(4):
                emptied(pe, f"cx{g}")
            w = pview(place1, "ctxkv", 256)
            for t in range(NT):
                b = bank(f"ckv{t}")
                for k in range(KD):
                    last = mm(psum[:, b, 0:256], actT[:, k, t * P:(t + 1) * P], w[:, k, :], k, KD)
                last.then_inc(bank_full[b], 1)
            b = bank("ckT")
            pe.wait_ge(ev("ck_ready"), 1)
            for t in range(NT):
                last = nc.tensor.transpose(psum[:, b, t * P:(t + 1) * P], kvt[:, t * 256:t * 256 + P], ident[:, :])
            last.then_inc(bank_full[b], 1)
            for b in range(8):
                pe.wait_ge(bank_read[b], fills[b])

            pe.wait_ge(ev("trips_ready"), 1)
            n_iter = pe.value_load(trips[0:1, 0:1], min_val=STEPS, max_val=MAXSTEPS)

            def rows_T():
                for c in range(KD):
                    last = nc.tensor.transpose(psum[:, c // 4, (c % 4) * BOTH:(c % 4 + 1) * BOTH], xrow[:, c * P:(c + 1) * P], ident[0:BOTH, 0:BOTH])
                last.then_inc(ev("rowsT_full"), 1)

            def both(bank_, lhs, slots, cols, nk, done):
                for k in range(nk):
                    for h in range(2):
                        w = ring[:, slots + h, :].rearrange("p (k n) -> p k n", k=nk)
                        last = mm(psum[h * CAP:(h + 1) * CAP, bank_, :], lhs[:, k, h * CAP:(h + 1) * CAP], w[:, k, cols], k, nk)
                last.then_inc(ev(done), 1)

            def landed_both(slots, i):
                for h in range(2):
                    pe.wait_ge(piece_in[slots + h], 16 * i + 16 * (base_use[slots + h] + 1))

            pe.wait_ge(ev("rows_in"), 16)
            rows_T()
            with pe.Fori(0, n_iter) as i:
                landed_both(0, i)
                pe.wait_ge(ev("rowsT_ready"), i + 1)
                both(3, xT, 0, slice(0, FF), KD, "gate_full")
                landed_both(2, i)
                both(4, xT, 2, slice(0, FF), KD, "up_full")
                pe.wait_ge(ev("rows_in"), 16 * i + 32)
                pe.sem_inc(pe_step, 1)
                rows_T()
                pe.wait_ge(ev("hid_ready"), i + 1)
                pe.sem_inc(pe_step, 1)
                for k in range(4):
                    last = nc.tensor.transpose(psum[:, 2, k * BOTH:(k + 1) * BOTH], hrow[:, k * P:(k + 1) * P], ident[0:BOTH, 0:BOTH])
                last.then_inc(ev("hidT_full"), 1)
                landed_both(4, i)
                pe.wait_ge(ev("hidT_ready"), i + 1)
                for n in range(2):
                    pe.wait_ge(ev(f"down_read{n}"), i + 1)
                    both(5 + n, hidT, 4, slice(n * 512, (n + 1) * 512), 4, f"down_full{n}")

            pe.wait_ge(ev("down_read0"), n_iter + 1)
            pe.wait_ge(ev("down_read1"), n_iter + 1)
            pe.sem_inc(pe_step, 1)
            everyday.append(tuple(range(8)))
            to_T("zn", scratch, "zn_ready")
            for g in range(4):
                emptied(pe, f"zn{g}")
            landed(place2, "q")
            w = pview(place2, "q")
            for t in range(NT):
                b = bank(f"q{t}")
                for k in range(KD):
                    last = mm(psum[:, b, :], actT[:, k, t * P:(t + 1) * P], w[:, k, :], k, KD)
                last.then_inc(bank_full[b], 1)
            landed(place2, "kv")
            w = pview(place2, "kv", 256)
            for t in range(NT):
                b = bank(f"kv{t}")
                for k in range(KD):
                    last = mm(psum[:, b, 0:256], actT[:, k, t * P:(t + 1) * P], w[:, k, :], k, KD)
                last.then_inc(bank_full[b], 1)
            for j in range(3):
                landed(place2, f"hy{j}")
                proj_T(f"hy{j}", pview(place2, f"hy{j}"), actT, KD, 4)
            pe.wait_ge(ev("qk2_ready"), 1)
            for g in range(2):
                b = bank(f"qT{g}")
                for c in range(2):
                    for t in range(NT):
                        last = nc.tensor.transpose(psum[:, b, c * T + t * P:c * T + t * P + P],
                                                   qtok[:, t, (2 * g + c) * P:(2 * g + c + 1) * P], ident[:, :])
                last.then_inc(bank_full[b], 1)
            b = bank("kT")
            for t in range(NT):
                last = nc.tensor.transpose(psum[:, b, t * P:(t + 1) * P], ktok[:, t, :], ident[:, :])
            last.then_inc(bank_full[b], 1)
            emptied(pe, "qT0")
            emptied(pe, "qT1")
            pe.wait_ge(ev("k2_ready"), 1)
            units = [(h, t) for h in range(HEADS) for t in range(NT)]

            def score2(u):
                h, t = units[u]
                b = bank(f"sc{u}", (0, 1, 2, 3, 4))
                score(b, 0, h, t, 0, 2 * T).then_inc(bank_full[b], 1)

            def pt2(u):
                pe.wait_ge(ev("p2_ready"), u + 1)
                b = bank(f"qt{u}", (0, 1, 2, 3, 4))
                for kc in range(4):
                    last = nc.tensor.transpose(psum[:, b, kc * P:(kc + 1) * P], prob2[:, u % 4, kc * P:(kc + 1) * P], ident[:, :])
                last.then_inc(bank_full[b], 1)

            def pv2(u):
                h, t = units[u]
                emptied(pe, f"qt{u}")
                if u % 4 == 0:
                    bank(f"pw{h // 2}", (7,))
                b = groups[f"pw{h // 2}"][0]
                r = slice((h % 2) * HD, (h % 2) * HD + HD)
                for kc in range(4):
                    last = mm(psum[r, b, t * P:(t + 1) * P], vtok[:, kc, (h // 4) * HD:(h // 4 + 1) * HD],
                              pT2[:, u % 2, kc * P:(kc + 1) * P], kc, 4)
                if u % 4 == 3:
                    last.then_inc(bank_full[b], 1)

            def hy_rows(o):
                src = (zs[:, 0:4, :], y1T)[o]
                pe.wait_ge(ev(("short_ready", "y1_ready")[o]), 1)
                for t in range(NT):
                    b = bank(f"vt{o}{t}", (5, 6))
                    for c in range(KC):
                        last = nc.tensor.transpose(psum[:, b, c * P:(c + 1) * P], src[:, c, t * P:(t + 1) * P], ident[:, :])
                    last.then_inc(bank_full[b], 1)

            def hy_spectrum(o, part):
                for t in range(NT):
                    emptied(pe, f"vt{o}{t}")
                for f in range(NT):
                    b = bank(f"U{o}{part}{f}", (5, 6))
                    for t in range(NT):
                        last = mm(psum[:, b, :], dft[:, part, t, f * P:(f + 1) * P], vtime[:, t, :], t, NT)
                    last.then_inc(bank_full[b], 1)

            def hy_back(o, g):
                pe.wait_ge(ev("Y_ready"), o + 1)
                b = bank(f"I{o}{g}", (5, 6))
                for c in range(2):
                    for k in range(4):
                        last = mm(psum[:, b, c * T:(c + 1) * T], Y[:, k, (2 * g + c) * P:(2 * g + c + 1) * P], idft[:, k, :], k, 4)
                last.then_inc(bank_full[b], 1)

            hy_parts = {0: (hy_rows, 0), 1: (hy_spectrum, 0, 0), 3: (hy_spectrum, 0, 1), 6: (hy_back, 0, 0), 7: (hy_back, 0, 1),
                        9: (hy_rows, 1), 10: (hy_spectrum, 1, 0), 12: (hy_spectrum, 1, 1), 15: (hy_back, 1, 0)}
            for u in range(3):
                score2(u)
            for u in range(16):
                if u + 3 < 16:
                    score2(u + 3)
                if u in hy_parts:
                    hy_parts[u][0](*hy_parts[u][1:])
                pt2(u)
                if u:
                    pv2(u - 1)
            pv2(15)
            hy_back(1, 1)
            merge(place2, "b", [(attnT, tuple(f"pw{i}" for i in range(4))), (hyoT, ())])

            out_proj(place2, "b")
            pe.wait_ge(ev("keys1_in"), 16)
            landed(place2, "keys")
            kp = ring[:, place2["keys"][0], 0:2048].rearrange("p (c d) -> p c d", d=P)
            for g in range(4):
                b = bank(f"keyT{g}")
                for c in range(4):
                    last = nc.tensor.transpose(psum[:, b, c * P:(c + 1) * P], kp[:, 4 * g + c, :], ident[:, :])
                last.then_inc(bank_full[b], 1)
            to_T("pn", scratch, "pn_ready")
            for g in range(4):
                emptied(pe, f"pn{g}")
                emptied(pe, f"keyT{g}")
            for t in range(NT):
                for n in range(2):
                    b = bank(f"xp{t}{n}")
                    for c in range(4):
                        last = nc.tensor.transpose(psum[:, b, c * P:(c + 1) * P], actT[:, 4 * n + c, t * P:(t + 1) * P], ident[:, :])
                    last.then_inc(bank_full[b], 1)

            def key_scores(t, g):
                for pair in range(2):
                    emptied(pe, f"pq{g}{pair}")
                b = bank(f"ks{t}{g}")
                for i in range(4):
                    h, half = (4 * g + i) // 2, (4 * g + i) % 2
                    last = mm(psum[:, b, i * P:(i + 1) * P], pqT[:, 2 * h + half, t * P:(t + 1) * P],
                              keysT[:, half * 8 + h, :], 0, 1)
                last.then_inc(bank_full[b], 1)

            for j in range(4):
                landed(place2, f"pq{j}")
                proj_T(f"pq{j}", pview(place2, f"pq{j}"), actT, KD, 4)
                if j:
                    key_scores(0, j - 1)
            key_scores(0, 3)
            for g in range(4):
                key_scores(1, g)

        @block.sync
        def _(sp):
            for t in range(NT):
                sp.dma_start(resid[:, t, :], A["x"][0, t * P:(t + 1) * P, :]).then_inc(ev(f"x_in{t}"), 16)
            sp.dma_start(ident[:, :], A["c_ident"]).then_inc(const_in, 16)
            rows_A = [("g_mix", 8), ("b_dw", 4), ("ln_conv_g", 4), ("ln_conv_b", 4), ("norm_mix_g_2", 8),
                      ("norm_ffn_g_2", 8), ("g_ffn", 8)]
            r = 0
            for nm, n in rows_A:
                sp.dma_start(prm[r:r + n, 0, :], A[nm][0].rearrange("(r c) -> r c", c=P)).then_inc(prm_in, 16)
                r += n
            sp.dma_start(prm[r:r + 36, 0, :], A["hy_conv_w_2"][0].rearrange("j (r c) -> (j r) c", c=P)).then_inc(prm_in, 16)
            r += 36
            sp.dma_start(prm[r:r + 12, 0, :], A["hy_conv_b_2"][0].rearrange("(r c) -> r c", c=P)).then_inc(prm_in, 16)
            r += 12
            sp.dma_start(prm[r:r + 8, 0, :], A["hy_skip_2"][0].rearrange("j (r c) -> (j r) c", c=P)).then_inc(prm_in, 16)
            assert r + 8 == 100
            sp.dma_start(prm[0:124, 1, :], A["w_dw"][0, :, 0, :].rearrange("j (r c) -> (j r) c", c=P)).then_inc(prm_in, 16)
            sp.dma_start(prm[0:48, 2, :], A["ada_b_2"][0].rearrange("(r c) -> r c", c=P)).then_inc(prm_in, 16)
            for i, nm in enumerate(("hf_b1_2", "hf_b2_2", "hf_b3_2", "hf_freq_2")):
                sp.dma_start(prmD[i:i + 1, :], A[nm]).then_inc(prm_in, 16)
            sp.dma_start(crow[0:8, :], A["c_2"][0].rearrange("(r c) -> r c", c=P)).then_inc(prm_in, 16)
            sp.dma_start(crow[8:16, :], A["c_ctx_2"].rearrange("(r c) -> r c", c=P)).then_inc(prm_in, 16)
            sp.dma_start(w1s, A["hf_w1_2"][0]).then_inc(ev("filt_in"), 16)
            sp.dma_start(feat, A["c_feat"]).then_inc(ev("filt_in"), 16)
            sp.dma_start(w23[:, 0, :], A["hf_w2_2"][0]).then_inc(ev("filt_in"), 16)
            sp.dma_start(w23[:, 1, :], A["hf_w3_2"][0]).then_inc(ev("filt_in"), 16)

            last_reader = {**{f"ada{j}": f"mr{p}" for p, pair_ in enumerate(mod_pairs) for j in pair_}, "ctxkv": "ckv1", "filt4": "h13", "wa": "wa1", "wg": "wg1",
                           "wq": "wq1", "wkv": "v1", "o0": "ao03", "g00": "ag01", "g01": "ag03", "o1": "ao13",
                           "g10": "ag11", "g11": "ag13", "wo0": "ax10", "wo1": "ax11"}

            def filled(name):
                b, n = groups[name]
                sp.wait_ge(bank_full[b], n)

            for i, (nm, src) in enumerate(pieces):
                s = i % SLOTS
                if i >= SLOTS:
                    filled(last_reader[pieces[i - SLOTS][0]])
                dst = ring[0:64, s, 0:2048] if nm == "filt4" else view(s, src)
                sp.dma_start(dst, src).then_inc(piece_in[s], 16)
                if nm == "filt4":
                    for dstt, cn in ((before, "c_before"), (rel, "c_rel"), (iota, "c_iota")):
                        sp.dma_start(dstt[:, :], A[cn]).then_inc(ev("tables_in"), 16)
                    sp.dma_start(tok2[:, :, :], A["c_decay"].rearrange("p a m c -> p a (m c)")).then_inc(dec_in, 16)
                if nm == "wkv":
                    filled("xn3")
                    for a, c0 in ((0, 2 * D), (1, 5 * D)):
                        sp.dma_start(scratch[0:1, a, :], A["ada_b_2"][:, c0:c0 + D]).then_inc(ev("gbias_in"), 16)
                if nm == "wq":
                    sp.dma_start(dft[:, :, :, :], A["c_dft"]).then_inc(ev("tables_in"), 16)
                    sp.dma_start(idft[:, :, :], A["c_idft"]).then_inc(ev("tables_in"), 16)
                    sp.dma_start(rope[:, :, :, :], A["c_rope"]).then_inc(ev("tables_in"), 16)
                if nm == "wo0":
                    filled("pt7")
                    sp.dma_start(ctxr, A["ctx_2"][0].rearrange("(t p) d -> p t d", p=P)).then_inc(ctx_in, 16)

            def expert_piece(s, e):
                h, j = s % 2, s // 2
                w = (A["w_gate"], A["w_up"], A["w_down"])[j][0]
                src = w[e, :, :] if isinstance(e, int) else w[bass.ds(e, 1), :, :].rearrange("e k n -> (e k) n")
                k = 4 if j == 2 else KD
                sp.dma_start(ring[:, s, :].rearrange("p (k n) -> p k n", k=k),
                             src.rearrange("(k p) n -> p k n", p=P)).then_inc(piece_in[s], 16)

            for s in (2, 3, 4, 5, 0, 1):
                prev = [nm for i, (nm, _) in enumerate(pieces) if i % SLOTS == s][-1]
                filled(last_reader[prev])
                expert_piece(s, s % 2)

            def expert_step(i, experts):
                for s in range(SLOTS):
                    sp.wait_ge(ev(("gate_full", "up_full", "down_full1")[s // 2]), i)
                    expert_piece(s, experts[s % 2])

            with sp.Fori(1, STEPS - 1) as i:
                expert_step(i, (2 * i, 2 * i + 1))
            sp.wait_ge(ev("trips_ready"), 1)
            n_iter = sp.value_load(trips[0:1, 0:1], min_val=STEPS, max_val=MAXSTEPS)
            with sp.Fori(STEPS - 1, n_iter) as i:
                expert_step(i, [sp.value_load(elist[0:1, bass.ds(i * 2 + h, 1)], min_val=0, max_val=EXPERTS - 1) for h in range(2)])

            last2 = {"q": "q1", "kv": "kv1", "hy0": "hy01", "hy1": "hy11", "hy2": "hy21", "room": "I11", "o0": "bo03", "g00": "bg01",
                     "g01": "bg03", "o1": "bo13", "g10": "bg11", "g11": "bg13",
                     "wo0": "bx10", "wo1": "bx11", "keys": "keyT3", "pq0": "pq01", "pq1": "pq11", "pq2": "pq21",
                     "pq3": "pq31"}
            for i, (nm, src) in enumerate(pieces2):
                s = i % SLOTS
                if i < SLOTS:
                    sp.wait_ge(ev(("gate_full", "up_full", "down_full1")[s // 2]), n_iter)
                else:
                    filled(last2[pieces2[i - SLOTS][0]])
                if nm == "hy0":
                    sp.wait_ge(ev("fetched"), 16 * 4)
                if nm == "room":
                    continue
                if nm == "keys":
                    kp = ring[:, s, 0:2048].rearrange("p (a h d) -> p a h d", a=2, d=P)
                    for half, knm in enumerate(("peer_keys1_2", "peer_keys2_2")):
                        sp.dma_start(kp[:, half, :, :], A[knm][0].rearrange("h n d -> n h d")).then_inc(
                            (ev("keys1_in"), piece2_in[s])[half], 16)
                    continue
                sp.dma_start(view(s, src), src).then_inc(piece2_in[s], 16)
                if nm == "q":
                    sp.wait_ge(ev("amerged"), 1)
                    sp.dma_start(gfrow, A["g_final"].rearrange("(a n) -> a n", a=1).to_broadcast([P, D])).then_inc(ev("gf_in"), 16)
                if nm == "g11":
                    filled("pw3")
                    sp.wait_ge(ev("grow_sent"), 16)
                    sp.dma_start(g1row, gate_rows[0:1, 0:D].to_broadcast([P, D])).then_inc(ev("g1_in"), 16)
                if nm == "pq3":
                    filled("pq31")
                    sp.dma_start(g2row, gate_rows[0:1, D:2 * D].to_broadcast([P, D])).then_inc(ev("g2_in"), 16)
                    sp.dma_start(flrow, A["final_norm_g_2"].rearrange("(a n) -> a n", a=1).to_broadcast([P, D])).then_inc(ev("g2_in"), 16)
            for t in range(NT):
                sp.wait_ge(ev("final_ready"), t + 1)
                sp.dma_start(out[0, t * P:(t + 1) * P, :], resid[:, t, :]).then_inc(ev("out_sent"), 16)
            sp.wait_ge(ev("out_sent"), 16 * NT)

        @block.gpsimd
        def _(pool):
            steps = [0]

            def own(ins):
                steps[0] += 1
                ins.then_inc(pool_step, 1)
                pool.wait_ge(pool_step, steps[0])

            nc.gpsimd.memset(ones[:, :], 1.0).then_inc(const_in, 16)
            nc.gpsimd.memset(epscol[:, :], EPS).then_inc(const_in, 16)
            for dst, nm in ((rbias[:, 0:GROUPS], "b_group"), (rbias[:, GROUPS:], "b_expert"), (sinkrow[:, :], "sinks"),
                            (qkg[:, 0, :], "q_norm_g_2"), (qkg[:, 1, :], "k_norm_g_2")):
                pool.dma_start(dst, A[nm].to_broadcast([P, A[nm].shape[1]])).then_inc(ev("bcast_in"), 16)
            pool.dma_start(wroute[:, :, 0:GROUPS], A["w_group"][0].rearrange("(k p) n -> p k n", p=P)).then_inc(ev("bcast_in"), 16)
            pool.dma_start(wroute[:, :, GROUPS:], A["w_expert"][0].rearrange("(k p) n -> p k n", p=P)).then_inc(ev("bcast_in"), 16)
            b, n = groups["prm"]
            pool.wait_ge(bank_full[b], n)
            own(nc.gpsimd.memset(zeros, 0.0))
            pool.wait_ge(ev("conv_ready"), 1)
            z4 = zeros.unsqueeze(1).to_broadcast([P, 4, T])
            for b in range(ROWS // P + 1):
                pool.dma_start(xs[b * P:(b + 1) * P, :].rearrange("r (q c) -> r q c", q=4), z4).then_inc(ev("zeroed"), 16)
            for b in range(EXPERTS * CAP // P, ROWS // P):
                pool.dma_start(ys[b * P:(b + 1) * P, :].rearrange("r (q c) -> r q c", q=4), z4).then_inc(ev("zeroed"), 16)
            pool.wait_ge(ev("zeroed"), 16 * ZEROED)
            pool.wait_ge(ev("slots_ready"), 1)
            pool.wait_ge(ev("rn_ready"), NT)
            for t in range(NT):
                for k in range(2):
                    pool.indirect_dma_start(out=xs[:, :], out_offset=bass.IndirectOffsetOnAxis(ap=sloti[:, 2 * t + k:2 * t + k + 1], axis=0),
                                            in_=scratch[:, t, :], in_offset=None).then_inc(ev("sent"), 16)
            pool.wait_ge(ev("sent"), 16 * 2 * NT)
            pool.dma_start(xrow, xs[0:BOTH, :]).then_inc(ev("rows_in"), 16)
            pool.wait_ge(ev("trips_ready"), 1)
            n_iter = pool.value_load(trips[0:1, 0:1], min_val=STEPS, max_val=MAXSTEPS)
            with pool.Fori(0, n_iter) as i:
                pool.wait_ge(ev("rowsT_full"), i + 1)
                pool.sem_inc(pool_step, 1)
                pool.dma_start(xrow, xs[bass.ds((i + 1) * BOTH, BOTH), :]).then_inc(ev("rows_in"), 16)
            pool.wait_ge(ev("stored"), n_iter * 16 + 1)
            pool.sem_inc(pool_step, 1)
            for j in range(4):
                pool.indirect_dma_start(out=back[:, j, :], out_offset=None, in_=ys[:, :],
                                        in_offset=bass.IndirectOffsetOnAxis(ap=sloti[:, j:j + 1], axis=0)).then_inc(ev("fetched"), 16)

            per = PICKS // ROWBUFS
            for t in range(NT):
                for r, tab in enumerate(("peer_u_2", "peer_v_2")):
                    for part in range(1 if r else 4):
                        if r == 0:
                            pool.wait_ge(ev("rowid_ready"), 4 * t + part + 1)
                        with pool.Fori(*((0, per) if r else (part * per // 4, (part + 1) * per // 4))) as i:
                            for b in range(ROWBUFS):
                                pool.wait_ge(ev("row_used"), (i + (2 * t + r) * per) * ROWBUFS + b + 1)
                                pool.sem_inc(pool_step, 1)
                                nc.gpsimd.tensor_copy(cur[:, b:b + 1], rowid[:, t, bass.ds(i * ROWBUFS + b, 1)]).then_inc(ev("cur_set"), 1)
                                pool.wait_ge(ev("cur_set"), (i + (2 * t + r) * per) * ROWBUFS + b + 1)
                                pool.sem_inc(pool_step, 1)
                                pool.indirect_dma_start(out=rows[:, b, :], out_offset=None, in_=A[tab][0],
                                                        in_offset=bass.IndirectOffsetOnAxis(ap=cur[:, b:b + 1], axis=0)).then_inc(ev(f"row_in{b}"), 16)

        @block.scalar
        def _(act):
            counts = {}

            def a(ins, name=None):
                s = ev(name) if name else act_step
                counts[s.name] = counts.get(s.name, 0) + 1
                ins.then_inc(s, 1)
                act.wait_ge(s, counts[s.name])

            def last(ins, name):
                b, n = groups[name]
                ins.then_inc(bank_read[b], 1)
                act.wait_ge(bank_read[b], n)

            def squares(tag, src, ready=None, junk=scratch):
                for t in range(NT):
                    if ready:
                        act.wait_ge(ev(ready), t + 1)
                    if tag == "xn":
                        act.wait_ge(ev(f"x_in{t}"), 16)
                    a(nc.scalar.activation(junk[:, t, :], src[:, t, :], ACT.Square, accum_out=stat(f"{tag}_ss")[:, t:t + 1]))
                    a(nc.scalar.activation(stat(f"{tag}_sd")[:, t:t + 1], stat(f"{tag}_ss")[:, t:t + 1], ACT.Sqrt, bias=epscol[:, 0:1], scale=1.0 / D), f"{tag}_sd")

            def take_T(name, scale, bias=None):
                for g in range(4):
                    ps = full(act, f"{name}{g}")
                    for c in range(2):
                        k = 2 * g + c
                        kw = {} if bias is None else {"bias": bias[:, k:k + 1]}
                        ins = nc.scalar.activation(actT[:, k, :], ps[:, c * T:(c + 1) * T], ACT.Identity, scale=scale[:, k:k + 1], **kw)
                    last(ins, f"{name}{g}")

            def copy_out(name, dst, w=512, func=ACT.Copy, **kw):
                last(nc.scalar.activation(dst, full(act, name)[:, 0:w], func, **kw), name)

            act.wait_ge(const_in, 16 * N_CONST)
            squares("xn", resid)
            act.wait_ge(ev("cols_ready"), 1)
            take_T("xn", colsA[:, 0:8])

            def sine(i):
                act.wait_ge(ev("sine_arg"), i + 1)
                a(nc.scalar.activation(fsmall[:, 2 * i, :], fsmall[:, 2 * i + 1, :], ACT.Sin), "sine_done")

            def pair(dst, g):
                return dst[:, 2 * g:2 * g + 2, :].rearrange("p c t -> p (c t)")

            sine(0)
            copy_out("wa0", pair(aT, 0))
            sine(1)
            copy_out("wa1", pair(aT, 1))
            sine(2)
            ps = full(act, "prm")
            last(nc.scalar.activation(scT[:, :, :].rearrange("p k j -> p j k"), ps[:, 280:296].rearrange("p (j k) -> p j k", j=2), ACT.Silu), "prm")
            for g in range(2):
                copy_out(f"wg{g}", pair(sgT, g), func=ACT.Sigmoid)
            for g in range(2):
                copy_out(f"wq{g}", pair(qT, g))
            ps = full(act, "k1")
            for g in range(KV):
                for half in range(2):
                    ins = nc.scalar.activation(kdup[half * HD:(half + 1) * HD, g, 0:T], ps[g * HD:(g + 1) * HD, 0:T], ACT.Copy)
            last(ins, "k1")
            copy_out("v1", vtok[:, 0:2, :].rearrange("p t c -> p (t c)"), 256)
            act.wait_ge(ev("filters_ready"), 1)
            for par in range(2):
                ps = full(act, f"s0{par}").rearrange("p (i k) -> p i k", i=4)
                dst = prob1[:, 0, :, 0:P].rearrange("p (i r) k -> p r i k", r=2)[:, par, :, :]
                last(nc.scalar.activation(dst, ps, ACT.Copy, scale=HD ** -0.5), f"s0{par}")
            for par in range(2):
                for pr in range(2):
                    ps = full(act, f"s1{par}{pr}").rearrange("p (i k) -> p i k", i=2)
                    dst = prob1[:, 1, 4 * pr:4 * pr + 4, :].rearrange("p (i r) k -> p r i k", r=2)[:, par, :, :]
                    last(nc.scalar.activation(dst, ps, ACT.Copy, scale=HD ** -0.5), f"s1{par}{pr}")
            emptied(act, "h13")
            for p in range(len(mod_pairs)):
                if p >= COLUMN_PAIRS:
                    if p == COLUMN_PAIRS:
                        full(act, "mod")
                elif p >= 2:
                    act.wait_ge(ev("mod_turned"), p - 1)
                m = 1 if p >= COLUMN_PAIRS else 2
                ps = full(act, f"mr{p}")
                for h in range(2):
                    ins = nc.scalar.activation(mrow[0:m, (2 * p + h) % 4, :], ps[64 * h:64 * h + m, :], ACT.Copy)
                last(ins, f"mr{p}")
            act.dma_start(gate_rows, tok2[0:1, :, :].rearrange("p a d -> p (a d)")).then_inc(ev("grow_sent"), 16)
            for t in range(NT):
                act.wait_ge(ev("ln_var"), t + 1)
                a(nc.scalar.activation(stat("ln_sd")[:, t:t + 1], stat("ln_v")[:, t:t + 1], ACT.Sqrt, bias=epscol[:, 0:1]), "ln_sd")
            for g in range(2):
                ps = full(act, f"yb{g}")
                for c in range(2):
                    k = 2 * g + c
                    ins = nc.scalar.activation(yactT[:, k, :], ps[:, c * T:(c + 1) * T], ACT.Silu, scale=colsA[:, 12 + k:13 + k], bias=colsA[:, 16 + k:17 + k])
                last(ins, f"yb{g}")

            def gate_of(tag, j):
                br, i = j // 4, j % 4
                if j >= 2:
                    emptied(act, f"{tag}o{(j - 2) // 4}{(j - 2) % 4}")
                copy_out(f"{tag}g{br}{i}", sgate[tag][:, j % 2, :], func=ACT.Sigmoid)

            for t in range(NT):
                act.wait_ge(ev("p1_shift"), t + 1)
                w = P * (t + 1)
                a(nc.scalar.activation(prob1[:, t, :, 0:w], prob1[:, t, :, 0:w], ACT.Exp))
                a(nc.scalar.activation(stat("p1_es", 16)[:, 8 * t:8 * t + 8], stat("p1_sm", 16)[:, 8 * t:8 * t + 8], ACT.Exp), "p1_exp")
                gate_of("a", t)
            gate_of("a", 2)
            gate_of("a", 3)
            for h in range(HEADS):
                copy_out(f"pt{h}", pTbuf[:, h % 4, 0:384], 384)
                if h % 2 == 0 and h:
                    copy_out(f"pv{h // 2 - 1}", attnT[:, h // 2 - 1, :], T)
            copy_out("pv3", attnT[:, 3, :], T)
            for j in range(4, 8):
                gate_of("a", j)
            act.wait_ge(ctx_in, 16)
            squares("cx", ctxr, None, qjunk)
            squares("rn", resid, "ah_ready")
            take_T("rn", colsA[:, 36:44])
            take_T("cx", modsc[:, 1, :], mod[:, 0:KD, 1])
            act.wait_ge(ev("rt_gmax"), 1)
            for t in range(NT):
                a(nc.scalar.activation(rt[:, 600 + 4 * t:604 + 4 * t], rt[:, 72 + 36 * t:76 + 36 * t], ACT.Exp, bias=stat("rt_ng")[:, t:t + 1],
                                       accum_out=stat("rt_gs")[:, t:t + 1]), "rt_gsum")
            act.wait_ge(ev("rt_top"), 1)
            for t in range(NT):
                a(nc.scalar.activation(stat("rt_e1")[:, t:t + 1], rt[:, 144 + 8 * t + 1:144 + 8 * t + 2], ACT.Exp, bias=stat("rt_nv")[:, t:t + 1]), "rt_e1")

            act.wait_ge(ev("ck_ss"), 1)
            a(nc.scalar.activation(stat("ck_sd", 4), stat("ck_ss", 4), ACT.Sqrt, bias=epscol[:, 0:1], scale=1.0 / HD), "ck_sd")

            act.wait_ge(ev("trips_ready"), 1)
            n_iter = act.value_load(trips[0:1, 0:1], min_val=STEPS, max_val=MAXSTEPS)
            act.sem_inc(ev("down_read0"), 1)
            act.sem_inc(ev("stored"), 1)
            with act.Fori(0, n_iter) as i:
                act.wait_ge(ev("gate_full"), i + 1)
                nc.scalar.activation(silu, psum[0:BOTH, 3, :], ACT.Silu).then_inc(ev("silu_ready"), 1)
                act.wait_ge(ev("hidT_full"), i + 1)
                nc.scalar.activation(hidT.rearrange("p k c -> p (k c)"), psum[:, 2, 0:4 * BOTH], ACT.Copy).then_inc(ev("hidT_ready"), 1)
                act.wait_ge(ev("down_full0"), i + 1)
                act.wait_ge(ev("stored"), 16 * i + 1)
                nc.scalar.activation(yrow[:, 0:512], psum[0:BOTH, 5, :], ACT.Copy).then_inc(ev("down_read0"), 1)
                act.wait_ge(ev("down_read0"), i + 2)
                act.wait_ge(ev("down_read1"), i + 2)
                act.dma_start(ys[bass.ds(i * BOTH, BOTH), :], yrow).then_inc(ev("stored"), 16)

            squares("fn", resid, "moe_added", normjunk)
            squares("zn", resid, "x2_ready", normjunk)
            take_T("zn", modsc[:, 0, :], mod[:, 0:KD, 0])
            for t in range(NT):
                copy_out(f"q{t}", qtok[:, t, :])
            act.wait_ge(ev("qk_ss"), 1)
            a(nc.scalar.activation(stat("qk_sd", 20), stat("qk_ss", 20), ACT.Sqrt, bias=epscol[:, 0:1], scale=1.0 / HD), "qk_sd")
            for j in range(6):
                if j == 0:
                    act.wait_ge(ev("pads_zero"), 1)
                if j >= 2:
                    act.wait_ge(ev("short_done"), j - 1)
                ps = full(act, f"hy{j // 2}{j % 2}").rearrange("p (c t) -> p c t", c=2)
                last(nc.scalar.activation(hpad[:, j % 2, :, 1:T + 1], ps, ACT.Copy), f"hy{j // 2}{j % 2}")
            for g in range(2):
                copy_out(f"qT{g}", qT[:, 2 * g:2 * g + 2, :].rearrange("p c t -> p (c t)"))

            def exp_unit(u):
                act.wait_ge(ev("nmax"), u + 1)
                if u >= 4:
                    full(act, f"qt{u - 4}")
                else:
                    full(act, "kT")
                last(nc.scalar.activation(prob2[:, u % 4, :], full(act, f"sc{u}"), ACT.Exp, bias=stat("nm2", 16)[:, u:u + 1], scale=HD ** -0.5,
                                          accum_out=stat("sum2", 16)[:, u:u + 1]), f"sc{u}")

            def hy_rows(o):
                for t in range(NT):
                    copy_out(f"vt{o}{t}", vtime[:, t, :])

            def hy_spectrum(o, part):
                if o == 0 and part == 0:
                    act.wait_ge(ev("down_read1"), n_iter + 1)
                for f in range(NT):
                    copy_out(f"U{o}{part}{f}", Usb[:, 2 * part + f, :])

            hy_parts = {0: (hy_rows, 0), 1: (hy_spectrum, 0, 0), 3: (hy_spectrum, 0, 1),
                        9: (hy_rows, 1), 10: (hy_spectrum, 1, 0), 12: (hy_spectrum, 1, 1)}
            exp_unit(0)
            exp_unit(1)
            for u in range(16):
                if u + 2 < 16:
                    exp_unit(u + 2)
                if u in hy_parts:
                    hy_parts[u][0](*hy_parts[u][1:])
                copy_out(f"qt{u}", pT2[:, u % 2, :])
                if u % 4 == 0 and u:
                    copy_out(f"pw{u // 4 - 1}", attnT[:, u // 4 - 1, :], T)
            copy_out("pw3", attnT[:, 3, :], T)
            for j in range(8):
                gate_of("b", j)
            for g in range(4):
                copy_out(f"keyT{g}", keysT[:, 4 * g:4 * g + 4, :].rearrange("p c n -> p (c n)"))
            squares("pn", resid, "bh_ready")
            take_T("pn", modsc[:, 2, :], mod[:, 24:32, 0])
            for t in range(NT):
                for n in range(2):
                    copy_out(f"xp{t}{n}", tok2[:, t, n * 512:(n + 1) * 512])

            def scores_out(t, g):
                copy_out(f"ks{t}{g}", S[:, t, 4 * g:4 * g + 4, :].rearrange("p c n -> p (c n)"))

            for j in range(4):
                for g in range(2):
                    k = 4 * j + 2 * g
                    copy_out(f"pq{j}{g}", pqT[:, k:k + 2, :].rearrange("p c t -> p (c t)"))
                if j:
                    scores_out(0, j - 1)
            scores_out(0, 3)
            for g in range(4):
                scores_out(1, g)
            for t in range(NT):
                act.wait_ge(ev("best_shift"), t + 1)
                a(nc.scalar.activation(gates[:, t, :], gates[:, t, :], ACT.Exp), "best_exp")
                act.wait_ge(ev("dots_ready"), t + 1)
                a(nc.scalar.activation(dots[:, t, :], dots[:, t, :], ACT.Gelu_apprx_tanh), "gelu_done")
                act.wait_ge(ev("x3_ready"), t + 1)
                a(nc.scalar.activation(tok2[:, t, :], resid[:, t, :], ACT.Square, accum_out=stat("ff_ss")[:, t:t + 1]))
                a(nc.scalar.activation(stat("ff_sd")[:, t:t + 1], stat("ff_ss")[:, t:t + 1], ACT.Sqrt, bias=epscol[:, 0:1], scale=1.0 / D), "ff_sd")

        @block.vector
        def _(dve):
            counts = {}
            V = nc.vector

            def v(ins, name=None):
                s = ev(name) if name else dve_step
                counts[s.name] = counts.get(s.name, 0) + 1
                ins.then_inc(s, 1)
                dve.wait_ge(s, counts[s.name])

            def v_pair(ins):
                counts[dve_step.name] = counts.get(dve_step.name, 0) + 1
                ins.then_inc(dve_step, 1)
                dve.wait_ge(dve_step, counts[dve_step.name] - 1)

            def v_done():
                dve.wait_ge(dve_step, counts[dve_step.name])

            def last(ins, name):
                b, n = groups[name]
                ins.then_inc(bank_read[b], 1)
                dve.wait_ge(bank_read[b], n)

            def norm_rows(tag, src, name, gain=None):
                for t in range(NT):
                    dve.wait_ge(ev(f"{tag}_sd"), t + 1)
                    r = stat(f"{tag}_r")[:, t:t + 1]
                    v(V.reciprocal(r, stat(f"{tag}_sd")[:, t:t + 1]))
                    if gain is None:
                        v(V.tensor_scalar(scratch[:, t, :], src[:, t, :], r, None, ALU.mult), name)
                    else:
                        v(V.scalar_tensor_tensor(src[:, t, :], src[:, t, :], r, gain, ALU.mult, ALU.mult), name)

            dve.wait_ge(const_in, 16 * N_CONST)
            norm_rows("xn", resid, "xn_ready")
            ps = full(dve, "prm")
            v(V.tensor_copy(colsA[:, 0:100], ps[:, 0:100]))
            v(V.tensor_copy(colsB[:, :], ps[:, 104:228]))
            v(V.tensor_copy(colsC[:, :], ps[:, 228:276]))
            v(V.tensor_copy(colsD[:, :], ps[0:64, 276:280]), "cols_ready")
            C1 = 6.28125
            C2 = 2 * np.pi - C1
            MAGIC = 12582912.0
            for i in range(3):
                x, n = fsmall[:, 2 * i + 1, :], fsmall[:, 6, :]
                ps = full(dve, f"f{i}")
                last(V.tensor_scalar(x, ps[0:64, 0:T], colsD[:, i:i + 1], colsD[:, 3:4], ALU.add, ALU.mult), f"f{i}")
                v(V.tensor_scalar(n, x, 1.0 / (2 * np.pi), MAGIC, ALU.mult, ALU.add))
                v(V.tensor_scalar(n, n, MAGIC, None, ALU.subtract))
                v(V.scalar_tensor_tensor(x, n, -C1, x, ALU.mult, ALU.add))
                v(V.scalar_tensor_tensor(x, n, -C2, x, ALU.mult, ALU.add))
                v(V.tensor_scalar(x, x, 3.1415925, -3.1415925, ALU.min, ALU.max), "sine_arg")
            def keys_dup(name, c0, done=None):
                ps = full(dve, name)
                for g in range(KV):
                    for half in range(2):
                        ins = V.tensor_copy(kdup[half * HD:(half + 1) * HD, g, c0:c0 + T], ps[g * HD:(g + 1) * HD, 0:T])
                        if g == KV - 1 and half == 1:
                            last(ins, name)
                        else:
                            v(ins)

            dve.wait_ge(dec_in, 16)
            dve.wait_ge(ev("tables_in"), 16 * 6)
            for t in range(NT):
                for m in range(4):
                    last(V.tensor_tensor(filt[:, t, m, :], full(dve, f"h{t}{m}"), decay[:, t, m % 2, :], ALU.mult), f"h{t}{m}")
            rn = arena2[:, 3584:4096]
            for o in range(2):
                if o:
                    full(dve, "habs0")
                for t in range(NT):
                    f, g = filt[:, t, 2 * o, :], filt[:, t, 2 * o + 1, :]
                    v(V.scalar_tensor_tensor(absb[:, t, :], f, -1.0, f, ALU.mult, ALU.max))
                    v(V.scalar_tensor_tensor(rn, g, -1.0, g, ALU.mult, ALU.max))
                    v(V.tensor_tensor(absb[:, t, :], absb[:, t, :], rn, ALU.add), "abs_ready")
                for t in range(NT):
                    f, g = filt[:, t, 2 * o, :], filt[:, t, 2 * o + 1, :]
                    v(V.tensor_tensor(rn, f, g, ALU.add))
                    v(V.tensor_tensor(g, f, g, ALU.subtract))
                    v(V.tensor_copy(f, rn), "ed_ready" if t else None)
                last(V.tensor_scalar(rn, full(dve, f"habs{o}"), EPS, None, ALU.add), f"habs{o}")
                v(V.reciprocal(rn, rn))
                for part in range(2):
                    full(dve, f"sp{o}{part}1")
                    for fr in range(NT):
                        last(V.tensor_tensor(spec[:, o, part, fr, :], full(dve, f"sp{o}{part}{fr}"), rn, ALU.mult), f"sp{o}{part}{fr}")
            v(V.tensor_copy(stat("dummy", 1), epscol[:, 0:1]), "filters_ready")

            v(V.memset(vpad[:, :, 0:30], 0.0))
            for g in range(2):
                emptied(dve, f"wa{g}")
                emptied(dve, f"wg{g}")
            v(V.tensor_tensor(vpad[:, :, 30:30 + T], aT, sgT, ALU.mult))
            n = 0
            for j in range(TAPS):
                for c in range(KC):
                    w = colsB[:, j * KC + c:j * KC + c + 1]
                    if n >= KC:
                        dve.wait_ge(ev("tap"), n - KC + 1)
                    if j == 0:
                        V.tensor_scalar(yT[:, c, :], vpad[:, c, 0:T], w, colsA[:, 8 + c:9 + c], ALU.mult, ALU.add).then_inc(ev("tap"), 1)
                    else:
                        V.scalar_tensor_tensor(yT[:, c, :], vpad[:, c, j:j + T], w, yT[:, c, :], ALU.mult, ALU.add).then_inc(ev("tap"), 1)
                    n += 1
            dve.wait_ge(ev("tap"), n)
            v(V.tensor_copy(stat("dummy", 1), epscol[:, 0:1]), "conv_ready")
            for t in range(NT):
                v(V.bn_stats(stat("bn", 12)[:, 6 * t:6 * t + 6], full(dve, f"yt{t}")))
                v(V.bn_aggr(stat("mv", 4)[:, 2 * t:2 * t + 2], stat("bn", 12)[:, 6 * t:6 * t + 6]))
                v(V.tensor_copy(stat("ln_v")[:, t:t + 1], stat("mv", 4)[:, 2 * t + 1:2 * t + 2]), "ln_var")
            for t in range(NT):
                dve.wait_ge(ev("ln_sd"), t + 1)
                v(V.reciprocal(stat("ln_r")[:, t:t + 1], stat("ln_sd")[:, t:t + 1]))
                last(V.tensor_scalar(ytok[:, t, :], full(dve, f"yt{t}"), stat("mv", 4)[:, 2 * t:2 * t + 1], stat("ln_r")[:, t:t + 1],
                                     ALU.subtract, ALU.mult), f"yt{t}")

            dve.wait_ge(ev("bcast_in"), 16 * 7)
            for par in range(2):
                emptied(dve, f"s0{par}")
            m, sm, es = stat("p1_m", 16), stat("p1_sm", 16), stat("p1_es", 16)
            for t in range(NT):
                w = P * (t + 1)
                if t:
                    for par in range(2):
                        for pr in range(2):
                            emptied(dve, f"s1{par}{pr}")
                for h in range(HEADS):
                    p = prob1[:, t, h, 0:w]
                    v(V.scalar_tensor_tensor(p, rel[:, 2 * P - w:2 * P], -SLOPES[h], p, ALU.mult, ALU.add))
                mt = m[:, 8 * t:8 * t + 8]
                v(V.tensor_reduce(mt, prob1[:, t, :, 0:w], AX.X, ALU.max))
                v(V.tensor_tensor(mt, mt, sinkrow[:, :], ALU.max))
                v(V.tensor_tensor(sm[:, 8 * t:8 * t + 8], sinkrow[:, :], mt, ALU.subtract))
                v(V.tensor_tensor(prob1[:, t, :, 0:w], prob1[:, t, :, 0:w], rep_(mt, 2, [P, HEADS, w]), ALU.subtract), "p1_shift")
            for t in range(NT):
                w = P * (t + 1)
                mt = m[:, 8 * t:8 * t + 8]
                dve.wait_ge(ev("p1_exp"), t + 1)
                v(V.tensor_reduce(mt, prob1[:, t, :, 0:w], AX.X, ALU.add))
                v(V.tensor_tensor(mt, mt, es[:, 8 * t:8 * t + 8], ALU.add))
                v(V.reciprocal(mt, mt))
                v(V.tensor_tensor(prob1[:, t, :, 0:w], prob1[:, t, :, 0:w], rep_(mt, 2, [P, HEADS, w]), ALU.mult), "p1_ready")
            ps = full(dve, "mod")
            for q in range(4):
                j = (0, 1, 3, 4)[q]
                ins = V.tensor_tensor(mod[:, 8 * j:8 * j + 8, :], ps[:, 16 * q:16 * q + 16].rearrange("p (k j) -> p k j", j=2),
                                      rep_(colsC[:, 8 * j:8 * j + 8], 2, [P, 8, 2]), ALU.add)
                if q < 3:
                    v(ins)
                else:
                    last(ins, "mod")
            for r, (c, j, g) in enumerate(((8, 0, 20), (8, 1, 20), (32, 0, 28))):
                v(V.scalar_tensor_tensor(modsc[:, r, :], mod[:, c:c + 8, j], 1.0, colsA[:, g:g + 8], ALU.add, ALU.mult),
                  "modsc_ready" if r == 2 else None)

            def merge(tag):
                for j in range(8):
                    br, i = j // 4, j % 4
                    emptied(dve, f"{tag}g{br}{i}")
                    ps = full(dve, f"{tag}o{br}{i}")
                    dst = mergedT[:, 2 * i:2 * i + 2, :].rearrange("p c t -> p (c t)")
                    if br == 0:
                        last(V.tensor_tensor(dst, sgate[tag][:, j % 2, :], ps, ALU.mult), f"{tag}o{br}{i}")
                    else:
                        last(V.tensor_tensor(mtmp[tag][:, j % 2, :], sgate[tag][:, j % 2, :], ps, ALU.mult), f"{tag}o{br}{i}")
                        v(V.tensor_tensor(dst, dst, mtmp[tag][:, j % 2, :], ALU.add), f"{tag}merged" if i == 3 else None)

            dve.wait_ge(ev("grow_sent"), 16)
            merge("a")
            for t in range(NT):
                for n in range(2):
                    r = resid[:, t, n * 512:(n + 1) * 512]
                    last(V.tensor_tensor(r, r, full(dve, f"ax{t}{n}"), ALU.add), f"ax{t}{n}")
                v(V.tensor_copy(stat("dummy", 1), epscol[:, 0:1]), "ah_ready")

            norm_rows("rn", resid, "rn_ready")
            for t in range(NT):
                dve.wait_ge(ev("cx_sd"), t + 1)
                v(V.reciprocal(stat("cx_r")[:, t:t + 1], stat("cx_sd")[:, t:t + 1]))
                v(V.tensor_scalar(ctxr[:, t, :], ctxr[:, t, :], stat("cx_r")[:, t:t + 1], None, ALU.mult), "ctxn_ready")
            lg = rt[:, 72:144].rearrange("p (t e) -> p t e", t=NT)
            ps = full(dve, "route")
            last(V.tensor_tensor(lg, ps[:, 0:128].rearrange("p (t e) -> p t e", t=NT)[:, :, 0:36], rep_(rbias[:, :], 1, [P, NT, 36]), ALU.add), "route")
            g8 = rt[:, 0:16].rearrange("p (t e) -> p t e", t=NT)
            gm = rt[:, 16:32]
            gi = rt[:, 32:48].bitcast(U32)
            gf = stat("gf")
            og = rt[:, 64:72].rearrange("p (t e) -> p t e", t=NT)
            v(V.memset(g8, -3.0e38))
            v(V.tensor_copy(g8[:, :, 0:GROUPS], lg[:, :, 0:GROUPS]))
            for t in range(NT):
                v(V.max(gm[:, 8 * t:8 * t + 8], g8[:, t, :]))
                v(V.max_index(gi[:, 8 * t:8 * t + 8], gm[:, 8 * t:8 * t + 8], g8[:, t, :]))
                v(V.tensor_copy(gf[:, t:t + 1], gi[:, 8 * t:8 * t + 1]))
                v(V.tensor_scalar(og[:, t, :], iota[:, 0:GROUPS], gf[:, t:t + 1], None, ALU.is_equal))
                v(V.tensor_scalar(stat("rt_ng")[:, t:t + 1], gm[:, 8 * t:8 * t + 1], -1.0, None, ALU.mult), "rt_gmax" if t else None)
            em = rt[:, 144:160]
            e8 = rt[:, 160:176].rearrange("p (t e) -> p t e", t=NT)
            ei = rt[:, 176:192].bitcast(U32)
            ef = stat("ef", 4)
            tmp = rt[:, 192:224].rearrange("p (g e) -> p g e", g=GROUPS)
            for t in range(NT):
                el = lg[:, t, GROUPS:].rearrange("p (g e) -> p g e", g=GROUPS)
                v(V.tensor_tensor(tmp, el, rep_(og[:, t, :], 2, [P, GROUPS, PER_GROUP]), ALU.mult))
                v(V.tensor_reduce(e8[:, t, :], rt[:, 192:224].rearrange("p (g e) -> p e g", g=GROUPS), AX.X, ALU.add))
                v(V.max(em[:, 8 * t:8 * t + 8], e8[:, t, :]))
                v(V.max_index(ei[:, 8 * t:8 * t + 8], em[:, 8 * t:8 * t + 8], e8[:, t, :]))
                v(V.tensor_copy(ef[:, 2 * t:2 * t + 2], ei[:, 8 * t:8 * t + 2]))
                v(V.tensor_scalar(stat("rt_nv")[:, t:t + 1], em[:, 8 * t:8 * t + 1], -1.0, None, ALU.mult), "rt_top" if t else None)
            oh = rt[:, 256:384].rearrange("p (j e) -> p j e", j=4)
            asg = arena2[:, 512:576].rearrange("p (t e) -> p t e", t=NT)
            for t in range(NT):
                for k in range(2):
                    j = 2 * t + k
                    v(V.scalar_tensor_tensor(ef[:, j:j + 1], gf[:, t:t + 1], float(PER_GROUP), ef[:, j:j + 1], ALU.mult, ALU.add))
                    v(V.tensor_scalar(oh[:, j, :], iota[:, :], ef[:, j:j + 1], None, ALU.is_equal))
                v(V.tensor_tensor(asg[:, t, :], oh[:, 2 * t, :], oh[:, 2 * t + 1, :], ALU.add), "assign_ready" if t else None)
            dve.wait_ge(ev("rt_gsum"), 2)
            dve.wait_ge(ev("rt_e1"), 2)
            pk = picks[:, :].rearrange("p (t k) -> p t k", k=2)
            wa_, wb_ = stat("wa_"), stat("wb_")
            v(V.tensor_scalar(wa_, stat("rt_e1"), 1.0, None, ALU.add))
            v(V.tensor_tensor(wa_, wa_, stat("rt_gs"), ALU.mult))
            v(V.reciprocal(wb_, wa_))
            v(V.tensor_copy(pk[:, :, 0], wb_))
            v(V.tensor_tensor(pk[:, :, 1], wb_, stat("rt_e1"), ALU.mult))
            v(V.memset(rt[:, 640:896], 0.0))
            posb = rt[:, 384:480]
            last(V.tensor_copy(posb, full(dve, "pos")[:, 0:96]), "pos")
            cnt = posb[:, 64:96]
            sums = rt[:, 640:896].rearrange("p (r n) -> p r n", r=2)
            ext, ext0 = sums[:, 0, 32:64], rt[:, 896:928]
            v(V.tensor_scalar(ext, cnt, float(CAP), None, ALU.is_gt))
            for r in range(2, BLOCKS):
                v(V.scalar_tensor_tensor(ext, cnt, float(CAP * r), ext, ALU.is_gt, ALU.add))
            v(V.tensor_copy(ext0, ext))
            side, d = 0, 1
            while d < EXPERTS:
                v(V.tensor_tensor(sums[:, 1 - side, 32:64], sums[:, side, 32:64], sums[:, side, 32 - d:64 - d], ALU.add))
                side, d = 1 - side, 2 * d
            upto = sums[:, side, 32:64]
            v(V.tensor_tensor(ext0, upto, ext0, ALU.subtract))
            pc, pp, po, pg = stat("pc", 4), stat("pp", 4), stat("po", 4), stat("pg", 4)
            hits = arena2[:, 1024:1280]
            own = posb[:, 0:64].rearrange("p (t e) -> p t e", t=NT)
            h4 = hits[:, 0:128].rearrange("p (t k e) -> p t k e", t=NT, k=2)
            v_pair(V.tensor_tensor(h4, rt[:, 256:384].rearrange("p (t k e) -> p t k e", t=NT, k=2), rep_(own, 2, [P, NT, 2, EXPERTS]), ALU.mult))
            v_pair(V.tensor_tensor(hits[:, 128:256].rearrange("p (j e) -> p j e", j=4), oh, rep_(ext0, 1, [P, 4, EXPERTS]), ALU.mult))
            v_pair(V.tensor_reduce(pc, hits[:, 0:128].rearrange("p (j e) -> p j e", j=4), AX.X, ALU.add))
            v_pair(V.tensor_reduce(po, hits[:, 128:256].rearrange("p (j e) -> p j e", j=4), AX.X, ALU.add))
            v_done()
            v(V.tensor_scalar(pp, pc, float(CAP), None, ALU.is_ge))
            for r in range(2, BLOCKS):
                v(V.scalar_tensor_tensor(pp, pc, float(CAP * r), pp, ALU.is_ge, ALU.add))
            v(V.scalar_tensor_tensor(pc, pp, -float(CAP), pc, ALU.mult, ALU.add))
            v(V.tensor_scalar(pg, pp, 1.0, None, ALU.is_ge))
            v(V.scalar_tensor_tensor(po, po, float(EXPERTS - 1), pp, ALU.add, ALU.add))
            v(V.tensor_tensor(po, po, ef, ALU.subtract))
            v(V.tensor_tensor(po, po, pg, ALU.mult))
            v(V.tensor_tensor(po, po, ef, ALU.add))
            v(V.scalar_tensor_tensor(slotf[:, :], po, float(CAP), pc, ALU.mult, ALU.add))
            v(V.tensor_copy(sloti[:, :], slotf[:, :]), "slots_ready")
            xe = rt[:, 928:1024]
            big = arena2[:, 1024:1024 + EXTRA * EXPERTS].rearrange("p (x e) -> p x e", x=EXTRA)
            v(V.tensor_tensor(big, rep_(iota[:, 0:EXTRA], 2, [P, EXTRA, EXPERTS]), rep_(upto, 1, [P, EXTRA, EXPERTS]), ALU.is_ge))
            v(V.tensor_copy(xe[:, 0:EXPERTS], iota[:, :]))
            v(V.tensor_reduce(xe[:, EXPERTS:EXPERTS + EXTRA], big, AX.X, ALU.add))
            v(V.tensor_scalar(xe[:, EXPERTS:EXPERTS + EXTRA], xe[:, EXPERTS:EXPERTS + EXTRA], float(EXPERTS - 1), None, ALU.min))
            v(V.tensor_copy(elist[:, :], xe[0:1, 0:EXPERTS + EXTRA]))
            np_ = stat("np", 1)
            v(V.tensor_scalar(np_, upto[:, EXPERTS - 1:EXPERTS], 0.0, float(STEPS), ALU.is_gt, ALU.add))
            for r in range(2, EXTRA, 2):
                v(V.scalar_tensor_tensor(np_, upto[:, EXPERTS - 1:EXPERTS], float(r), np_, ALU.is_gt, ALU.add))
            v(V.tensor_copy(trips[:, :], np_[0:1, :]), "trips_ready")

            kk = kvt[:, 0:512].rearrange("p (t c) -> p t c", c=T)[:, :, 0:P]
            sqc = arena1[:, 3600:3856].rearrange("p (t c) -> p t c", t=NT)
            for t in range(NT):
                ps = full(dve, f"ckv{t}")
                v(V.tensor_copy(kvt[:, t * T:t * T + P], ps[:, 0:P]))
                last(V.tensor_copy(vtok[:, 2 + t, :], ps[:, P:2 * P]), f"ckv{t}")
            v(V.tensor_tensor(sqc, kk, kk, ALU.mult))
            v(V.tensor_reduce(stat("ck_ss", 4), arena1[:, 3600:3856].rearrange("p (a d) -> p a d", d=HD), AX.X, ALU.add), "ck_ss")
            dve.wait_ge(ev("ck_sd"), 1)
            v(V.reciprocal(stat("ck_r", 4), stat("ck_sd", 4)))
            for t in range(NT):
                k3 = kvt[:, t * T:t * T + P].rearrange("p (h d) -> p h d", h=KV)
                v(V.tensor_tensor(k3, k3, rep_(stat("ck_r", 4)[:, 2 * t:2 * t + 2], 2, [P, KV, HD]), ALU.mult))
                v(V.tensor_tensor(k3, k3, rep_(qkg[:, 1, :], 1, [P, KV, HD]), ALU.mult), "ck_ready" if t else None)

            dve.wait_ge(ev("zeroed"), 16 * ZEROED)
            keys_dup("ckT", T)

            n_iter = dve.value_load(trips[0:1, 0:1], min_val=STEPS, max_val=MAXSTEPS)
            dve.sem_inc(ev("down_read1"), 1)

            def rows_out(n):
                dve.wait_ge(ev("rowsT_full"), n)
                V.tensor_tensor(xT, psum[:, 0:2, :].rearrange("p b (k c) -> p (b k) c", k=4),
                                rep_(colsA[:, 36:44], 2, [P, KD, BOTH]), ALU.mult).then_inc(ev("rowsT_ready"), 1)

            rows_out(1)
            with dve.Fori(0, n_iter) as i:
                dve.wait_ge(ev("silu_ready"), i + 1)
                dve.wait_ge(ev("up_full"), i + 1)
                V.tensor_tensor(hrow, silu, psum[0:BOTH, 4, :], ALU.mult).then_inc(ev("hid_ready"), 1)
                rows_out(i + 2)
                dve.wait_ge(ev("down_full1"), i + 1)
                dve.wait_ge(ev("stored"), 16 * i + 1)
                V.tensor_copy(yrow[:, 512:1024], psum[0:BOTH, 6, :]).then_inc(ev("down_read1"), 1)

            for j in range(4):
                dve.wait_ge(ev("fetched"), 16 * 4)
                r = resid[:, j // 2, :]
                v(V.scalar_tensor_tensor(r, back[:, j, :], picks[:, j:j + 1], r, ALU.mult, ALU.add), "moe_added" if j % 2 else None)
            dve.wait_ge(ev("gf_in"), 16)
            norm_rows("fn", resid, "x2_ready", gfrow)

            norm_rows("zn", resid, "zn_ready")
            v(V.memset(hpad[:, :, :, 0:1], 0.0))
            v(V.memset(hpad[:, :, :, T + 1:T + 2], 0.0), "pads_zero")
            for t in range(NT):
                ps = full(dve, f"kv{t}")
                v(V.tensor_copy(ktok[:, t, :], ps[:, 0:P]))
                last(V.tensor_copy(vtok[:, t, :], ps[:, P:2 * P]), f"kv{t}")
            for t in range(NT):
                emptied(dve, f"q{t}")
            ss = stat("qk_ss", 20)
            v(V.tensor_tensor(sq, qtok, qtok, ALU.mult))
            v(V.tensor_reduce(ss[:, 0:16], arena2[:, 1280:2304].rearrange("p (a d) -> p a d", d=HD), AX.X, ALU.add))
            v(V.tensor_tensor(arena2[:, 1280:1536], arena2[:, 1024:1280], arena2[:, 1024:1280], ALU.mult))
            v(V.tensor_reduce(ss[:, 16:20], arena2[:, 1280:1536].rearrange("p (a d) -> p a d", d=HD), AX.X, ALU.add), "qk_ss")
            dve.wait_ge(ev("qk_sd"), 1)
            v(V.reciprocal(stat("qk_r", 20), stat("qk_sd", 20)))
            for rows_, heads, r0, gi_ in ((qtok, HEADS, 0, 0), (ktok, KV, 16, 1)):
                for t in range(NT):
                    x3 = rows_[:, t, :].rearrange("p (h d) -> p h d", h=heads)
                    v(V.tensor_tensor(x3, x3, rep_(stat("qk_r", 20)[:, r0 + heads * t:r0 + heads * (t + 1)], 2, [P, heads, HD]), ALU.mult))
                    v(V.tensor_tensor(x3, x3, rep_(qkg[:, gi_, :], 1, [P, heads, HD]), ALU.mult))
                    x5 = rows_[:, t, :].rearrange("p (h a s j) -> p h a s j", a=2, s=2, j=16)
                    r5 = rtmp[:, t, 0:heads * HD].rearrange("p (h a s j) -> p h a s j", a=2, s=2, j=16)
                    s4 = rope[:, 1, t, :].rearrange("p (a s j) -> p a s j", a=2, s=2)
                    for half in range(2):
                        v(V.tensor_tensor(r5[:, :, :, half, :], x5[:, :, :, 1 - half, :],
                                          rep_(s4[:, :, half, :], 1, [P, heads, 2, 16]), ALU.mult))
                    v(V.tensor_tensor(x3, x3, rep_(rope[:, 0, t, :], 1, [P, heads, HD]), ALU.mult))
                    x2 = rows_[:, t, :]
                    fin = rows_ is ktok and t == NT - 1
                    v(V.tensor_tensor(x2, x2, rtmp[:, t, 0:heads * HD], ALU.add), "qk2_ready" if fin else None)
            for j in range(6):
                emptied(dve, f"hy{j // 2}{j % 2}")
                for c in range(2):
                    k = 2 * j + c
                    x = hpad[:, j % 2, c, :]
                    v(V.tensor_scalar(zs[:, k, :], x[:, 0:T], colsA[:, 44 + k:45 + k], colsA[:, 80 + k:81 + k], ALU.mult, ALU.add))
                    v(V.scalar_tensor_tensor(zs[:, k, :], x[:, 1:T + 1], colsA[:, 56 + k:57 + k], zs[:, k, :], ALU.mult, ALU.add))
                    v(V.scalar_tensor_tensor(zs[:, k, :], x[:, 2:T + 2], colsA[:, 68 + k:69 + k], zs[:, k, :], ALU.mult, ALU.add),
                      "short_done" if c else None)
            v(V.tensor_copy(stat("dummy", 1), epscol[:, 0:1]), "short_ready")
            keys_dup("kT", 0)
            v(V.tensor_copy(stat("dummy", 1), epscol[:, 0:1]), "k2_ready")

            def unit_max(u):
                v(V.tensor_reduce(stat("m2", 16)[:, u:u + 1], full(dve, f"sc{u}"), AX.X, ALU.max))
                v(V.tensor_scalar(stat("nm2", 16)[:, u:u + 1], stat("m2", 16)[:, u:u + 1], -HD ** -0.5, None, ALU.mult), "nmax")

            half_ = lambda ap: ap.rearrange("p k c -> p (k c)")
            Uc, Us = half_(Usb[:, 0:2, :]), half_(Usb[:, 2:4, :])

            def hy_product(o, part):
                for p_ in range(2):
                    for f in range(NT):
                        emptied(dve, f"U{o}{p_}{f}")
                Kc, Ks = half_(spec[:, o, 0, :, :]), half_(spec[:, o, 1, :, :])
                y = half_(Y[:, 2 * part:2 * part + 2, :])
                v(V.tensor_tensor(y, Uc, (Kc, Ks)[part], ALU.mult))
                v(V.tensor_tensor(prod, Us, (Ks, Kc)[part], ALU.mult))
                v(V.tensor_tensor(y, y, prod, (ALU.subtract, ALU.add)[part]), "Y_ready" if part else None)

            def hy_gate(o, g):
                src = (zs[:, 0:4, :], y1T)[o]
                gate = (zs[:, 4:8, :], zs[:, 8:12, :])[o]
                ps = full(dve, f"I{o}{g}")
                for c in range(2):
                    k = 2 * g + c
                    ins = V.scalar_tensor_tensor(prod[:, k * T:(k + 1) * T], src[:, k, :], colsA[:, 92 + 4 * o + k:93 + 4 * o + k],
                                                 ps[:, c * T:(c + 1) * T], ALU.mult, ALU.add)
                    if c:
                        last(ins, f"I{o}{g}")
                    else:
                        v(ins)
                if g:
                    v(V.tensor_tensor(gate.rearrange("p c t -> p (c t)"), gate.rearrange("p c t -> p (c t)"), prod, ALU.mult),
                      ("y1_ready", "hy_ready")[o])

            hy_parts = {4: (hy_product, 0, 0), 5: (hy_product, 0, 1), 7: (hy_gate, 0, 0), 8: (hy_gate, 0, 1),
                        13: (hy_product, 1, 0), 14: (hy_product, 1, 1)}
            unit_max(0)
            unit_max(1)
            for u in range(16):
                if u + 2 < 16:
                    unit_max(u + 2)
                emptied(dve, f"sc{u}")
                v(V.reciprocal(stat("m2", 16)[:, u:u + 1], stat("sum2", 16)[:, u:u + 1]))
                v(V.tensor_scalar(prob2[:, u % 4, :], prob2[:, u % 4, :], stat("m2", 16)[:, u:u + 1], None, ALU.mult), "p2_ready")
                if u in hy_parts:
                    hy_parts[u][0](*hy_parts[u][1:])
            hy_gate(1, 0)
            hy_gate(1, 1)
            merge("b")
            dve.wait_ge(ev("g1_in"), 16)
            for t in range(NT):
                for n in range(2):
                    r = resid[:, t, n * 512:(n + 1) * 512]
                    last(V.tensor_tensor(scratch[:, t, 0:512], g1row[:, n * 512:(n + 1) * 512], full(dve, f"bx{t}{n}"), ALU.mult), f"bx{t}{n}")
                    v(V.tensor_tensor(r, r, scratch[:, t, 0:512], ALU.add), "bh_ready" if n else None)
            norm_rows("pn", resid, "pn_ready")
            def top16(chains):
                for r in range(2):
                    for vals, idx, src in chains:
                        v_pair(V.max(vals[:, 8 * r:8 * r + 8], src))
                    for vals, idx, src in chains:
                        v_pair(V.max_index(idx[:, 8 * r:8 * r + 8], vals[:, 8 * r:8 * r + 8], src))
                    if r == 0:
                        for vals, idx, src in chains:
                            v_pair(V.match_replace(src, vals[:, 0:8], src, -3.0e38))

            def best_of(t, g):
                emptied(dve, f"ks{t}{g}")
                for h in (2 * g, 2 * g + 1):
                    top16([(top_v[:, t, c, :], top_i[:, t, c, :], S[:, t, c, :]) for c in (2 * h, 2 * h + 1)])
                v_done()
                sums = [(best[:, t, h, :], where[:, t, h * PTOP:(h + 1) * PTOP], cand[:, h * 256:(h + 1) * 256]) for h in (2 * g, 2 * g + 1)]
                for h, (_, _, c) in zip((2 * g, 2 * g + 1), sums):
                    v_pair(V.tensor_tensor(c.rearrange("p (a b) -> p a b", a=PTOP), rep_(top_v[:, t, 2 * h, :], 2, [P, PTOP, PTOP]),
                                           rep_(top_v[:, t, 2 * h + 1, :], 1, [P, PTOP, PTOP]), ALU.add))
                top16(sums)
                v_done()

            def rows_of_table(t, g):
                n = 2 * PTOP
                ns = slice(n * g, n * (g + 1))
                v(V.tensor_copy(top_f[:, t, 4 * g:4 * g + 4, :], top_i[:, t, 4 * g:4 * g + 4, :]))
                halves = ((0, ALU.logical_shift_right, 4), (1, ALU.bitwise_and, 15))
                for half, op, arg in halves:
                    v_pair(V.tensor_scalar(wi[:, half, ns], where[:, t, ns], arg, None, op))
                for half, op, arg in halves:
                    v_pair(V.tensor_copy(wf[:, half, ns], wi[:, half, ns]))
                hot = [cand[:, n * PTOP * half:n * PTOP * (half + 1)] for half in range(2)]
                for half, op, arg in halves:
                    v_pair(V.tensor_tensor(hot[half].rearrange("p (n a) -> p n a", a=PTOP), rep_(wf[:, half, ns], 2, [P, n, PTOP]),
                                           rep_(iota[:, 0:PTOP], 1, [P, n, PTOP]), ALU.is_equal))
                for half, op, arg in halves:
                    tf = top_f[:, t, 4 * g:4 * g + 4, :].rearrange("p (h s) k -> p h s k", s=2)[:, :, half, :]
                    oh4 = hot[half].rearrange("p (h k a) -> p h k a", h=2, k=PTOP)
                    v_pair(V.tensor_tensor(oh4, oh4, rep_(tf, 2, [P, 2, PTOP, PTOP]), ALU.mult))
                for half, op, arg in halves:
                    v_pair(V.tensor_reduce(wf[:, half, ns], hot[half].rearrange("p (n a) -> p n a", a=PTOP), AX.X, ALU.add))
                v_done()
                v(V.scalar_tensor_tensor(rowf[:, t, ns], wf[:, 0, ns], float(PKEYS), wf[:, 1, ns], ALU.mult, ALU.add))
                v(V.tensor_copy(rowid[:, t, ns], rowf[:, t, ns]), "rowid_ready")

            def gates_of_picks(t):
                g3 = gates[:, t, :].rearrange("p (h k) -> p h k", k=PTOP)
                v(V.tensor_tensor(g3, best[:, t, :, :], best[:, t, :, 0:1].to_broadcast([P, PH, PTOP]), ALU.subtract), "best_shift")
                dve.wait_ge(ev("best_exp"), t + 1)
                v(V.tensor_reduce(stat("gsum", 8), g3, AX.X, ALU.add))
                v(V.reciprocal(stat("gsum", 8), stat("gsum", 8)))
                v(V.tensor_tensor(g3, g3, rep_(stat("gsum", 8), 2, [P, PH, PTOP]), ALU.mult))

            per = PICKS // ROWBUFS

            def row_dots(t, i0, i1):
                with dve.Fori(i0, i1) as i:
                    for b in range(ROWBUFS):
                        dve.wait_ge(ev(f"row_in{b}"), (i + (2 * t * per + 1)) * 16)
                        V.tensor_tensor_reduce(dotjunk[:, b % 2, :], rows[:, b, :], tok2[:, t, :], 1.0, 0.0, ALU.mult, ALU.add,
                                               dotcols[:, b:b + 1]).then_inc(ev("row_used"), 1)
                        dve.wait_ge(ev("row_used"), (i + 2 * t * per) * ROWBUFS + (ROWBUFS + b))
                    dve.wait_ge(ev("row_used"), (i + 2 * t * per) * ROWBUFS + 2 * ROWBUFS)
                    V.tensor_copy(dots[:, t, bass.ds(i * ROWBUFS, ROWBUFS)], dotcols[:, :]).then_inc(ev("dots_kept"), 1)
                    dve.wait_ge(ev("dots_kept"), i + (t * per + 1))

            for t in range(NT):
                for n in range(2):
                    emptied(dve, f"xp{t}{n}")
            dve.sem_inc(ev("row_used"), ROWBUFS)

            def picks_of(t, g):
                best_of(t, g)
                rows_of_table(t, g)

            def dots_of(t, g):
                row_dots(t, g * per // 4, (g + 1) * per // 4)

            def weigh(t):
                v(V.tensor_copy(stat("dummy", 1), epscol[:, 0:1]), "dots_ready")
                gates_of_picks(t)
                dve.wait_ge(ev("gelu_done"), t + 1)
                v(V.tensor_tensor(gates[:, t, :], gates[:, t, :], dots[:, t, :], ALU.mult))
                v(V.memset(scratch[:, :, :], 0.0))

            def add_rows(t, i0, i1):
                with dve.Fori(i0, i1) as i:
                    for b in range(ROWBUFS):
                        dve.wait_ge(ev(f"row_in{b}"), (i + ((2 * t + 1) * per + 1)) * 16)
                        acc = scratch[:, b % 2, :]
                        V.scalar_tensor_tensor(acc, rows[:, b, :], gates[:, t, bass.ds(i * ROWBUFS + b, 1)], acc,
                                               ALU.mult, ALU.add).then_inc(ev("row_used"), 1)
                        dve.wait_ge(ev("row_used"), (i + (2 * t + 1) * per) * ROWBUFS + (ROWBUFS + b))
                dve.wait_ge(ev("row_used"), (i1 + (2 * t + 1) * per + 1) * ROWBUFS)

            def into_residual(t):
                dve.wait_ge(ev("g2_in"), 32)
                v(V.tensor_tensor(scratch[:, 0, :], scratch[:, 0, :], scratch[:, 1, :], ALU.add))
                v(V.tensor_tensor(scratch[:, 0, :], scratch[:, 0, :], g2row, ALU.mult))
                v(V.tensor_tensor(resid[:, t, :], resid[:, t, :], scratch[:, 0, :], ALU.add), "x3_ready")

            def final_norm(t):
                dve.wait_ge(ev("ff_sd"), t + 1)
                v(V.reciprocal(stat("ff_r")[:, t:t + 1], stat("ff_sd")[:, t:t + 1]))
                v(V.scalar_tensor_tensor(resid[:, t, :], resid[:, t, :], stat("ff_r")[:, t:t + 1], flrow, ALU.mult, ALU.mult), "final_ready")

            picks_of(0, 0)
            for g in range(4):
                if g < 3:
                    picks_of(0, g + 1)
                dots_of(0, g)
            weigh(0)
            for g in range(3):
                add_rows(0, g * per // 4, (g + 1) * per // 4)
                picks_of(1, g)
            add_rows(0, 3 * per // 4, per)
            into_residual(0)
            dots_of(1, 0)
            final_norm(0)
            dots_of(1, 1)
            picks_of(1, 3)
            dots_of(1, 2)
            dots_of(1, 3)
            weigh(1)
            add_rows(1, 0, per)
            into_residual(1)
            final_norm(1)


_INS = ['x', 'g_mix', 'w_in', 'w_dw', 'b_dw', 'ln_conv_g', 'ln_conv_b', 'sinks', 'w_conv_out', 'w_attn_out', 'w_out', 'g_ffn',
        'w_group', 'b_group', 'w_expert', 'b_expert', 'w_gate', 'w_up', 'w_down', 'g_final', 'c_2', 'ctx_2', 'c_ctx_2',
        'ada_w_2', 'ada_b_2', 'norm_mix_g_2', 'norm_ffn_g_2', 'w_in_2', 'q_norm_g_2', 'k_norm_g_2', 'hy_conv_w_2',
        'hy_conv_b_2', 'hf_w1_2', 'hf_b1_2', 'hf_w2_2', 'hf_b2_2', 'hf_w3_2', 'hf_b3_2', 'hf_w4_2', 'hf_freq_2', 'hy_skip_2',
        'w_attn_out_2', 'w_hy_out_2', 'w_out_2', 'peer_wq_2', 'peer_keys1_2', 'peer_keys2_2', 'peer_u_2', 'peer_v_2',
        'final_norm_g_2']


def kernel(**inputs):
    import numpy as _np
    import concourse.bacc as _bacc
    from concourse import mybir as _mybir
    from concourse.bass_utils import run_bass_kernel_spmd as _run

    nc = _bacc.Bacc("TRN2", target_bir_lowering=False, num_devices=1)
    arrays, aps = {}, {}
    named = {n: _np.ascontiguousarray(inputs[n]) for n in _INS}
    named.update(shape_constants())
    for name, a in named.items():
        arrays[f"in_{name}_dram"] = a
        aps[name] = nc.dram_tensor(f"in_{name}_dram", a.shape, _mybir.dt.from_np(a.dtype), kind="ExternalInput").ap()
    out = nc.dram_tensor("out_0_dram", (1, T, D), F32, kind="ExternalOutput").ap()
    build(nc, aps, out)
    r = _run(nc, [arrays], core_ids=[0])
    return r.results[0]["out_0_dram"]
```
